# Optimizing a Trainium2 kernel written in Bass

```python
import math
import jax, jax.numpy as jnp
from jax import lax
import numpy as np
import jax
import jax.numpy as jnp

D_MODEL = 2048
BATCH = 1
SEQ = 256
DEPTH = 1

NSA_HEADS = 8
NSA_KV_HEADS = 2
NSA_GROUP = NSA_HEADS // NSA_KV_HEADS
HEAD_DIM = 128
NSA_DIM = NSA_HEADS * HEAD_DIM
NSA_KV_DIM = NSA_KV_HEADS * HEAD_DIM
CMP_BLOCK = 32
CMP_STRIDE = 16
SEL_BLOCK = 64
SEL_TOPK = 16
WINDOW = 512
WIN_Q_BLOCK = 128
SEL_Q_BLOCK = 64
ROPE_THETA = 10000.0
FORCE_SCORE = 1e9
DN_HEADS = 8
DN_HEAD_DIM = 128
DN_DIM = DN_HEADS * DN_HEAD_DIM
DN_CHUNK = 64
CONV_K = 4
D_FF = -(-(8 * D_MODEL) // (3 * 256)) * 256
NORM_EPS = 1e-6
NEG_INF = -1e30
IN_SPLITS = (NSA_DIM, 6 * NSA_KV_DIM, 3 * NSA_HEADS, 3 * DN_DIM, DN_DIM, DN_HEADS, DN_HEADS, 2 * D_MODEL)
N_IN = sum(IN_SPLITS)


def rms_norm(x, w):
    xf = x.astype(jnp.float32)
    y = xf * lax.rsqrt(jnp.mean(xf * xf, axis=-1, keepdims=True) + NORM_EPS)
    return (y * w.astype(jnp.float32)).astype(x.dtype)

def l2norm(x):
    return x * lax.rsqrt(jnp.sum(x * x, axis=-1, keepdims=True) + NORM_EPS)

def rope_tables(seq):
    inv = 1.0 / (ROPE_THETA ** (jnp.arange(0, HEAD_DIM, 2, dtype=jnp.float32) / HEAD_DIM))
    ang = jnp.arange(seq, dtype=jnp.float32)[:, None] * inv[None, :]
    return jnp.cos(ang), jnp.sin(ang)

def apply_rope(x, cos, sin):
    x1, x2 = jnp.split(x.astype(jnp.float32), 2, axis=-1)
    c = cos[None, :, None, :]
    s = sin[None, :, None, :]
    return jnp.concatenate([x1 * c - x2 * s, x2 * c + x1 * s], axis=-1).astype(x.dtype)

def masked_softmax(s, mask):
    return jax.nn.softmax(jnp.where(mask, s.astype(jnp.float32), NEG_INF), axis=-1)

def split_points():
    return [int(v) for v in np.cumsum(IN_SPLITS)[:-1]]

def cmp_to_sel_overlap(n_cmp, n_sel):
    cs = np.arange(n_cmp)[:, None] * CMP_STRIDE
    ss = np.arange(n_sel)[None, :] * SEL_BLOCK
    ov = np.clip(np.minimum(cs + CMP_BLOCK, ss + SEL_BLOCK) - np.maximum(cs, ss), 0, None)
    return jnp.asarray(ov / CMP_BLOCK, dtype=jnp.float32)

def compress_blocks(t, pe, w1, w2):
    b, s, hk, d = t.shape
    n_cmp = (s - CMP_BLOCK) // CMP_STRIDE + 1
    idx = np.arange(n_cmp)[:, None] * CMP_STRIDE + np.arange(CMP_BLOCK)[None, :]
    blk = jnp.swapaxes(t[:, idx], 2, 3) + pe
    blk = blk.reshape(b, n_cmp, hk, CMP_BLOCK * d)
    return jax.nn.gelu(blk @ w1) @ w2

def nsa_mixer(q, kv, gate_logits, cmp_pe_k, cmp_w1_k, cmp_w2_k, cmp_pe_v, cmp_w1_v, cmp_w2_v, cos, sin):
    b, s, _, d = q.shape
    hk, g = NSA_KV_HEADS, NSA_GROUP
    scale = HEAD_DIM ** -0.5
    kv = kv.reshape(b, s, 6, hk, d)
    k_c = apply_rope(kv[:, :, 0], cos, sin)
    v_c = kv[:, :, 1]
    k_s = apply_rope(kv[:, :, 2], cos, sin)
    v_s = kv[:, :, 3]
    k_w = apply_rope(kv[:, :, 4], cos, sin)
    v_w = kv[:, :, 5]
    qg = q.reshape(b, s, hk, g, d)
    t_pos = jnp.arange(s)

    kc = compress_blocks(k_c, cmp_pe_k, cmp_w1_k, cmp_w2_k)
    vc = compress_blocks(v_c, cmp_pe_v, cmp_w1_v, cmp_w2_v)
    n_cmp = kc.shape[1]
    s_cmp = jnp.einsum('bshgd,bchd->bhgsc', qg, kc) * scale
    cmp_end = jnp.arange(n_cmp) * CMP_STRIDE + CMP_BLOCK - 1
    cmp_valid = cmp_end[None, :] <= t_pos[:, None]
    p_cmp = masked_softmax(s_cmp, cmp_valid) * jnp.any(cmp_valid, axis=-1)[:, None].astype(jnp.float32)
    o_cmp = jnp.einsum('bhgsc,bchd->bshgd', p_cmp, vc.astype(jnp.float32))

    n_sel = s // SEL_BLOCK
    imp = jnp.einsum('bhgsc,cj->bhsj', p_cmp, cmp_to_sel_overlap(n_cmp, n_sel))
    blk_t = (t_pos // SEL_BLOCK)[:, None]
    j = jnp.arange(n_sel)[None, :]
    forced = (j == 0) | (j == blk_t) | (j == blk_t - 1)
    imp = jnp.where(forced, FORCE_SCORE, jnp.where(j > blk_t, -FORCE_SCORE, imp))
    n_top = min(SEL_TOPK, n_sel)
    _, sel_idx = lax.top_k(imp, n_top)
    kb = k_s.reshape(b, n_sel, SEL_BLOCK, hk, d).transpose(0, 3, 1, 2, 4)
    vb = v_s.reshape(b, n_sel, SEL_BLOCK, hk, d).transpose(0, 3, 1, 2, 4)
    nqb = s // SEL_Q_BLOCK
    q_blocks = qg.reshape(b, nqb, SEL_Q_BLOCK, hk, g, d).transpose(1, 0, 2, 3, 4, 5)
    idx_blocks = sel_idx.reshape(b, hk, nqb, SEL_Q_BLOCK, n_top).transpose(2, 0, 1, 3, 4)
    pos_blocks = t_pos.reshape(nqb, SEL_Q_BLOCK)
    gather = jax.vmap(jax.vmap(lambda blocks, ix: blocks[ix]))

    def sel_block(args):
        qb, ib, tb = args
        kg = gather(kb, ib)
        vg = gather(vb, ib)
        sc = jnp.einsum('bqhgd,bhqnkd->bhgqnk', qb, kg) * scale
        kpos = ib[..., None] * SEL_BLOCK + jnp.arange(SEL_BLOCK)
        valid = (kpos <= tb[None, None, :, None, None]).reshape(b, hk, 1, SEL_Q_BLOCK, n_top * SEL_BLOCK)
        p = masked_softmax(sc.reshape(b, hk, g, SEL_Q_BLOCK, n_top * SEL_BLOCK), valid)
        p = p.reshape(b, hk, g, SEL_Q_BLOCK, n_top, SEL_BLOCK)
        return jnp.einsum('bhgqnk,bhqnkd->bqhgd', p, vg.astype(jnp.float32))

    o_sel = lax.map(sel_block, (q_blocks, idx_blocks, pos_blocks))
    o_sel = o_sel.transpose(1, 0, 2, 3, 4, 5).reshape(b, s, hk, g, d)

    nb = s // WIN_Q_BLOCK
    n_prev = WINDOW // WIN_Q_BLOCK
    pad = ((0, 0), (WINDOW, 0), (0, 0), (0, 0))
    kp = jnp.pad(k_w, pad).reshape(b, nb + n_prev, WIN_Q_BLOCK, hk, d)
    vp = jnp.pad(v_w, pad).reshape(b, nb + n_prev, WIN_Q_BLOCK, hk, d)
    k_band = jnp.concatenate([kp[:, i:i + nb] for i in range(n_prev + 1)], axis=2)
    v_band = jnp.concatenate([vp[:, i:i + nb] for i in range(n_prev + 1)], axis=2)
    qw = qg.reshape(b, nb, WIN_Q_BLOCK, hk, g, d)
    s_win = jnp.einsum('bnqhgd,bnkhd->bhgnqk', qw, k_band) * scale
    qpos = t_pos.reshape(nb, WIN_Q_BLOCK)
    kpos = (jnp.arange(nb) * WIN_Q_BLOCK - WINDOW)[:, None] + jnp.arange((n_prev + 1) * WIN_Q_BLOCK)[None, :]
    diff = qpos[:, :, None] - kpos[:, None, :]
    win_valid = (diff >= 0) & (diff < WINDOW) & (kpos[:, None, :] >= 0)
    p_win = masked_softmax(s_win, win_valid)
    o_win = jnp.einsum('bhgnqk,bnkhd->bnqhgd', p_win, v_band.astype(jnp.float32)).reshape(b, s, hk, g, d)

    gates = jax.nn.sigmoid(gate_logits.astype(jnp.float32)).reshape(b, s, hk, g, 3)
    o = gates[..., 0:1] * o_cmp + gates[..., 1:2] * o_sel + gates[..., 2:3] * o_win
    return o.reshape(b, s, NSA_DIM)

def gated_deltanet(qkv, z, a, beta_logit, conv_w, a_log, dt_bias, norm_w):
    b, s, c3 = qkv.shape
    h, dk, c = DN_HEADS, DN_HEAD_DIM, DN_CHUNK
    n = s // c
    qkv = lax.conv_general_dilated(qkv, conv_w.astype(qkv.dtype), window_strides=(1,), padding=[(CONV_K - 1, 0)],
                                   dimension_numbers=('NWC', 'WIO', 'NWC'), feature_group_count=c3)
    qkv = jax.nn.silu(qkv.astype(jnp.float32))
    q, k, v = [t.reshape(b, s, h, dk) for t in jnp.split(qkv, 3, axis=-1)]
    q = l2norm(q) * dk ** -0.5
    k = l2norm(k)
    beta = jax.nn.sigmoid(beta_logit.astype(jnp.float32))
    gdec = -jnp.exp(a_log.astype(jnp.float32)) * jax.nn.softplus(a.astype(jnp.float32) + dt_bias.astype(jnp.float32))

    def chunks(t):
        return t.reshape(b, n, c, h, -1).transpose(0, 3, 1, 2, 4)

    q, k, v = chunks(q), chunks(k), chunks(v)
    beta = chunks(beta[..., None])[..., 0]
    gc = jnp.cumsum(chunks(gdec[..., None])[..., 0], axis=-1)
    lower_incl = np.tril(np.ones((c, c), dtype=bool))
    strict = np.tril(np.ones((c, c), dtype=bool), -1)
    decay = jnp.exp(jnp.where(lower_incl, gc[..., :, None] - gc[..., None, :], -jnp.inf))
    kb = k * beta[..., None]
    lmat = jnp.where(strict, jnp.einsum('bhnid,bhnjd->bhnij', kb, k) * decay, 0.0)
    eye = jnp.eye(c, dtype=jnp.float32)
    tinv = lax.linalg.triangular_solve(eye + lmat, jnp.broadcast_to(eye, lmat.shape), left_side=True, lower=True)
    u = tinv @ (v * beta[..., None])
    w = tinv @ (kb * jnp.exp(gc)[..., None])
    attn = jnp.einsum('bhnid,bhnjd->bhnij', q, k) * decay
    g_last = gc[..., -1]
    k_dec = k * jnp.exp(g_last[..., None] - gc)[..., None]
    q_dec = q * jnp.exp(gc)[..., None]

    def step(state, xs):
        q_i, k_i, u_i, w_i, attn_i, gl_i = xs
        v_new = u_i - jnp.einsum('bhck,bhkv->bhcv', w_i, state)
        o_i = jnp.einsum('bhck,bhkv->bhcv', q_i, state) + jnp.einsum('bhij,bhjv->bhiv', attn_i, v_new)
        state = state * jnp.exp(gl_i)[..., None, None] + jnp.einsum('bhck,bhcv->bhkv', k_i, v_new)
        return state, o_i

    xs = tuple(jnp.moveaxis(t, 2, 0) for t in (q_dec, k_dec, u, w, attn, g_last))
    state0 = jnp.zeros((b, h, dk, dk), jnp.float32)
    _, o = lax.scan(step, state0, xs)
    o = o.transpose(1, 0, 3, 2, 4).reshape(b, s, h, dk)
    o = rms_norm(o, norm_w) * jax.nn.silu(z.astype(jnp.float32).reshape(b, s, h, dk))
    return o.reshape(b, s, DN_DIM)

def first_inputs(seed: int = 0) -> dict:
    key = jax.random.key(seed)
    ks = jax.random.split(key, 24)

    def nrm(k, shape, fan_in):
        return jax.random.normal(k, shape, jnp.float32) * fan_in ** -0.5

    def gain(k, shape):
        return 1.0 + 0.02 * jax.random.normal(k, shape, jnp.float32)

    dt = jnp.exp(jax.random.uniform(ks[5], (DEPTH, DN_HEADS), jnp.float32, math.log(1e-3), math.log(1e-1)))
    return {
        'x': jax.random.normal(ks[0], (BATCH, SEQ, D_MODEL), jnp.float32),
        'norm1_w': gain(ks[1], (DEPTH, D_MODEL)),
        'w_in': nrm(ks[2], (DEPTH, D_MODEL, N_IN), D_MODEL),
        'conv_w': nrm(ks[3], (DEPTH, CONV_K, 1, 3 * DN_DIM), CONV_K),
        'a_log': jnp.log(jax.random.uniform(ks[4], (DEPTH, DN_HEADS), jnp.float32, 1.0, 16.0)),
        'dt_bias': dt + jnp.log(-jnp.expm1(-dt)),
        'dn_norm_w': gain(ks[6], (DEPTH, DN_HEAD_DIM)),
        'cmp_pe_k': 0.02 * jax.random.normal(ks[7], (DEPTH, CMP_BLOCK, HEAD_DIM), jnp.float32),
        'cmp_w1_k': nrm(ks[8], (DEPTH, CMP_BLOCK * HEAD_DIM, HEAD_DIM), CMP_BLOCK * HEAD_DIM),
        'cmp_w2_k': nrm(ks[9], (DEPTH, HEAD_DIM, HEAD_DIM), HEAD_DIM),
        'cmp_pe_v': 0.02 * jax.random.normal(ks[10], (DEPTH, CMP_BLOCK, HEAD_DIM), jnp.float32),
        'cmp_w1_v': nrm(ks[11], (DEPTH, CMP_BLOCK * HEAD_DIM, HEAD_DIM), CMP_BLOCK * HEAD_DIM),
        'cmp_w2_v': nrm(ks[12], (DEPTH, HEAD_DIM, HEAD_DIM), HEAD_DIM),
        'w_up_nsa': nrm(ks[13], (DEPTH, NSA_DIM, D_MODEL), NSA_DIM),
        'w_up_dn': nrm(ks[14], (DEPTH, DN_DIM, D_MODEL), DN_DIM),
        'w_o': nrm(ks[15], (DEPTH, D_MODEL, D_MODEL), D_MODEL),
        'norm2_w': gain(ks[16], (DEPTH, D_MODEL)),
        'w_ffn_gate': nrm(ks[17], (DEPTH, D_MODEL, D_FF), D_MODEL),
        'w_ffn_up': nrm(ks[18], (DEPTH, D_MODEL, D_FF), D_MODEL),
        'w_ffn_down': nrm(ks[19], (DEPTH, D_FF, D_MODEL), D_FF),
        'norm_f_w': gain(ks[20], (D_MODEL,)),
    }

def first_block(x, norm1_w, w_in, conv_w, a_log, dt_bias, dn_norm_w, cmp_pe_k, cmp_w1_k, cmp_w2_k,
              cmp_pe_v, cmp_w1_v, cmp_w2_v, w_up_nsa, w_up_dn, w_o, norm2_w, w_ffn_gate, w_ffn_up,
              w_ffn_down, norm_f_w):
    b, s, _ = x.shape
    cos, sin = rope_tables(s)
    for l in range(DEPTH):
        h = rms_norm(x, norm1_w[l])
        proj = h @ w_in[l]
        nsa_q, nsa_kv, nsa_g, dn_qkv, dn_z, dn_a, dn_b, merge_g = jnp.split(proj, split_points(), axis=-1)
        q = apply_rope(nsa_q.reshape(b, s, NSA_HEADS, HEAD_DIM), cos, sin)
        o_nsa = nsa_mixer(q, nsa_kv, nsa_g, cmp_pe_k[l], cmp_w1_k[l], cmp_w2_k[l],
                          cmp_pe_v[l], cmp_w1_v[l], cmp_w2_v[l], cos, sin).astype(x.dtype)
        o_dn = gated_deltanet(dn_qkv, dn_z, dn_a, dn_b, conv_w[l], a_log[l], dt_bias[l], dn_norm_w[l]).astype(x.dtype)
        g_nsa, g_dn = jnp.split(jax.nn.sigmoid(merge_g), 2, axis=-1)
        mixed = g_nsa * (o_nsa @ w_up_nsa[l]) + g_dn * (o_dn @ w_up_dn[l])
        x = x + mixed @ w_o[l]
        h2 = rms_norm(x, norm2_w[l])
        x = x + (jax.nn.silu(h2 @ w_ffn_gate[l]) * (h2 @ w_ffn_up[l])) @ w_ffn_down[l]
    return rms_norm(x, norm_f_w)


D_MIX = D_MODEL
RWKV_HEAD = 64
RWKV_WIDTH = D_MIX // 2
RWKV_HEADS = RWKV_WIDTH // RWKV_HEAD
DECAY_LORA = 64
AAA_LORA = 64
GATE_LORA = 160
GN_EPS = 64e-5
QK_NOPE = 128
QK_ROPE = 64
V_HEAD = 128
MLA_WIDTH = D_MIX - RWKV_WIDTH
MLA_HEADS = MLA_WIDTH // V_HEAD
Q_LORA = 512
KV_LORA = 512
Q_BLOCK = 128
D_FF_2 = 5632
CONV_W = 3
NEG_INF_2 = -1e30

IN_SPLITS_2 = (RWKV_WIDTH, RWKV_WIDTH, RWKV_WIDTH, DECAY_LORA, AAA_LORA, GATE_LORA,
             Q_LORA, KV_LORA, QK_ROPE)
D_IN = sum(IN_SPLITS_2)
RWKV_SHIFT_DIM = 3 * RWKV_WIDTH + DECAY_LORA + AAA_LORA + GATE_LORA


def _split(t, sizes):
    idx = np.cumsum(sizes)[:-1].tolist()
    return jnp.split(t, idx, axis=-1)

def rms_norm_2(x, g):
    xf = x.astype(jnp.float32)
    y = xf * lax.rsqrt(jnp.mean(xf * xf, axis=-1, keepdims=True) + NORM_EPS)
    return (y * g.astype(jnp.float32)).astype(x.dtype)

def token_shift(h, mu):
    prev = jnp.pad(h, ((0, 0), (1, 0), (0, 0)))[:, :-1]
    return h + (prev - h) * mu

def apply_rope_2(t, positions):
    half = t.shape[-1] // 2
    inv_freq = ROPE_THETA ** (-jnp.arange(half, dtype=jnp.float32) / half)
    ang = positions.astype(jnp.float32)[..., None] * inv_freq
    ang = ang.reshape(ang.shape[:2] + (1,) * (t.ndim - 3) + (half,))
    cos, sin = jnp.cos(ang), jnp.sin(ang)
    tf = t.astype(jnp.float32)
    t1, t2 = tf[..., :half], tf[..., half:]
    return jnp.concatenate([t1 * cos - t2 * sin, t2 * cos + t1 * sin], axis=-1).astype(t.dtype)

def rwkv7_scan(r, w, k, v, a, b):
    bsz, _, h, n = r.shape

    def step(state, inp):
        r_t, w_t, k_t, v_t, a_t, b_t = inp
        sa = jnp.einsum('bhvk,bhk->bhv', state, a_t)
        state = (state * w_t[:, :, None, :]
                 + sa[..., None] * b_t[:, :, None, :]
                 + v_t[..., None] * k_t[:, :, None, :])
        return state, jnp.einsum('bhvk,bhk->bhv', state, r_t)

    init = jnp.zeros((bsz, h, n, n), jnp.float32)
    xs = tuple(jnp.moveaxis(t, 1, 0) for t in (r, w, k, v, a, b))
    _, out = lax.scan(step, init, xs)
    return jnp.moveaxis(out, 0, 1)

def rwkv7_mixer(h_r, h_k, h_v, h_w, h_a, h_g, w0, w2, a0, a2, g2, k_k, k_a, r_k, gn_w, gn_b):
    f32 = jnp.float32
    bsz, s, c = h_r.shape
    hd = (bsz, s, RWKV_HEADS, RWKV_HEAD)
    r = h_r.astype(f32)
    k = h_k.astype(f32)
    v = h_v.astype(f32)
    w_log = -jax.nn.softplus(-(w0.astype(f32) + jnp.tanh(h_w.astype(f32)) @ w2.astype(f32))) - 0.5
    decay = jnp.exp(-jnp.exp(w_log))
    a = jax.nn.sigmoid(a0.astype(f32) + h_a.astype(f32) @ a2.astype(f32))
    g = jax.nn.sigmoid(h_g.astype(f32)) @ g2.astype(f32)
    kk = (k * k_k).reshape(hd)
    kk = kk * lax.rsqrt(jnp.maximum(jnp.sum(kk * kk, axis=-1, keepdims=True), 1e-24))
    k = k * (1.0 + (a - 1.0) * k_a)
    r, k, v, decay, a = (t.reshape(hd) for t in (r, k, v, decay, a))
    y = rwkv7_scan(r, decay, k, v, -kk, kk * a)
    mu = jnp.mean(y, axis=-1, keepdims=True)
    var = jnp.mean(jnp.square(y - mu), axis=-1, keepdims=True)
    y = ((y - mu) * lax.rsqrt(var + GN_EPS)).reshape(bsz, s, c) * gn_w + gn_b
    bonus = jnp.sum(r * k * r_k, axis=-1, keepdims=True) * v
    return (y + bonus.reshape(bsz, s, c)) * g

def mla_mixer(c_q, c_kv, k_pe, positions, q_norm_g, w_uq, kv_norm_g, w_ukv):
    f32 = jnp.float32
    bsz, s, _ = c_q.shape
    q = (rms_norm_2(c_q, q_norm_g) @ w_uq).reshape(bsz, s, MLA_HEADS, QK_NOPE + QK_ROPE)
    q_nope = q[..., :QK_NOPE]
    q_pe = apply_rope_2(q[..., QK_NOPE:], positions)
    kv = (rms_norm_2(c_kv, kv_norm_g) @ w_ukv).reshape(bsz, s, MLA_HEADS, QK_NOPE + V_HEAD)
    k_nope, v = kv[..., :QK_NOPE], kv[..., QK_NOPE:]
    k_pe = apply_rope_2(k_pe, positions)
    scale = (QK_NOPE + QK_ROPE) ** -0.5
    outs = []
    for i in range(s // Q_BLOCK):
        q0, q1 = i * Q_BLOCK, (i + 1) * Q_BLOCK
        sc = (jnp.einsum('bqhd,bkhd->bhqk', q_nope[:, q0:q1], k_nope[:, :q1])
              + jnp.einsum('bqhr,bkr->bhqk', q_pe[:, q0:q1], k_pe[:, :q1])).astype(f32) * scale
        causal = (q0 + jnp.arange(Q_BLOCK))[:, None] >= jnp.arange(q1)[None, :]
        p = jax.nn.softmax(jnp.where(causal, sc, NEG_INF_2), axis=-1)
        outs.append(jnp.einsum('bhqk,bkhd->bqhd', p.astype(v.dtype), v[:, :q1]))
    return jnp.concatenate(outs, axis=1).reshape(bsz, s, MLA_WIDTH)

def conv_glu_ffn(h, w_gate, w_up, conv_w, conv_b, w_down):
    gate = h @ w_gate
    gate = lax.conv_general_dilated(
        gate, conv_w[:, None, :].astype(gate.dtype), window_strides=(1,),
        padding=[(CONV_W - 1, 0)], dimension_numbers=('NWC', 'WIO', 'NWC'),
        feature_group_count=D_FF_2) + conv_b
    return (jax.nn.silu(gate) * (h @ w_up)) @ w_down

def second_inputs(seed: int = 0) -> dict:
    key = jax.random.key(seed)
    ks = jax.random.split(key, 32)
    L = DEPTH

    def nrm(k, shape, scale):
        return jax.random.normal(k, shape, jnp.float32) * scale

    def gain(k, shape):
        return 1.0 + nrm(k, shape, 0.05)

    x = nrm(ks[0], (BATCH, SEQ, D_MODEL), 1.0)
    offset = jax.random.randint(ks[1], (BATCH, 1), 0, 4096, dtype=jnp.int32)
    positions = offset + jnp.arange(SEQ, dtype=jnp.int32)[None, :]
    return {
        'x': x,
        'positions': positions,
        'attn_norm_g': gain(ks[2], (L, D_MODEL)),
        'w_in': nrm(ks[3], (L, D_MODEL, D_IN), D_MODEL ** -0.5),
        'rwkv_mu': jax.random.uniform(ks[4], (L, RWKV_SHIFT_DIM), jnp.float32),
        'rwkv_w0': jax.random.uniform(ks[5], (L, RWKV_WIDTH), jnp.float32, -6.0, -1.0),
        'rwkv_w2': nrm(ks[6], (L, DECAY_LORA, RWKV_WIDTH), 0.1 * DECAY_LORA ** -0.5),
        'rwkv_a0': nrm(ks[7], (L, RWKV_WIDTH), 0.5),
        'rwkv_a2': nrm(ks[8], (L, AAA_LORA, RWKV_WIDTH), 0.5 * AAA_LORA ** -0.5),
        'rwkv_g2': nrm(ks[9], (L, GATE_LORA, RWKV_WIDTH), GATE_LORA ** -0.5),
        'rwkv_k_k': 0.85 + nrm(ks[10], (L, RWKV_WIDTH), 0.05),
        'rwkv_k_a': gain(ks[11], (L, RWKV_WIDTH)),
        'rwkv_r_k': nrm(ks[12], (L, RWKV_HEADS, RWKV_HEAD), 0.1),
        'rwkv_gn_w': gain(ks[13], (L, RWKV_WIDTH)),
        'rwkv_gn_b': nrm(ks[14], (L, RWKV_WIDTH), 0.02),
        'mla_q_norm_g': gain(ks[15], (L, Q_LORA)),
        'mla_w_uq': nrm(ks[16], (L, Q_LORA, MLA_HEADS * (QK_NOPE + QK_ROPE)), Q_LORA ** -0.5),
        'mla_kv_norm_g': gain(ks[17], (L, KV_LORA)),
        'mla_w_ukv': nrm(ks[18], (L, KV_LORA, MLA_HEADS * (QK_NOPE + V_HEAD)), KV_LORA ** -0.5),
        'w_out': nrm(ks[19], (L, D_MIX, D_MODEL), D_MIX ** -0.5),
        'ffn_norm_g': gain(ks[20], (L, D_MODEL)),
        'ffn_w_gate': nrm(ks[21], (L, D_MODEL, D_FF_2), D_MODEL ** -0.5),
        'ffn_w_up': nrm(ks[22], (L, D_MODEL, D_FF_2), D_MODEL ** -0.5),
        'ffn_conv_w': nrm(ks[23], (L, CONV_W, D_FF_2), CONV_W ** -0.5),
        'ffn_conv_b': nrm(ks[24], (L, D_FF_2), 0.02),
        'ffn_w_down': nrm(ks[25], (L, D_FF_2, D_MODEL), D_FF_2 ** -0.5),
        'final_norm_g': gain(ks[26], (D_MODEL,)),
    }

def second_block(x, positions, attn_norm_g, w_in, rwkv_mu, rwkv_w0, rwkv_w2, rwkv_a0, rwkv_a2,
              rwkv_g2, rwkv_k_k, rwkv_k_a, rwkv_r_k, rwkv_gn_w, rwkv_gn_b, mla_q_norm_g,
              mla_w_uq, mla_kv_norm_g, mla_w_ukv, w_out, ffn_norm_g, ffn_w_gate, ffn_w_up,
              ffn_conv_w, ffn_conv_b, ffn_w_down, final_norm_g):
    for l in range(DEPTH):
        h = rms_norm_2(x, attn_norm_g[l])
        proj = h @ w_in[l]
        shifted = token_shift(proj[..., :RWKV_SHIFT_DIM], rwkv_mu[l])
        h_r, h_k, h_v, h_w, h_a, h_g = _split(shifted, IN_SPLITS_2[:6])
        c_q, c_kv, k_pe = _split(proj[..., RWKV_SHIFT_DIM:], IN_SPLITS_2[6:])
        y_rwkv = rwkv7_mixer(h_r, h_k, h_v, h_w, h_a, h_g, rwkv_w0[l], rwkv_w2[l], rwkv_a0[l],
                             rwkv_a2[l], rwkv_g2[l], rwkv_k_k[l], rwkv_k_a[l], rwkv_r_k[l],
                             rwkv_gn_w[l], rwkv_gn_b[l])
        y_mla = mla_mixer(c_q, c_kv, k_pe, positions, mla_q_norm_g[l], mla_w_uq[l],
                          mla_kv_norm_g[l], mla_w_ukv[l])
        y = jnp.concatenate([y_rwkv.astype(x.dtype), y_mla.astype(x.dtype)], axis=-1)
        x = x + y @ w_out[l]
        h = rms_norm_2(x, ffn_norm_g[l])
        x = x + conv_glu_ffn(h, ffn_w_gate[l], ffn_w_up[l], ffn_conv_w[l], ffn_conv_b[l],
                             ffn_w_down[l]).astype(x.dtype)
    return rms_norm_2(x, final_norm_g)


def setup_inputs(seed=0):
    out = dict(first_inputs(seed))
    for name, value in second_inputs(seed + 1).items():
        if name != "x":
            out[name + "_2"] = value
    return out


def reference(
    x, norm1_w, w_in, conv_w, a_log, dt_bias, dn_norm_w, cmp_pe_k, cmp_w1_k, cmp_w2_k, cmp_pe_v,
    cmp_w1_v, cmp_w2_v, w_up_nsa, w_up_dn, w_o, norm2_w, w_ffn_gate, w_ffn_up, w_ffn_down,
    norm_f_w, positions_2, attn_norm_g_2, w_in_2, rwkv_mu_2, rwkv_w0_2, rwkv_w2_2, rwkv_a0_2,
    rwkv_a2_2, rwkv_g2_2, rwkv_k_k_2, rwkv_k_a_2, rwkv_r_k_2, rwkv_gn_w_2, rwkv_gn_b_2,
    mla_q_norm_g_2, mla_w_uq_2, mla_kv_norm_g_2, mla_w_ukv_2, w_out_2, ffn_norm_g_2,
    ffn_w_gate_2, ffn_w_up_2, ffn_conv_w_2, ffn_conv_b_2, ffn_w_down_2, final_norm_g_2,
):
    x = first_block(
        x, norm1_w, w_in, conv_w, a_log, dt_bias, dn_norm_w, cmp_pe_k, cmp_w1_k, cmp_w2_k,
        cmp_pe_v, cmp_w1_v, cmp_w2_v, w_up_nsa, w_up_dn, w_o, norm2_w, w_ffn_gate, w_ffn_up,
        w_ffn_down, norm_f_w,
    )
    return second_block(
        x, positions_2, attn_norm_g_2, w_in_2, rwkv_mu_2, rwkv_w0_2, rwkv_w2_2, rwkv_a0_2,
        rwkv_a2_2, rwkv_g2_2, rwkv_k_k_2, rwkv_k_a_2, rwkv_r_k_2, rwkv_gn_w_2, rwkv_gn_b_2,
        mla_q_norm_g_2, mla_w_uq_2, mla_kv_norm_g_2, mla_w_ukv_2, w_out_2, ffn_norm_g_2,
        ffn_w_gate_2, ffn_w_up_2, ffn_conv_w_2, ffn_conv_b_2, ffn_w_down_2, final_norm_g_2,
    )


_drawn_inputs = setup_inputs


def setup_inputs(seed=0):
    import zlib

    import numpy as np

    out = dict(_drawn_inputs(seed))
    spreads = {}
    factors = {'norm1_w': 3.36,
     'dn_norm_w': 6.308,
     'cmp_pe_k': 8.0,
     'cmp_pe_v': 8.0,
     'norm2_w': 3.164,
     'rwkv_w2_2': 30.72,
     'rwkv_k_k_2': 13.705,
     'rwkv_gn_w_2': 10.665,
     'rwkv_gn_b_2': 29.752,
     'mla_q_norm_g_2': 8.0,
     'mla_kv_norm_g_2': 5.349,
     'ffn_conv_b_2': 18.685,
     'rwkv_k_a_2': 2.95,
     'ffn_norm_g_2': 4.994}
    for name, (base, spread) in spreads.items():
        noise = np.random.default_rng([zlib.crc32(name.encode()), seed]).standard_normal(out[name].shape)
        drawn = base * np.exp(spread * noise) if base else spread * noise
        out[name] = jnp.asarray(drawn.astype(out[name].dtype))
    for name, factor in factors.items():
        out[name] = (out[name] * factor).astype(out[name].dtype)
    return out
```

```python
from contextlib import ExitStack

import numpy as np
import concourse.bass as bass
from concourse import mybir

F32 = mybir.dt.float32
I32 = mybir.dt.int32
ALU = mybir.AluOpType
ACT = mybir.ActivationFunctionType
AX = mybir.AxisListType
MUL, ADD, SUB, MAX = ALU.mult, ALU.add, ALU.subtract, ALU.max

SEQ = 256
DM = 2048
BLK = 2048
RING = 6
NEG = -1e30
EPS = 1e-6


class Queue:

    def __init__(self, sem, serial):
        self.sem, self.serial, self.n, self.ops, self.seen = sem, serial, 0, [], {}

    def wait(self, *toks):
        for t in toks:
            if t is None:
                continue
            if isinstance(t, list):
                self.wait(*t)
                continue
            sem, v = t
            if self.seen.get(id(sem), 0) < v:
                self.seen[id(sem)] = v
                self.ops.append(lambda e, sem=sem, v=v: e.wait_ge(sem, v))

    def do(self, fn, *toks):
        self.wait(*toks)
        if self.serial and self.n:
            self.wait((self.sem, self.n))
        self.n += 1
        sem = self.sem
        self.ops.append(lambda e: fn(e).then_inc(sem, 1))
        return (self.sem, self.n)

    def raw(self, fn):
        self.ops.append(fn)

    def last(self):
        return (self.sem, self.n) if self.n else None


class Bank:
    def __init__(self, ap):
        self.ap, self.free = ap, []


class Banks:
    def __init__(self, banks):
        self.b, self.i = banks, 0

    def take(self):
        self.i += 1
        return self.b[(self.i - 1) % len(self.b)]


class Arena:
    def __init__(self, ap, n):
        self.ap, self.n, self.at = ap, n, 0

    def take(self, *dims):
        size = 1
        for d in dims:
            size *= d
        a = self.ap[:, self.at:self.at + size]
        self.at += size
        assert self.at <= self.n, (self.at, self.n)
        return shaped(a, dims)


def shaped(a, dims):
    if len(dims) == 1:
        return a
    if len(dims) == 2:
        return a.rearrange("p (a b) -> p a b", a=dims[0])
    return a.rearrange("p (a b c) -> p a b c", a=dims[0], b=dims[1])


def over(ap, n):
    return ap.unsqueeze(2).to_broadcast([ap.shape[0], ap.shape[1], n])


def rep(ap, n):
    return ap.unsqueeze(1).to_broadcast([ap.shape[0], n, ap.shape[1]])


def layout():
    at, out = 0, {}
    for name, n in [
        ("ident", 128), ("ones", 128), ("bones", 128), ("utri", 128), ("M1", 128), ("MT", 7 * 128),
        ("zero", 128), ("causal", 128), ("causalT", 128), ("SU", 128),
        ("head", 2), ("R1", 128), ("R2", 128), ("cos1", 256), ("sin1", 256), ("inv2", 1), ("cmpmask", 32), ("anyv", 2),
        ("eps", 1), ("eps128", 1), ("eps64", 1), ("zc", 1), ("halfpi", 1),
        ("norm1", 16), ("norm2", 16), ("normf", 16), ("attn_g", 16), ("ffn_g", 16), ("final_g", 16),
        ("conv", 4 * 24), ("a_log", 8), ("dt_bias", 8), ("dn_norm", 1), ("pe_k", 32), ("pe_v", 32),
        ("w2k", 128), ("w2v", 128), ("mu", 27), ("w0", 8), ("a0", 8), ("k_k", 8), ("k_a", 8), ("r_k", 8),
        ("gn_w", 8), ("gn_b", 8), ("qn", 4), ("kvn", 4), ("conv2", 3 * 44), ("conv2b", 44),
    ]:
        out[name] = (at, n)
        at += n
    return out, at


def build(nc):
    cols, NC = layout()
    specs = []
    ctx = ExitStack()
    with ctx:
        def sb(name, n, dt=F32):
            return ctx.enter_context(nc.sbuf_tensor(name, [128, n], dt))

        def sem(name):
            return ctx.enter_context(nc.semaphore(name))

        cst = sb("cst", NC)
        xT_ = sb("xT", 16 * SEQ)
        hT_ = sb("hT", 16 * SEQ)
        yT_ = sb("yT", 16 * SEQ)
        ring = sb("ring", RING * BLK)
        posi = sb("posi", SEQ, I32)
        NU = (nc.sbuf_bytes_remaining // 4 // 64) * 64 - 64
        U_ = sb("U", NU)
        psum = [ctx.enter_context(nc.psum_tensor(f"ps{i}", [128, 512], F32)) for i in range(8)]
        banks = [Bank(p) for p in psum]

        PE = Queue(sem("s_pe"), False)
        DV = Queue(sem("s_dve"), True)
        AC = Queue(sem("s_act"), True)
        PO = Queue(sem("s_pool"), True)
        SP = Queue(sem("s_sp"), False)
        s_cst, s_x, s_pos, s_out, s_lora = sem("s_cst"), sem("s_x"), sem("s_pos"), sem("s_out"), sem("s_lora")
        s_ring = [sem(f"s_ring{i}") for i in range(RING)]

        d_cst = nc.dram_tensor("in_cst_dram", [128, NC], F32, kind="ExternalInput").ap()
        d_x = nc.dram_tensor("in_x_dram", [128, 16 * SEQ], F32, kind="ExternalInput").ap()
        d_pos = nc.dram_tensor("in_pos_dram", [128, SEQ], I32, kind="ExternalInput").ap()
        d_lora = nc.dram_tensor("in_lora_dram", [128, 3 * 1024], F32, kind="ExternalInput").ap()
        d_out = nc.dram_tensor("out_0_dram", [128, 16 * SEQ], F32, kind="ExternalOutput").ap()
        stream = {}

        xT = shaped(xT_[:, :], (16, SEQ))
        hT = shaped(hT_[:, :], (16, SEQ))
        yT = shaped(yT_[:, :], (16, SEQ))

        def C(name, a=0, b=None):
            at, n = cols[name]
            return cst[:, at + a:at + (n if b is None else b)]

        ident, ones, bones = C("ident"), C("ones"), C("bones")

        released = []

        def load(m):
            slot = m % RING

            def fn(e):
                if m < len(specs):
                    off, n = stream["at"][m]
                    e.dma_start(ring[:, slot * BLK:slot * BLK + n],
                                stream["ap"][off:off + 128 * n].rearrange("(p n) -> p n", p=128))\
                        .then_inc(s_ring[slot], 16)
            return fn

        class Block:
            def __init__(self, name, k0, kt, cl):
                self.m = len(specs)
                assert kt * len(cl) <= BLK
                assert self.m < RING or (self.m - RING) in released
                specs.append((name, k0, kt, list(cl)))
                self.nc = len(cl)
                self.base = (self.m % RING) * BLK
                self.tok = (s_ring[self.m % RING], 16 * (self.m // RING + 1))

            def tile(self, k, a, b):
                at = self.base + k * self.nc
                return ring[:, at + a:at + b]

            def release(self, tok):
                released.append(self.m)
                SP.wait(tok)
                SP.raw(load(self.m + RING))

        SP.raw(lambda e: e.dma_start(cst[:, :], d_cst).then_inc(s_cst, 16))
        SP.raw(lambda e: e.dma_start(xT_[:, :], d_x).then_inc(s_x, 16))
        for m in range(RING):
            SP.raw(load(m))
        SP.raw(lambda e: e.dma_start(posi[:, :], d_pos).then_inc(s_pos, 16))
        t_cst, t_x, t_pos, t_lora = (s_cst, 16), (s_x, 16), (s_pos, 16), (s_lora, 16)
        for q in (PE, DV, AC, PO):
            q.wait(t_cst)

        def mm(out, l, r, start, stop):
            PE.raw(lambda e: e.matmul(out, l, r, start=start, stop=stop))

        def mml(out, l, r, start, stop):
            return PE.do(lambda e: e.matmul(out, l, r, start=start, stop=stop))

        def trl(out, i):
            return PE.do(lambda e: e.transpose(out, i, ident))

        def act(out, i, f, *toks, scale=1.0, bias=None):
            if bias is None:
                return AC.do(lambda e: e.activation(out, i, f, scale=scale), *toks)
            return AC.do(lambda e: e.activation(out, i, f, scale=scale, bias=bias), *toks)

        def copy(out, i, *toks, scale=1.0):
            return act(out, i, ACT.Copy, *toks, scale=scale)

        def tt(q, out, a, b, op, *toks):
            return q.do(lambda e: e.tensor_tensor(out, a, b, op), *toks)

        def ts(q, out, a, s1, s2, op0, op1, *toks):
            return q.do(lambda e: e.tensor_scalar(out, a, s1, s2, op0, op1), *toks)

        def ts1(q, out, a, s1, op0, *toks):
            return q.do(lambda e: e.tensor_scalar(out, a, s1, None, op0), *toks)

        def stt(q, out, a, s, b, op0, op1, *toks):
            return q.do(lambda e: e.scalar_tensor_tensor(out=out, in0=a, scalar=s, in1=b, op0=op0, op1=op1), *toks)

        def recip(out, a, *toks):
            return DV.do(lambda e: e.reciprocal(out, a), *toks)

        def red(out, a, op, *toks):
            return DV.do(lambda e: e.tensor_reduce(out, a, AX.X, op), *toks)

        def until(key, table):
            while key not in table:
                yield

        gbanks = Banks(banks[0:2])
        done = {}

        def tgemm(name, tiles, kt, rhs, pre, evac, k0=0):
            tpb = max(1, 16 // kt)
            blk = None
            for g in range(0, len(tiles), 2):
                b = gbanks.take()
                out = shaped(b.ap[:, :], (2, SEQ))
                PE.wait(b.free, pre)
                two = tiles[g:g + 2]
                count = 0
                for u, cl in enumerate(two):
                    i = g + u
                    for ka in range(0, kt, 16):
                        kn = min(16, kt - ka)
                        if i % tpb == 0:
                            blk = Block(name, k0 + ka, kn, [c for t in tiles[i:i + tpb] for c in t])
                            PE.wait(blk.tok)
                        at = (i % tpb) * 128
                        for k in range(kn):
                            f = mml if k == kn - 1 else mm
                            tok = f(out[:, u, :], blk.tile(k, at, at + 128), rhs(ka + k),
                                    ka + k == 0, ka + k == kt - 1)
                            count += 1
                            if count % 8 == 0 and k < kn - 1:
                                yield
                        if i % tpb == tpb - 1 or i == len(tiles) - 1:
                            blk.release(tok)
                        if (i % tpb == tpb - 1) and count % 8 == 0:
                            yield
                b.free = [None]
                r = evac(g // 2, out[:, 0:len(two), :], tok)
                if hasattr(r, "send"):
                    r = yield from r
                b.free = [r]
                yield

        def rowgemm(name, cl, kt, lhs, pre, evac):
            per = BLK // len(cl)
            blks = [Block(name, a, min(per, kt - a), cl) for a in range(0, kt, per)]
            for i in range(2):
                b = gbanks.take()
                PE.wait(b.free, pre)
                for k in range(kt):
                    blk = blks[k // per]
                    PE.wait(blk.tok)
                    f = mml if k % per == per - 1 or k == kt - 1 else mm
                    tok = f(b.ap[:, 0:len(cl)], lhs(k, i), blk.tile(k % per, 0, len(cl)), k == 0, k == kt - 1)
                    if i and (k % per == per - 1 or k == kt - 1):
                        blk.release(tok)
                b.free = [evac(i, b.ap[:, 0:len(cl)], tok)]

            yield

        def norm(src, gain, dst, kt, pre, war=None, feats=DM):
            b = gbanks.take()
            n = 4
            sq = []
            for j in range(0, kt, n):
                o, i = dst[:, j:j + n, :], src[:, j:j + n, :]
                if (j // n) % 2:
                    sq.append(tt(DV, o, i, i, MUL, pre, war))
                else:
                    sq.append(act(o, i, ACT.Square, pre, war))
            PE.wait(b.free)
            for k in range(kt):
                PE.wait(sq[k // n])
                f = mml if k == kt - 1 else mm
                tok = f(b.ap[:, 0:SEQ], ones, dst[:, k, :], k == 0, k == kt - 1)
            rt = rtmp[:, 0:SEQ]
            t = act(rt, b.ap[:, 0:SEQ], ACT.Sqrt, tok, DV.last(), scale=1.0 / feats, bias=C("eps"))
            b.free = [t]
            t = recip(rt, rt, t)
            toks = []
            for k in range(kt):
                toks.append(stt(DV, dst[:, k, :], src[:, k, :], C(gain, k, k + 1), rt, MUL, MUL, tok))
            return toks

        ar = Arena(U_[:, :], NU)
        rtmp = ar.take(SEQ)

        def hk(k):
            return hT[:, k, :]

        def hki(k, i):
            return hT[:, k, i * 128:(i + 1) * 128]

        def C128(a):
            return list(range(a, a + 128))

        def tiles_of(a, n):
            return [C128(a + 128 * i) for i in range(n)]

        t_h = norm(xT, "norm1", hT, 16, t_x)[-1]

        Q0, KV0, NG0, DQ0, DZ0, DA0, DB0, MG0 = 0, 1024, 2560, 2584, 5656, 6680, 6688, 6696

        mark1 = ar.at
        qT = ar.take(8, SEQ)
        ksT, kwT = ar.take(2, SEQ), ar.take(2, SEQ)
        vs, vw = ar.take(2, 256), ar.take(2, 256)
        kc = ar.take(32)
        vc = ar.take(2, 128)
        kv_at = ar.at
        kcT_, vcT = ar.take(2, SEQ), ar.take(2, SEQ)
        rp1 = ar.take(2, SEQ)
        at0 = ar.at
        Bb = ar.take(32, 33)
        hid, hid2 = ar.take(33), ar.take(33)
        ar.at = at0
        Sb = [ar.take(1024), U_[:, kv_at:kv_at + 1024]]
        PT = [ar.take(4, 128) for _ in range(5)]
        assert ar.at >= at0 + 33 * 34
        mxb, smb = ar.take(4), ar.take(4)
        dn0 = ar.at
        gl = ar.take(2, 40)
        gate = ar.take(2, 24)
        beta = ar.take(2, 8)
        gdec = ar.take(2, 8)
        gct, ngc, kdf = ar.take(2, 8), ar.take(2, 8), ar.take(2, 8)
        ea, sp1, sp2 = ar.take(8), ar.take(2, 8), ar.take(2, 8)

        side = {}

        def rope(buf, cosn, sinn, R, t, key, rb, tmp, nt):
            b = rb.take()
            PE.wait(b.free, t)
            v = shaped(b.ap[:, 0:nt * SEQ], (nt, SEQ))
            t1 = mml(v, R, buf, True, True)
            t2 = tt(DV, tmp, v, rep(sinn, nt), MUL, t1)
            b.free = [t2]
            t2 = tt(DV, buf, buf, rep(cosn, nt), MUL, t1)
            t2 = tt(DV, buf, buf, tmp, ADD)
            done[key] = t2

        nb = Banks(banks[2:5])
        db = Banks(banks[5:8])
        t_raw = {}

        def keep(dst, key):
            def evac(g, ap, tok):
                t = copy(dst, ap, tok)
                t_raw[key] = t
                return t
            return evac

        def main1a():
            for g in range(4):
                yield from tgemm("w_in", tiles_of(Q0 + 256 * g, 2), 16, hk, t_h, keep(qT[:, 2 * g:2 * g + 2, :], ("q", g)))
            for key, j, dst in (("kc", 0, kcT_), ("vc", 1, vcT), ("ks", 2, ksT), ("kw", 4, kwT)):
                yield from tgemm("w_in", tiles_of(KV0 + 256 * j, 2), 16, hk, t_h, keep(dst, key))
            for key, j, dst in (("vs", 3, vs), ("vw", 5, vw)):
                def ev(i, ap, tok, dst=dst, key=key):
                    t = copy(dst[:, i, :], ap, tok)
                    t_raw[key] = t
                    return t
                yield from rowgemm("w_in", list(range(KV0 + 256 * j, KV0 + 256 * j + 256)), 16, hki, t_h, ev)

            def evg(i, ap, tok):
                t = copy(gl[:, i, :], ap, tok)
                t_raw["gl"] = t
                return t
            yield from rowgemm("w_in", list(range(NG0, NG0 + 24)) + list(range(DA0, DA0 + 16)), 16, hki, t_h, evg)

        def gates():
            yield from until("gl", t_raw)
            t = act(gate, gl[:, :, 0:24], ACT.Tanh, t_raw["gl"], scale=0.5)
            t = ts(DV, gate, gate, 0.5, 0.5, MUL, ADD, t)
            for i in range(2):
                g3 = gate[:, i, :].rearrange("p (h b) -> p h b", b=3)[:, :, 0]
                t = ts1(DV, g3, g3, C("anyv", i, i + 1), MUL)
            done["gate"] = t
            yield
            t = act(beta, gl[:, :, 32:40], ACT.Tanh, scale=0.5)
            t = ts(DV, beta, beta, 0.5, 0.5, MUL, ADD, t)
            t = tt(DV, sp1, gl[:, :, 24:32], rep(C("dt_bias"), 2), ADD)
            t = ts1(DV, sp2, sp1, -1.0, MUL)
            t = tt(DV, sp2, sp2, sp1, ALU.min)
            t = act(sp2, sp2, ACT.Exp, t)
            t = act(sp2, sp2, ACT.Ln, bias=C("ones", 0, 1))
            t1 = act(ea, C("a_log"), ACT.Exp)
            yield
            t = ts1(DV, sp1, sp1, 0.0, MAX)
            t = tt(DV, sp1, sp1, sp2, ADD, t1)
            t = stt(DV, gdec, sp1, -1.0, rep(ea, 2), MUL, MUL)
            b = db.take()
            PE.wait(b.free, t)
            g16 = gdec.rearrange("p a b -> p (a b)")
            mml(b.ap[:, 0:16], C("utri"), g16, True, True)
            t = mml(b.ap[:, 16:32], ones, g16, True, True)
            yield
            gc16 = gct.rearrange("p a b -> p (a b)")
            t = copy(gc16, b.ap[:, 0:16], t)
            t1 = copy(ngc.rearrange("p a b -> p (a b)"), b.ap[:, 0:16], scale=-1.0)
            t = tt(DV, kdf.rearrange("p a b -> p (a b)"), b.ap[:, 16:32], gc16, SUB, t1)
            b.free = [t]
            t = act(kdf, kdf, ACT.Exp, t)
            done["dn"] = t
            yield

        def compress(src, key, pe, w1, w2, is_k):
            yield from until(key, t_raw)
            t0 = t_raw[key]
            if is_k:
                yield from until("rope" + key, done)
                t0 = done["rope" + key]
            t = DV.do(lambda e: e.memset(Bb, 0.0), PE.last())
            for h in range(2):
                for half in range(2):
                    o = Bb[:, 16 * half:16 * half + 16, 16 * h:16 * h + 15]
                    i = src[:, h, 16 * half:16 * half + 240].rearrange("p (n j) -> p j n", j=16)
                    t = DV.do(lambda e, o=o, i=i: e.tensor_copy(o, i), t0)
            o = Bb[:, :, 32]
            t = DV.do(lambda e: e.tensor_copy(o, C(pe)))
            yield
            b = nb.take()
            PE.wait(b.free, t)
            for half in range(2):
                blk = Block(w1, 16 * half, 16, range(128))
                PE.wait(blk.tok)
                for j in range(16):
                    f = mml if j == 15 else mm
                    tok = f(b.ap[:, 0:33], blk.tile(j, 0, 128), Bb[:, 16 * half + j, :],
                            half == 0 and j == 0, half == 1 and j == 15)
                blk.release(tok)
            yield
            t = copy(hid, b.ap[:, 0:33], tok)
            b.free = [t]
            x = hid[:, 0:32]
            u = hid2[:, 0:32]
            t = ts1(DV, x, x, hid[:, 32:33], ADD, t)
            t = tt(DV, u, x, x, MUL)
            t = ts(DV, u, u, 0.044715, 1.0, MUL, ADD)
            t = tt(DV, u, u, x, MUL)
            yield
            t = act(u, u, ACT.Tanh, t, scale=0.7978845608028654)
            t = stt(DV, u, u, 1.0, x, ADD, MUL, t)
            b = nb.take()
            PE.wait(b.free, t)
            if is_k:
                t = mml(b.ap[:, 0:32], C(w2), u, True, True)
                yield
                t = copy(kc, b.ap[:, 0:32], t, scale=0.5)
                b.free = [t]
                done["kc"] = t
            else:
                for h in range(2):
                    t = mml(b.ap[0:16, 128 * h:128 * h + 128], hid2[:, 16 * h:16 * h + 16], C(w2), True, True)
                yield
                t = copy(vc[0:16, :, :], shaped(b.ap[0:16, 0:256], (2, 128)), t, scale=0.5)
                b.free = [t]
                done["vc"] = t
            yield

        def softmax4(S, nk, t, mult):
            t = red(mxb, S, MAX, t)
            t = tt(DV, S, S, over(mxb, nk), SUB)
            yield
            t = act(S, S, ACT.Exp, t)
            yield
            t = red(smb, S, ADD, t)
            t = recip(smb, smb)
            if mult is not None:
                t = tt(DV, smb, smb, mult, MUL)
            t = tt(DV, S, S, over(smb, nk), MUL)
            yield
            return t

        def score_banks(rb, i, pair, scale, S, war):
            nk = 128 * (i + 1)
            per = 512 // nk
            for a in range(0, 4, per):
                b = rb.take()
                PE.wait(b.free)
                v = shaped(b.ap[:, :], (per, nk))
                for h in range(a, a + per):
                    tok = pair(h, v[:, h - a, :], nk)
                yield
                m = C("causal") if i == 0 else cst[:, cols["zero"][0]:cols["zero"][0] + 256]
                t = stt(DV, S[:, a:a + per, :], v, scale, rep(m, per), MUL, ADD, tok, war)
                b.free = [t]
            yield
            return t

        def turn(rb, S, j, dst, t, war):
            b = rb.take()
            PE.wait(b.free, t)
            for h in range(4):
                tok = trl(b.ap[:, 128 * h:128 * h + 128], S[:, h, 128 * j:128 * j + 128])
            yield
            t = copy(dst, shaped(b.ap[:, :], (4, 128)), tok, war)
            b.free = [t]
            yield
            return t, tok

        def nsa():
            for g in range(4):
                yield from until(("q", g), t_raw)
                rope(qT[:, 2 * g:2 * g + 2, :], C("cos1"), C("sin1"), C("R1"), t_raw[("q", g)], ("rq", g), nb, rp1, 2)
                yield
            yield from until("kc", t_raw)
            rope(kcT_, C("cos1"), C("sin1"), C("R1"), t_raw["kc"], "ropekc", nb, rp1, 2)
            yield
            yield from compress(kcT_, "kc", "pe_k", "cmp_w1_k", "w2k", True)
            yield from compress(vcT, "vc", "pe_v", "cmp_w1_v", "w2v", False)
            yield from until("ks", t_raw)
            rope(ksT, C("cos1"), C("sin1"), C("R1"), t_raw["ks"], "ropeks", nb, rp1, 2)
            yield
            yield from until("kw", t_raw)
            rope(kwT, C("cos1"), C("sin1"), C("R1"), t_raw["kw"], "ropekw", nb, rp1, 2)
            yield from until("vw", t_raw)
            yield from until("gate", done)
            t_q = done[("rq", 3)]
            scale = 128 ** -0.5
            free_S = [done["kc"], done["vc"]]
            free_S2 = [[done["kc"], done["vc"]], [done["kc"], done["vc"]]]
            free_PT = [[done["kc"], done["vc"]] for _ in range(5)]
            turn_n = 0
            for kv in range(2):
                for i in range(2):
                    q = [qT[:, 4 * kv + h, 128 * i:128 * i + 128] for h in range(4)]
                    gt = gate[:, i, :].rearrange("p (h b) -> p h b", b=3)[:, 4 * kv:4 * kv + 4, :]
                    s = turn_n % 2
                    turn_n += 1
                    S = shaped(Sb[s][:, 0:64], (4, 16))
                    b = nb.take()
                    PE.wait(b.free, t_q, done["kc"])
                    for h in range(4):
                        tok = mml(b.ap[:, 16 * h:16 * h + 16], q[h], kc[:, 16 * kv:16 * kv + 16], True, True)
                    yield
                    t = stt(DV, S, shaped(b.ap[:, 0:64], (4, 16)), scale, rep(C("cmpmask", 16 * i, 16 * i + 16), 4),
                            MUL, ADD, tok, free_S2[s])
                    b.free = [t]
                    t = yield from softmax4(S, 16, t, gt[:, :, 0])
                    b = nb.take()
                    PE.wait(b.free, t)
                    for h in range(4):
                        tok = trl(b.ap[0:16, 128 * h:128 * h + 128], S[:, h, :])
                    yield
                    free_S2[s] = [tok]
                    t = copy(PT[0][0:16, :, :], shaped(b.ap[0:16, :], (4, 128)), tok, free_PT[0])
                    b.free = [t]
                    pt = [(PT[0][0:16, :, :], vc[0:16, kv, :], t, 0)]
                    n = 1
                    for br, kT, v, key in ((1, ksT, vs, "vs"), (2, kwT, vw, "vw")):
                        s = turn_n % 2
                        turn_n += 1
                        nk = 128 * (i + 1)
                        S = shaped(Sb[s][:, 0:4 * nk], (4, nk))

                        def pair(h, out, nk, kT=kT):
                            PE.wait(done["ropeks"], done["ropekw"])
                            return mml(out, q[h], kT[:, kv, 0:nk], True, True)
                        t = yield from score_banks(nb, i, pair, scale, S, free_S2[s])
                        t = yield from softmax4(S, nk, t, gt[:, :, br])
                        for j in range(i + 1):
                            t2, tok = yield from turn(nb, S, j, PT[n], t, free_PT[n])
                            pt.append((PT[n], v[:, j, 128 * kv:128 * kv + 128], [t2, t_raw[key]], n))
                            n += 1
                        free_S2[s] = [tok]
                    b = nb.take()
                    PE.wait(b.free)
                    for h in range(4):
                        for j, (P, v, t, _) in enumerate(pt):
                            PE.wait(t, done["vc"])
                            f = mml if j == len(pt) - 1 else mm
                            tok = f(b.ap[:, 128 * h:128 * h + 128], v, P[:, h, :], j == 0, j == len(pt) - 1)
                    for (_, _, _, n) in pt:
                        free_PT[n] = [tok]
                    yield
                    t = copy(yT[:, 4 * kv:4 * kv + 4, 128 * i:128 * i + 128], shaped(b.ap[:, :], (4, 128)), tok)
                    b.free = [t]
                    yield
            done["nsa"] = t

        def invert(rb, X, XT, LT, Y, CT, t_x, t_xt, t_lt, war):
            ty, tp = war, None
            tx, txt = t_x, t_xt
            for lev in range(1, 7):
                tc = tt(PO, CT, LT, rep(C("MT", 128 * lev, 128 * lev + 128), 4), MUL, t_lt, ty)
                b = rb.take()
                PE.wait(b.free, tc, tx)
                for m in range(4):
                    tok = mml(b.ap[:, 128 * m:128 * m + 128], CT[:, m, :], X[:, m, :], True, True)
                yield
                ty = tok
                te = copy(Y, shaped(b.ap[:, :], (4, 128)), tok, tp)
                b.free = [te]
                yield
                if lev < 6:
                    b = rb.take()
                    PE.wait(b.free, te, txt)
                    for m in range(4):
                        tok = mml(b.ap[:, 128 * m:128 * m + 128], XT[:, m, :], Y[:, m, :], True, True)
                b2 = rb.take()
                PE.wait(b2.free, te, txt)
                for m in range(4):
                    tok2 = mml(b2.ap[:, 128 * m:128 * m + 128], Y[:, m, :], XT[:, m, :], True, True)
                tp = tok2
                yield
                if lev < 6:
                    tx = tt(DV, X, X, shaped(b.ap[:, :], (4, 128)), SUB, tok)
                    b.free = [tx]
                txt = tt(DV, XT, XT, shaped(b2.ap[:, :], (4, 128)), SUB, tok2)
                b2.free = [txt]
                yield
            return txt

        raw = [ar.take(6, 259) for _ in range(2)]
        zr = [ar.take(2, SEQ) for _ in range(2)]
        cv = ar.take(6, SEQ)
        tm = ar.take(6, SEQ)
        EG, DT = ar.take(4, 128), ar.take(4, 128)
        UG, Dd, CTm = [shaped(tm[:, 2 * j:2 * j + 2, :].rearrange("p a b -> p (a b)"), (4, 128)) for j in range(3)]
        Kg, qd, Vr, Kd = ar.take(2, 128), ar.take(2, 128), ar.take(4, 128), ar.take(2, 128)
        Lm, LTm, At = [ar.take(4, 128) for _ in range(3)]
        Xm, XTm, Ym = EG, DT, Lm
        Rr, VN, Sd = ar.take(2, 128), ar.take(4, 128), ar.take(2, 128)
        free_raw = {}
        for r in raw:
            t_pad = PO.do(lambda e, r=r: e.memset(r[:, :, 0:3], 0.0))

        def main1b():
            for g in range(4):
                for n, base in enumerate((DQ0, DQ0 + 1024, DQ0 + 2048, DZ0)):
                    def evac(_, ap, tok, n=n, g=g):
                        if g >= 2:
                            yield from until(g - 2, free_raw)
                        w = free_raw[g - 2] if g >= 2 else None
                        dst = zr[g % 2] if n == 3 else raw[g % 2][:, 2 * n:2 * n + 2, 3:259]
                        t = copy(dst, ap, tok, w)
                        if n == 3:
                            t_raw[("dn", g)] = t
                        return t
                    yield from tgemm("w_in", tiles_of(base + 256 * g, 2), 16, hk, t_h, evac)

        def deltanet():
            yield from until("dn", done)
            for g in range(4):
                yield from until(("dn", g), t_raw)
                R = raw[g % 2]
                t_in = t_raw[("dn", g)]
                for s in range(3):
                    for h in range(2):
                        n = 2 * s + h
                        ct = 8 * s + 2 * g + h
                        w = [C("conv", 24 * j + ct, 24 * j + ct + 1) for j in range(4)]
                        t = ts1(DV, cv[:, n, :], R[:, n, 0:256], w[0], MUL, t_in, t_pad, PE.last())
                        for j in range(1, 4):
                            t = stt(DV, cv[:, n, :], R[:, n, j:j + 256], w[j], cv[:, n, :], MUL, ADD)
                    yield
                t = act(tm, cv, ACT.Tanh, t, PO.last(), scale=0.5)
                yield
                t = stt(DV, cv, tm, 1.0, cv, ADD, MUL, t)
                t = act(tm[:, 0:4, :], cv[:, 0:4, :], ACT.Square, t, scale=0.5)
                yield
                for s in range(2):
                    b = db.take()
                    PE.wait(b.free, t)
                    v = shaped(b.ap[:, :], (2, SEQ))
                    tok = mml(v, ones, tm[:, 2 * s:2 * s + 2, :], True, True)
                    t2 = act(tm[:, 2 * s:2 * s + 2, :], v, ACT.Sqrt, tok, scale=(128.0, 1.0)[s], bias=C(("eps128", "eps")[s]))
                    b.free = [t2]
                yield
                t = recip(tm[:, 0:4, :], tm[:, 0:4, :], t2)
                t = stt(DV, cv[:, 0:4, :], cv[:, 0:4, :], 0.5, tm[:, 0:4, :], MUL, MUL)
                t = ts1(DV, cv[:, 4:6, :], cv[:, 4:6, :], 0.5, MUL)
                t_cv = t
                yield

                def qT_(m):
                    return cv[:, m // 2, 128 * (m % 2):128 * (m % 2) + 128]

                def kT_(m):
                    return cv[:, 2 + m // 2, 128 * (m % 2):128 * (m % 2) + 128]

                def vT_(m):
                    return cv[:, 4 + m // 2, 128 * (m % 2):128 * (m % 2) + 128]

                def col(a, m):
                    hh = 2 * g + m // 2
                    return a[:, m % 2, hh:hh + 1]
                for m in range(4):
                    t = ts1(PO, UG[:, m, :], C("utri"), col(gdec, m), MUL, done["dn"], PE.last(), DV.last())
                b = db.take()
                PE.wait(b.free, t)
                GB = shaped(b.ap[:, :], (4, 128))
                t_gb = mml(GB, ones, UG, True, True)
                yield
                t_eg = act(EG, GB, ACT.Exp, t_gb, DV.last())
                t = tt(DV, DT, GB, rep(C("causalT"), 4), ADD, t_gb, t_eg)
                t1 = stt(DV, Dd, GB, -1.0, rep(C("causal"), 4), MUL, ADD)
                b.free = [t1, t_eg]
                for m in range(4):
                    act(DT[:, m, :], DT[:, m, :], ACT.Exp, t1, bias=col(ngc, m))
                    t_d = act(Dd[:, m, :], Dd[:, m, :], ACT.Exp, bias=col(gct, m))
                yield
                b = db.take()
                PE.wait(b.free, t_cv)
                for m in range(4):
                    tok = mml(b.ap[:, 128 * m:128 * m + 128], kT_(m), kT_(m), True, True)
                for m in range(4):
                    t = stt(DV, Lm[:, m, :], b.ap[:, 128 * m:128 * m + 128], col(beta, m), Dd[:, m, :],
                            MUL, MUL, tok, t_d)
                b.free = [t]
                t_l = t
                b = db.take()
                PE.wait(b.free)
                for m in range(4):
                    tok = mml(b.ap[:, 128 * m:128 * m + 128], kT_(m), qT_(m), True, True)
                t_at = tt(DV, At, shaped(b.ap[:, :], (4, 128)), DT, MUL, tok)
                b.free = [t_at]
                yield
                b = db.take()
                PE.wait(b.free, t_l)
                for m in range(4):
                    tok = trl(b.ap[:, 128 * m:128 * m + 128], Lm[:, m, :])
                yield
                t_lt = copy(LTm, shaped(b.ap[:, :], (4, 128)), tok, PO.last())
                b.free = [t_lt]
                for h in range(2):
                    t = tt(PO, Kg[:, h, :], kT_(2 * h + 1), EG[:, 2 * h + 1, :], MUL, t_eg, t_cv)
                    t_kg = tt(PO, qd[:, h, :], qT_(2 * h + 1), EG[:, 2 * h + 1, :], MUL)
                t = tt(PO, Xm, Lm, rep(C("M1"), 4), MUL, t_l, t_at)
                t = tt(PO, XTm, LTm, rep(C("MT", 0, 128), 4), MUL, t_lt)
                t_x1 = tt(DV, Xm, rep(ident, 4), Xm, SUB, t)
                t_xt1 = tt(DV, XTm, rep(ident, 4), XTm, SUB)
                yield
                b = db.take()
                PE.wait(b.free, t_cv)
                for m in range(4):
                    tok = trl(b.ap[:, 128 * m:128 * m + 128], vT_(m))
                t_v = copy(Vr, shaped(b.ap[:, :], (4, 128)), tok)
                b.free = [t_v]
                b = db.take()
                PE.wait(b.free)
                for h in range(2):
                    tok = trl(b.ap[:, 128 * h:128 * h + 128], kT_(2 * h))
                for h in range(2):
                    t = ts1(DV, Kd[:, h, :], b.ap[:, 128 * h:128 * h + 128], col(kdf, 2 * h), MUL, tok)
                b.free = [t]
                yield
                t_inv = yield from invert(db, Xm, XTm, LTm, Ym, CTm, t_x1, t_xt1, t_lt, None)
                for h in range(2):
                    t = ts1(DV, Rr[:, h, :], Vr[:, 2 * h, :], col(beta, 2 * h), MUL, t_v)
                b = db.take()
                PE.wait(b.free, t, t_inv)
                for h in range(2):
                    tok = mml(b.ap[:, 128 * h:128 * h + 128], XTm[:, 2 * h, :], Rr[:, h, :], True, True)
                t_r0 = tok
                yield
                vn = VN.rearrange("p (h c) n -> p h c n", c=2)
                t_vn = copy(vn[:, :, 0, :], shaped(b.ap[:, 0:256], (2, 128)), tok)
                b.free = [t_vn]
                yield
                b = db.take()
                PE.wait(b.free, t_vn)
                for h in range(2):
                    tok = mml(b.ap[:, 128 * h:128 * h + 128], Kd[:, h, :], VN[:, 2 * h, :], True, True)
                yield
                t_s = copy(Sd, shaped(b.ap[:, 0:256], (2, 128)), tok)
                b.free = [t_s]
                yield
                b = db.take()
                PE.wait(b.free, t_s, t_kg)
                for h in range(2):
                    tok = mml(b.ap[:, 128 * h:128 * h + 128], Kg[:, h, :], Sd[:, h, :], True, True)
                yield
                for h in range(2):
                    t = tt(DV, Rr[:, h, :], Vr[:, 2 * h + 1, :], b.ap[:, 128 * h:128 * h + 128], SUB, tok, t_r0)
                    b.free = [t]
                    t = ts1(DV, Rr[:, h, :], Rr[:, h, :], col(beta, 2 * h + 1), MUL)
                b = db.take()
                PE.wait(b.free, t)
                for h in range(2):
                    tok = mml(b.ap[:, 128 * h:128 * h + 128], XTm[:, 2 * h + 1, :], Rr[:, h, :], True, True)
                yield
                t_vn = copy(vn[:, :, 1, :], shaped(b.ap[:, 0:256], (2, 128)), tok)
                b.free = [t_vn]
                yield
                b = db.take()
                PE.wait(b.free, t_vn, t_at)
                for m in range(4):
                    o = b.ap[:, 128 * m:128 * m + 128]
                    if m % 2:
                        mm(o, Sd[:, m // 2, :], qd[:, m // 2, :], True, False)
                    tok = mml(o, VN[:, m, :], At[:, m, :], m % 2 == 0, True)
                yield
                oc = tm[:, 0:2, :]
                sq = tm[:, 2:4, :]
                zz = tm[:, 4:6, :]
                t_o = copy(oc, shaped(b.ap[:, :], (2, SEQ)), tok)
                b.free = [t_o]
                t = tt(PO, sq, oc, oc, MUL, t_o)
                b = db.take()
                PE.wait(b.free, t)
                tok = mml(b.ap[:, :], ones, sq.rearrange("p a b -> p (a b)"), True, True)
                t_z = act(zz, zr[g % 2], ACT.Tanh, scale=0.5)
                yield
                t = act(sq, shaped(b.ap[:, :], (2, SEQ)), ACT.Sqrt, tok, scale=1.0 / 128, bias=C("eps"))
                b.free = [t]
                t = recip(sq, sq, t)
                t = stt(DV, zz, zz, 1.0, zr[g % 2], ADD, MUL, t_z)
                free_raw[g] = t
                t = stt(DV, oc, oc, C("dn_norm"), sq, MUL, MUL)
                t = stt(DV, yT[:, 8 + 2 * g:10 + 2 * g, :], oc, 0.5, zz, MUL, MUL)
                yield
            done["deltanet"] = t

        mark2 = ar.at
        ar.at = mark1
        mixT = ar.take(16, SEQ)
        sg = [ar.take(2, SEQ) for _ in range(2)]
        assert ar.at <= dn0
        ar.at = mark2
        sgf = [[], []]

        def merge(part, w_up, key):
            yield from until("nsa", done)
            for g in range(8):
                s = g % 2

                def evm(_, ap, tok):
                    t = act(sg[s], ap, ACT.Tanh, tok, sgf[s], done["nsa"], PE_nsa[0], scale=0.5)
                    sgf[s] = [t]
                    return t
                yield from tgemm("w_in", tiles_of(MG0 + DM * part + 256 * g, 2), 16, hk, t_h, evm)
                if g == 0:
                    yield from until(key, done)

                def evu(_, ap, tok):
                    m = mixT[:, 2 * g:2 * g + 2, :]
                    if part == 0:
                        t = stt(DV, m, sg[s], 1.0, ap, ADD, MUL, tok, sgf[s])
                        sgf[s] = [t]
                        return t
                    t0 = stt(DV, sg[s], sg[s], 1.0, ap, ADD, MUL, tok, sgf[s])
                    t = tt(DV, m, m, sg[s], ADD)
                    sgf[s] = [t]
                    done[("mix", g)] = t
                    return t0
                yield from tgemm(w_up, tiles_of(256 * g, 2), 8, lambda k: yT[:, 8 * part + k, :], done[key], evu)
        PE_nsa = [None]

        def wout(name, src, kt, k0, pre, scale=None):
            def ev(g, ap, tok):
                x = xT[:, 2 * g:2 * g + 2, :]
                if scale is None:
                    return tt(DV, x, x, ap, ADD, tok)
                return stt(DV, x, ap, scale, x, MUL, ADD, tok)
            yield from tgemm(name, tiles_of(0, 16), kt, src, pre, ev, k0=k0)

        def run(main, sides, ratio=1, sratio=1):
            alive = [s for s in sides]
            m_alive = True
            stuck = 0
            while m_alive or alive:
                before = (PE.n, DV.n, AC.n, PO.n, len(PE.ops), len(done), len(t_raw), len(free_raw))
                if m_alive:
                    for _ in range(ratio):
                        try:
                            next(main)
                        except StopIteration:
                            m_alive = False
                            break
                for s in list(alive):
                    for _ in range(sratio):
                        try:
                            next(s)
                        except StopIteration:
                            alive.remove(s)
                            break
                after = (PE.n, DV.n, AC.n, PO.n, len(PE.ops), len(done), len(t_raw), len(free_raw))
                stuck = stuck + 1 if after == before else 0
                assert stuck < 50, "no generator moves"

        def main1():
            yield from main1a()
            yield from main1b()
            yield from merge(0, "w_up_nsa", "nsa")
            yield from merge(1, "w_up_dn", "deltanet")
            yield from wout("w_o", lambda k: mixT[:, k, :], 16, 0, done[("mix", 7)], scale=0.5)

        run(main1(), [gates(), nsa(), deltanet()])

        def fence():
            toks = [q.last() for q in (PE, DV, AC, PO)]
            for q in (PE, DV, AC, PO):
                q.wait(toks)

        def ffn1():
            fence()
            ar.at = mark1
            actT = ar.take(44, SEQ)
            tb = [ar.take(2, SEQ) for _ in range(2)]
            t_h = norm(xT, "norm2", hT, 16, None)[-1]
            last = []
            for g in range(22):
                s = g % 2

                def evg(_, ap, tok):
                    t = act(tb[s], ap, ACT.Tanh, tok, last[-2] if g >= 2 else None, scale=0.5)
                    t = stt(DV, tb[s], tb[s], 1.0, ap, ADD, MUL, t)
                    return t
                yield from tgemm("w_ffn_gate", tiles_of(256 * g, 2), 16, hk, t_h, evg)

                def evu(_, ap, tok):
                    t = stt(DV, actT[:, 2 * g:2 * g + 2, :], tb[s], 0.5, ap, MUL, MUL, tok)
                    last.append(t)
                    return t
                yield from tgemm("w_ffn_up", tiles_of(256 * g, 2), 16, hk, t_h, evu)
            yield from wout("w_ffn_down", lambda k: actT[:, k, :], 44, 0, last[-1])
        run(ffn1(), [])

        fence()
        norm(xT, "normf", hT, 16, None)
        t_x = DV.last()
        for a in (0, 8):
            act(xT[:, a:a + 8, :], hT[:, a:a + 8, :], ACT.Copy, t_x)
        t_x = AC.last()
        ar.at = mark1
        lw = ar.take(3, 1024)
        SP.wait(DV.last(), PE.last(), AC.last())
        SP.raw(lambda e: e.dma_start(lw.rearrange("p a b -> p (a b)"), d_lora).then_inc(s_lora, 16))
        t_h = norm(xT, "attn_g", yT, 16, t_x)[-1]
        hT, yT = yT, hT

        cos2, sin2 = ar.take(SEQ), ar.take(SEQ)
        lh = ar.take(4, SEQ)
        cqT, ckvT, kpe = ar.take(4, SEQ), ar.take(4, SEQ), ar.take(2, SEQ)

        def trig():
            n, a = lh[:, 0, :], lh[:, 1, :]
            t = DV.do(lambda e: e.tensor_copy(a, posi[:, :]), t_pos)
            t = ts1(DV, a, a, C("inv2"), MUL)
            for dst, shift in ((sin2, 0.0), (cos2, float(np.float32(np.pi / 2)))):
                t = ts(DV, n, a, 1.0 / (2 * np.pi), shift / (2 * np.pi), MUL, ADD)
                t = ts1(DV, n, n, 12582912.0, ADD)
                t = ts1(DV, n, n, 12582912.0, SUB)
                t = stt(DV, dst, n, -6.28125, a, MUL, ADD)
                t = stt(DV, dst, n, -0.0019340515136718750, dst, MUL, ADD)
                t = stt(DV, dst, n, -float(2 * np.pi - 6.28125 - 0.0019340515136718750), dst, MUL, ADD)
                if shift:
                    t = ts1(DV, dst, dst, shift, ADD)
                t = ts(DV, dst, dst, 3.1415925, -3.1415925, ALU.min, MAX)
                t = act(dst, dst, ACT.Sin, t)
            done["trig"] = t
        trig()

        RK0 = 3072
        PO.wait(DV.last(), PE.last(), AC.last())

        NS = 2
        ws = []
        ws0 = ar.at
        for _ in range(NS):
            w = {}
            w["raw"] = ar.take(3, 257)
            a0 = ar.at
            w["r"], w["k"] = ar.take(SEQ), ar.take(SEQ)
            w["LD"], w["C"], w["E"], w["KK"], w["A"], w["F"] = [ar.take(SEQ) for _ in range(6)]
            end = ar.at
            ar.at = a0
            w["X"], w["XT"], w["CT"], w["Y"] = [ar.take(4, 128) for _ in range(4)]
            assert ar.at == end
            w["v"], w["g"], w["bon"] = [ar.take(SEQ) for _ in range(3)]
            w["AR"] = ar.take(2, 2, 128)
            w["B"], w["K"] = ar.take(2, SEQ), ar.take(2, SEQ)
            w["P1"], w["P2"] = ar.take(4, 256), ar.take(4, 256)
            w["Vp"] = ar.take(2, 2, 128)
            w["SAp"] = ar.take(2, 128)
            w["G"] = ar.take(128)
            w["Br"], w["Kr"] = ar.take(128), ar.take(128)
            w["S"] = ar.take(128)
            w["em"] = ar.take(4)
            ws.append(w)
            PO.do(lambda e, w=w: e.memset(w["raw"][:, :, 0:1], 0.0))
            PO.do(lambda e, w=w: e.memset(w["Vp"], 0.0))
            padz = PO.do(lambda e, w=w: e.memset(w["SAp"], 0.0))
        lraw = shaped(ws[1]["P2"].rearrange("p a b -> p (a b)")[:, 0:771], (3, 257))
        padz = PO.do(lambda e: e.memset(lraw[:, :, 0:1], 0.0))
        for q in (DV, AC, PE):
            q.wait(padz)
        free_rw, t_rw = {}, {}
        mla_at = ar.at

        def main2():
            lt = [C128(RK0), C128(RK0 + 128), list(range(RK0 + 256, RK0 + 288)) + [-1] * 96]

            def evl(g, ap, tok):
                t = copy(lraw[:, 2 * g:2 * g + ap.shape[1], 1:257], ap, tok)
                done[("lraw", g)] = t
                return t
            yield from tgemm("w_in_2", lt, 16, hk, t_h, evl)
            for p in range(8):
                w = ws[p % NS]
                for g in range(2):
                    def evr(_, ap, tok):
                        if p >= NS:
                            yield from until(p - NS, free_rw)
                        t = copy(w["raw"][:, 2 * g:2 * g + ap.shape[1], 1:257], ap, tok,
                                 free_rw[p - NS] if p >= NS else None)
                        if g:
                            t_rw[p] = t
                        return t
                    tl = [C128(128 * p), C128(1024 + 128 * p)] if g == 0 else [C128(2048 + 128 * p)]
                    yield from tgemm("w_in_2", tl, 16, hk, t_h, evr)
            CQ0 = 3360
            for g in range(4):
                dst = (cqT, ckvT)[g // 2][:, 2 * (g % 2):2 * (g % 2) + 2, :]
                yield from tgemm("w_in_2", tiles_of(CQ0 + 256 * g, 2), 16, hk, t_h, keep(dst, ("c", g)))
            pe_cols = list(range(CQ0 + 1024, CQ0 + 1088))
            yield from tgemm("w_in_2", [pe_cols + pe_cols], 16, hk, t_h, keep(kpe[:, 0:1, :], "kpe"))
            t_end = PE.last()
            qn = hT[:, 0:8, :]
            qp = hT[:, 8:12, :]
            done["qn"], done["qp"] = qn, qp
            for key, src, gain in (("cq", cqT, "qn"), ("ckv", ckvT, "kvn")):
                t = [t_raw[("c", g)] for g in range(4)]
                sq = hT[:, 12:16, :]
                t = tt(DV, sq, src, src, MUL, t, t_end, PE.last())
                b = gbanks.take()
                PE.wait(b.free, t)
                for k in range(4):
                    tok = mml(b.ap[:, 0:SEQ], ones, sq[:, k, :], k == 0, k == 3)
                t = act(rtmp, b.ap[:, 0:SEQ], ACT.Sqrt, tok, DV.last(), scale=1.0 / 512, bias=C("eps"))
                b.free = [t]
                t = recip(rtmp, rtmp, t)
                for k in range(4):
                    t = stt(DV, src[:, k, :], src[:, k, :], C(gain, k, k + 1), rtmp, MUL, MUL)
                done["n" + key] = t
                yield

            def evq(g, ap, tok):
                t = copy(hT[:, 2 * g:2 * g + 2, :], ap, tok)
                t_raw[("mq", g)] = t
                return t
            uq = [list(range(192 * h, 192 * h + 128)) for h in range(8)]
            uq += [[192 * h + 128 + j for h in (2 * a, 2 * a + 1) for j in range(64)] for a in range(4)]
            yield from tgemm("mla_w_uq_2", uq, 4, lambda k: cqT[:, k, :], done["ncq"], evq)
            done["mla_q"] = True
            yield from until("rwkv0", done)
            w0 = Arena(U_[:, :], NU)
            w0.at = ws_at[0]
            kn = w0.take(8, SEQ)
            vm = w0.take(2, 1024)
            done["kn"], done["vm"] = kn, vm
            wait0 = [done["rwkv0"]]

            def evk(g, ap, tok):
                t = copy(kn[:, 2 * g:2 * g + 2, :], ap, tok, wait0, PE.last())
                t_raw[("mk", g)] = t
                return t
            yield from tgemm("mla_w_ukv_2", [list(range(256 * h, 256 * h + 128)) for h in range(8)], 4,
                             lambda k: ckvT[:, k, :], done["nckv"], evk)
            for a in range(2):
                def evv(i, ap, tok):
                    t = copy(vm[:, i, 512 * a:512 * a + 512], ap, tok, wait0)
                    t_raw[("mv", a)] = t
                    return t
                vcols = [256 * h + 128 + j for h in range(4 * a, 4 * a + 4) for j in range(128)]
                yield from rowgemm("mla_w_ukv_2", vcols, 4,
                                   lambda k, i: ckvT[:, k, 128 * i:128 * i + 128], done["nckv"], evv)
            done["mla_kv"] = True
            yield from until("rwkv0", done)
            yield from until("rwkv1", done)
            yield from wout("w_out_2", lambda k: yT[:, k, :], 8, 0, [done["rwkv0"], done["rwkv1"]])
            yield from until("mla", done)
            yield from wout("w_out_2", lambda k: yT[:, 8 + k, :], 8, 8, done["mla"])

        def lora():
            for g in range(2):
                yield from until(("lraw", g), done)
            for j in range(3):
                d = lh[:, j, :]
                t = tt(DV, d, lraw[:, j, 0:256], lraw[:, j, 1:257], SUB, done[("lraw", 0)], done[("lraw", 1)],
                       done["trig"])
                t = stt(DV, d, d, C("mu", 24 + j, 25 + j), lraw[:, j, 1:257], MUL, ADD)
                yield
            t1 = ts1(DV, lh[:, 3, :], lh[:, 0, :], C("head", 1, 2), MUL)
            act(lh[:, 0, :], lh[:, 0, :], ACT.Tanh, t1)
            t = act(lh[:, 1:3, :], lh[:, 1:3, :], ACT.Tanh, scale=0.5)
            t = ts(DV, lh[:, 1:3, :], lh[:, 1:3, :], 0.5, 0.5, MUL, ADD, t)
            t = ts1(DV, lh[:, 0, :], lh[:, 0, :], C("head", 0, 1), MUL)
            done["lora"] = t
            yield

        def rwkv(s, rb):
            w = ws[s]
            v, G_, bon, AR, Bt, Kt = w["v"], w["g"], w["bon"], w["AR"], w["B"], w["K"]
            P1, P2, Vp, SAp, G, Br, Kr, S = [w[n] for n in ("P1", "P2", "Vp", "SAp", "G", "Br", "Kr", "S")]
            yield from until("lora", done)
            t_y = None
            for p in range(s, 8, NS):
                yield from until(p, t_rw)
                raw, r, k, LD, Cc, E, KK, A, F = [w[n] for n in ("raw", "r", "k", "LD", "C", "E", "KK", "A", "F")]
                pc = slice(128 * p, 128 * p + 128)
                c1 = slice(p, p + 1)

                def V1(name):
                    return C(name, p, p + 1)
                for j, d in enumerate((r, k, v)):
                    t = tt(DV, d, raw[:, j, 0:256], raw[:, j, 1:257], SUB, t_rw[p], PE.last())
                    t = stt(DV, d, d, C("mu", 8 * j + p, 8 * j + p + 1), raw[:, j, 1:257], MUL, ADD)
                free_rw[p] = t
                t_h3 = t
                b = rb.take()
                PE.wait(b.free, done["lora"], t_lora)
                mml(b.ap[:, 0:256], lw[:, 0, pc], lh[:, 0, :], True, True)
                tok = mml(b.ap[:, 256:512], lw[:, 0, pc], lh[:, 3, :], True, True)
                b2 = rb.take()
                PE.wait(b2.free)
                mml(b2.ap[:, 0:256], lw[:, 1, pc], lh[:, 1, :], True, False)
                tok2 = mml(b2.ap[:, 0:256], lw[:, 2, pc], lh[:, 2, :], False, True)
                yield
                t = ts(DV, LD, b.ap[:, 0:256], V1("w0"), 0.5, ADD, MUL, tok)
                t = ts(DV, A, b.ap[:, 256:512], V1("a0"), 0.5, ADD, MUL)
                b.free = [t]
                act(LD, LD, ACT.Tanh, t)
                act(A, A, ACT.Tanh)
                t = copy(G_, b2.ap[:, 0:256], tok2)
                b2.free = [t]
                yield
                ec = 0.5 * float(np.exp(-0.5))
                t = ts(DV, LD, LD, -ec, -ec, MUL, ADD, t)
                t = ts(DV, A, A, 0.5, 0.5, MUL, ADD)
                t = ts1(DV, KK, k, V1("k_k"), MUL)
                t_kk = act(E, KK, ACT.Square, t)
                for c in range(2):
                    cs = slice(128 * c, 128 * c + 128)
                    t_c = DV.do(lambda e, cs=cs: e.tensor_tensor_scan(Cc[:, cs], ones, LD[:, cs], 0.0, MUL, ADD))
                b = rb.take()
                PE.wait(b.free, t_kk)
                tok = mml(b.ap[:, 0:256], bones, E, True, True)
                yield
                t = ts1(DV, E, b.ap[:, 0:256], 1e-24, MAX, tok)
                b.free = [t]
                t = act(E, E, ACT.Sqrt, t)
                t1 = stt(DV, F, A, -1.0, k, ADD, MUL)
                t1 = stt(DV, k, F, V1("k_a"), k, MUL, ADD)
                yield
                t = recip(E, E, t)
                t = tt(DV, KK, KK, E, MUL)
                t = tt(DV, A, A, KK, MUL)
                t = tt(DV, E, r, k, MUL)
                t = ts1(DV, E, E, V1("r_k"), MUL)
                b = rb.take()
                PE.wait(b.free, t)
                tok = mml(b.ap[:, 0:256], bones, E, True, True)
                yield
                t = tt(DV, bon, b.ap[:, 0:256], v, MUL, tok)
                b.free = [t]
                for c in range(2):
                    cs = slice(128 * c, 128 * c + 128)
                    t = ts1(DV, w["em"][:, c:c + 1], Cc[:, 128 * c + 127:128 * c + 128], 0.5, MUL)
                    t = ts1(DV, E[:, cs], Cc[:, cs], w["em"][:, c:c + 1], SUB)
                t = tt(DV, LD, E, LD, SUB)
                t = tt(DV, w["em"][:, 2:3], w["em"][:, 0:1], w["em"][:, 1:2], ADD)
                yield
                t1 = act(F, LD, ACT.Exp, t)
                t2 = act(Cc, E, ACT.Exp)
                t3 = act(LD, E, ACT.Exp, scale=-1.0)
                t4 = act(w["em"][:, 3:4], w["em"][:, 2:3], ACT.Exp)
                yield
                t = tt(DV, AR[:, :, 0, :], shaped(KK, (2, 128)), shaped(F, (2, 128)), MUL, t1)
                t = tt(DV, AR[:, :, 1, :], shaped(r, (2, 128)), shaped(Cc, (2, 128)), MUL, t2)
                for h in range(2):
                    t = stt(DV, Bt[:, h, :], A, C("head", h, h + 1), LD, MUL, MUL, t3)
                    t_ab = stt(DV, Kt[:, h, :], k, C("head", h, h + 1), LD, MUL, MUL)
                yield
                b = rb.take()
                PE.wait(b.free, t_ab, t_h3)
                tok = trl(b.ap[:, 0:128], v[:, 0:128])
                tok = trl(b.ap[:, 128:256], v[:, 128:256])
                for h in range(2):
                    mml(b.ap[:, 256:384], Bt[:, h, 0:128], ident, h == 0, h == 1)
                for h in range(2):
                    tok = mml(b.ap[:, 384:512], Kt[:, h, 0:128], ident, h == 0, h == 1)
                yield
                for h in range(2):
                    t = copy(Vp[:, :, h, 64 * h:64 * h + 64], shaped(b.ap[:, 0:256], (2, 128))[:, :, 64 * h:64 * h + 64], tok, t_y)
                copy(Br, b.ap[:, 256:384])
                t_rows = copy(Kr, b.ap[:, 384:512])
                b.free = [t_rows]
                SUm = C("SU")
                for h in range(2):
                    for P, src in ((P1, Bt), (P2, Kt)):
                        b = rb.take()
                        PE.wait(b.free)
                        for c in range(2):
                            tok = mml(b.ap[:, 256 * c:256 * c + 256], src[:, h, 128 * c:128 * c + 128],
                                      AR[:, c, :, :].rearrange("p a b -> p (a b)"), True, True)
                        yield
                        bv = b.ap[:, :].rearrange("p (c a n) -> p c a n", c=2, a=2)
                        Pv = P.rearrange("p m (a n) -> p m a n", a=2)[:, 2 * h:2 * h + 2, :, :]
                        t = tt(DV, Pv[:, :, 0, :], bv[:, :, 0, :], rep(SUm, 2), MUL, tok)
                        t = tt(DV, Pv[:, :, 1, :], bv[:, :, 1, :], rep(C("utri"), 2), MUL)
                        b.free = [t]
                t_p = t
                X, XT, CT, Y = w["X"], w["XT"], w["CT"], w["Y"]
                b = rb.take()
                PE.wait(b.free)
                for h in range(2):
                    for c in range(2):
                        m = 2 * h + c
                        tok = mml(b.ap[:, 128 * m:128 * m + 128], AR[:, c, 0, :], Bt[:, h, 128 * c:128 * c + 128],
                                  True, True)
                yield
                LT = P1[:, :, 0:128]
                t = tt(DV, X, shaped(b.ap[:, :], (4, 128)), rep(C("M1"), 4), MUL, tok, AC.last())
                b.free = [t]
                t_x1 = tt(DV, X, rep(ident, 4), X, SUB)
                t = tt(PO, XT, LT, rep(C("MT", 0, 128), 4), MUL, t_p)
                t_xt1 = tt(PO, XT, rep(ident, 4), XT, SUB)
                yield
                t_inv = yield from invert(rb, X, XT, LT, Y, CT, t_x1, t_xt1, t_p, None)
                for c in range(2):
                    b = rb.take()
                    PE.wait(b.free, t_rows, t_inv)
                    if c == 1:
                        PE.wait(t_s)
                        mm(b.ap[:, 0:128], AR[:, 1, 0, :], S, True, False)
                    for h in range(2):
                        hc = slice(64 * h, 64 * h + 64)
                        tok = mml(b.ap[:, hc], P2[:, 2 * h + c, 0:128], Vp[:, c, h, hc], c == 0, c == 0 or h == 1)
                    yield
                    t = copy(G, b.ap[:, 0:128], tok)
                    b.free = [t]
                    yield
                    b = rb.take()
                    PE.wait(b.free, t)
                    for h in range(2):
                        hc = slice(64 * h, 64 * h + 64)
                        tok = mml(b.ap[:, hc], XT[:, 2 * h + c, :], G[:, hc], True, True)
                    yield
                    for h in range(2):
                        hc = slice(64 * h, 64 * h + 64)
                        t_sa = copy(SAp[:, h, hc], b.ap[:, hc], tok, PE.last(), scale=-1.0)
                    b.free = [t_sa]
                    yield
                    b = rb.take()
                    PE.wait(b.free, t_sa)
                    o = b.ap[:, 0:128]
                    if c == 1:
                        mm(o, S, AR[:, 1, 1, :], True, False)
                    for h in range(2):
                        mm(o, SAp[:, h, :], P1[:, 2 * h + c, 128:256], c == 0 and h == 0, False)
                        tok = mml(o, Vp[:, c, h, :], P2[:, 2 * h + c, 128:256], False, h == 1)
                    if c == 0:
                        b2 = rb.take()
                        PE.wait(b2.free)
                        n = 0
                        for rows, src in ((Br, SAp), (Kr, Vp[:, 0, :, :])):
                            for h in range(2):
                                tok2 = mml(b2.ap[:, 0:128], rows, src[:, h, :], n == 0, n == 3)
                                n += 1
                    yield
                    yc = w["X"].rearrange("p a b -> p (a b)")[:, 0:256]
                    t_yc = copy(yc[:, 128 * c:128 * c + 128], o, tok)
                    b.free = [t_yc]
                    if c == 0:
                        t_s = stt(DV, S, b2.ap[:, 0:128], w["em"][:, 3:4], bones, MUL, MUL, tok2)
                        b2.free = [t_s]
                    yield
                t_y = tok
                sq = w["X"].rearrange("p a b -> p (a b)")[:, 256:512]
                rs = w["CT"].rearrange("p a b -> p (a b)")[:, 0:256]
                b = rb.take()
                PE.wait(b.free, t_yc)
                tok = mml(b.ap[:, 0:256], bones, yc, True, True)
                yield
                t = stt(DV, yc, b.ap[:, 0:256], -1.0 / 64, yc, MUL, ADD, tok)
                b.free = [t]
                t = act(sq, yc, ACT.Square, t)
                b = rb.take()
                PE.wait(b.free, t)
                tok = mml(b.ap[:, 0:256], bones, sq, True, True)
                yield
                t = act(rs, b.ap[:, 0:256], ACT.Sqrt, tok, PE.last(), scale=1.0 / 64, bias=C("eps64"))
                b.free = [t]
                yield
                t = recip(rs, rs, t)
                t = tt(DV, yc, yc, rs, MUL)
                t = ts(DV, yc, yc, V1("gn_w"), V1("gn_b"), MUL, ADD)
                t = tt(DV, yc, yc, bon, ADD)
                t = tt(DV, yT[:, p, :], yc, G_, MUL)
                yield
            done[f"rwkv{s}"] = t

        rb0, rb1 = Banks(banks[2:5]), Banks(banks[5:8])
        ws_at = [0, 0]
        ws_at[0] = ws0
        assert ws_at[0] + NS * ((mla_at - ws_at[0]) // NS) == mla_at
        mxb2 = ar.take(4)
        smb2 = ar.take(4)

        def mla():
            rb = Banks(banks[2:5])
            yield from until("kpe", t_raw)
            rpt = rtmp
            yield from until("mla_q", done)
            yield from until("rwkv0", done)
            yield from until("rwkv1", done)
            yield from until("mla_kv", done)
            qn, qp, kn, vm = done["qn"], done["qp"], done["kn"], done["vm"]
            wa = Arena(U_[:, :], NU)
            wa.at = ws_at[0] + 4096
            tmp = wa.take(2, SEQ)
            Sm = [wa.take(1024), wa.take(1024)]
            PTm = [wa.take(4, 128) for _ in range(4)]
            assert wa.at <= mla_at
            DV.wait(done["rwkv0"], done["rwkv1"], done["trig"], PE.last(), AC.last())
            AC.wait(PE.last(), DV.last())
            for a in range(2):
                rope(qp[:, 2 * a:2 * a + 2, :], cos2, sin2, C("R2"), [t_raw[("mq", 4 + a)]], ("rqp", a), rb, tmp, 2)
                yield
            rope(kpe[:, 0:1, :], cos2, sin2, C("R2"), t_raw["kpe"], "rkpe", rb, tmp[:, 0:1, :], 1)
            ts1(DV, kpe[:, 1, :], kpe[:, 0, :], C("head", 1, 2), MUL)
            done["rkpe"] = ts1(DV, kpe[:, 0, :], kpe[:, 0, :], C("head", 0, 1), MUL)
            yield
            scale = 192 ** -0.5
            free_S = [[], []]
            free_P = [[], [], [], []]
            u = 0
            for a in range(2):
                for i in range(2):
                    nk = 128 * (i + 1)
                    S = shaped(Sm[u % 2][:, 0:4 * nk], (4, nk))

                    def pair(h, out, nk):
                        hh = 4 * a + h
                        PE.wait(t_raw[("mk", 3)], done["rkpe"], done[("rqp", 1)])
                        mm(out, qn[:, hh, 128 * i:128 * i + 128], kn[:, hh, 0:nk], True, False)
                        return mml(out, qp[:, hh // 2, 128 * i:128 * i + 128], kpe[:, hh % 2, 0:nk], False, True)
                    t = yield from score_banks(rb, i, pair, scale, S, free_S[u % 2])
                    t = yield from softmax4b(S, nk, t)
                    pt = []
                    for j in range(i + 1):
                        n = 2 * (u % 2) + j
                        t2, tok = yield from turn(rb, S, j, PTm[n], t, free_P[n])
                        pt.append((PTm[n], j, t2, n))
                    free_S[u % 2] = [tok]
                    b = rb.take()
                    PE.wait(b.free, t_raw[("mv", 1)])
                    for h in range(4):
                        hh = 4 * a + h
                        for x, (P, j, t2, n) in enumerate(pt):
                            PE.wait(t2)
                            tok = mml(b.ap[:, 128 * h:128 * h + 128], vm[:, j, 128 * hh:128 * hh + 128], P[:, h, :],
                                      x == 0, x == len(pt) - 1)
                    for (_, _, _, n) in pt:
                        free_P[n] = [tok]
                    yield
                    t = copy(yT[:, 8 + 4 * a:12 + 4 * a, 128 * i:128 * i + 128], shaped(b.ap[:, :], (4, 128)), tok)
                    b.free = [t]
                    u += 1
                    yield
            done["mla"] = t

        def softmax4b(S, nk, t):
            mx, sm = mxb2, smb2
            t = red(mx, S, MAX, t)
            t = tt(DV, S, S, over(mx, nk), SUB)
            yield
            t = act(S, S, ACT.Exp, t)
            yield
            t = red(sm, S, ADD, t)
            t = recip(sm, sm)
            t = tt(DV, S, S, over(sm, nk), MUL)
            yield
            return t

        t_raw.clear()
        for key in ("kc", "vc"):
            done.pop(key, None)
        run(main2(), [lora(), rwkv(0, rb0), rwkv(1, rb1), mla()])

        def ffn2():
            fence()
            ar.at = mark1
            actT = ar.take(44, SEQ)
            gp = [ar.take(2, 258) for _ in range(2)]
            cb = [ar.take(2, SEQ) for _ in range(2)]
            tb = [ar.take(2, SEQ) for _ in range(2)]
            for x in gp:
                tz = PO.do(lambda e, x=x: e.memset(x[:, :, 0:2], 0.0))
            t_h = norm(xT, "ffn_g", hT, 16, None)[-1]
            last = []
            for g in range(22):
                s = g % 2

                def evg(_, ap, tok):
                    t = copy(gp[s][:, :, 2:258], ap, tok, conv_done[-2] if g >= 2 else None)
                    t_g.append(t)
                    return t
                yield from tgemm("ffn_w_gate_2", tiles_of(256 * g, 2), 16, hk, t_h, evg)
                for u in range(2):
                    ct = 2 * g + u
                    w = [C("conv2", 44 * j + ct, 44 * j + ct + 1) for j in range(3)]
                    o = cb[s][:, u, :]
                    ts(DV, o, gp[s][:, u, 0:256], w[0], C("conv2b", ct, ct + 1), MUL, ADD, t_g[-1], tz)
                    stt(DV, o, gp[s][:, u, 1:257], w[1], o, MUL, ADD)
                    t = stt(DV, o, gp[s][:, u, 2:258], w[2], o, MUL, ADD)
                conv_done.append(t)
                t = act(tb[s], cb[s], ACT.Tanh, t, scale=0.5)
                stt(DV, tb[s], tb[s], 1.0, cb[s], ADD, MUL, t)

                def evu(_, ap, tok):
                    t = stt(DV, actT[:, 2 * g:2 * g + 2, :], tb[s], 0.5, ap, MUL, MUL, tok)
                    last.append(t)
                    return t
                yield from tgemm("ffn_w_up_2", tiles_of(256 * g, 2), 16, hk, t_h, evu)
            yield from wout("ffn_w_down_2", lambda k: actT[:, k, :], 44, 0, last[-1])
        t_g, conv_done = [], []
        run(ffn2(), [])
        fence()
        t_n = norm(xT, "final_g", hT, 16, None)
        hflat = hT.rearrange("p a b -> p (a b)")
        for j in range(4):
            SP.wait(t_n[4 * j + 3])
            SP.raw(lambda e, j=j: e.dma_start(d_out[:, 1024 * j:1024 * j + 1024], hflat[:, 1024 * j:1024 * j + 1024])
                   .then_inc(s_out, 16))
        SP.wait((s_out, 64))

        at, off = [], 0
        for (_, _, kt, cl) in specs:
            at.append((off, kt * len(cl)))
            off += 128 * kt * len(cl)
        stream["at"] = at
        stream["ap"] = nc.dram_tensor("in_w_dram", [off], F32, kind="ExternalInput").ap()

        block = ctx.enter_context(nc.Block())

        @block.sync
        def _(e):
            for f in SP.ops:
                f(e)

        @block.gpsimd
        def _(e):
            for f in PO.ops:
                f(e)

        @block.scalar
        def _(e):
            for f in AC.ops:
                f(e)

        @block.vector
        def _(e):
            for f in DV.ops:
                f(e)

        @block.tensor
        def _(e):
            for f in PE.ops:
                f(e)
    return specs, off


def constants(inp):
    cols, n = layout()
    out = np.zeros((128, n), np.float32)

    def put(name, a):
        at, w = cols[name]
        assert a.shape == (128, w), (name, a.shape)
        out[:, at:at + w] = a

    def chan(v):
        return np.asarray(v).reshape(-1, 128).T

    i = np.arange(128)
    I, J = i[:, None], i[None, :]
    put("ident", np.eye(128, dtype=np.float32))
    put("ones", np.ones((128, 128), np.float32))
    put("bones", (I // 64 == J // 64).astype(np.float32))
    put("utri", (I <= J).astype(np.float32))
    put("SU", (I < J).astype(np.float32))
    put("head", np.stack([i < 64, i >= 64], 1).astype(np.float32))

    def M(s):
        return ((I // s) % 2 == 1) & (J // s == I // s - 1)
    put("M1", M(1).astype(np.float32))
    put("MT", np.concatenate([M(2 ** l).T for l in range(7)], 1).astype(np.float32))
    put("causal", np.where(J <= I, 0, NEG).astype(np.float32))
    put("causalT", np.where(J >= I, 0, NEG).astype(np.float32))
    R1 = np.zeros((128, 128), np.float32)
    R1[i[:64] + 64, i[:64]] = -1
    R1[i[:64], i[:64] + 64] = 1
    put("R1", R1)
    R2 = np.zeros((128, 128), np.float32)
    for b in (0, 64):
        for j in range(32):
            R2[b + j + 32, b + j] = -1
            R2[b + j, b + j + 32] = 1
    put("R2", R2)
    inv1 = (1.0 / (10000.0 ** (np.arange(0, 128, 2) / 128))).astype(np.float32)
    ang = np.arange(SEQ, dtype=np.float32)[None, :] * inv1[i % 64][:, None]
    put("cos1", np.cos(ang))
    put("sin1", np.sin(ang))
    put("inv2", (10000.0 ** (-(i % 32) / 32)).astype(np.float32)[:, None])
    c = np.arange(16)
    cm = [np.where((c[None, :] * 16 + 31 <= (128 * t + i)[:, None]) & (c[None, :] < 15), 0, NEG) for t in range(2)]
    put("cmpmask", np.concatenate(cm, 1).astype(np.float32))
    put("anyv", np.stack([i >= 31, i >= 0], 1).astype(np.float32))
    put("eps", np.full((128, 1), EPS, np.float32))
    put("eps128", np.full((128, 1), 128 * EPS, np.float32))
    put("eps64", np.full((128, 1), 64e-5, np.float32))
    for name, key in (("norm1", "norm1_w"), ("norm2", "norm2_w"), ("normf", "norm_f_w"), ("attn_g", "attn_norm_g_2"),
                      ("ffn_g", "ffn_norm_g_2"), ("final_g", "final_norm_g_2"), ("w0", "rwkv_w0_2"),
                      ("a0", "rwkv_a0_2"), ("k_k", "rwkv_k_k_2"), ("k_a", "rwkv_k_a_2"), ("r_k", "rwkv_r_k_2"),
                      ("gn_w", "rwkv_gn_w_2"), ("gn_b", "rwkv_gn_b_2"), ("qn", "mla_q_norm_g_2"),
                      ("kvn", "mla_kv_norm_g_2"), ("conv2b", "ffn_conv_b_2"), ("dn_norm", "dn_norm_w"),
                      ("conv", "conv_w"), ("conv2", "ffn_conv_w_2")):
        put(name, chan(inp[key]))
    put("a_log", np.broadcast_to(inp["a_log"].reshape(1, 8), (128, 8)))
    put("dt_bias", np.broadcast_to(inp["dt_bias"].reshape(1, 8), (128, 8)))
    put("pe_k", inp["cmp_pe_k"][0].T)
    put("pe_v", inp["cmp_pe_v"][0].T)
    put("w2k", inp["cmp_w2_k"][0])
    put("w2v", inp["cmp_w2_v"][0])
    mu = np.zeros(27 * 128, np.float32)
    mu[:3360] = inp["rwkv_mu_2"].reshape(-1)
    put("mu", chan(mu))
    return out


def kernel(**inputs):
    import concourse.bacc as _bacc
    from concourse.bass_utils import run_bass_kernel_spmd as _run

    inp = {k: np.asarray(v) for k, v in inputs.items()}
    nc = _bacc.Bacc("TRN2", target_bir_lowering=False, num_devices=1)
    specs, total = build(nc)
    w = np.empty(total, np.float32)
    at = 0
    for name, k0, kt, cl in specs:
        src = inp[name].reshape(-1, inp[name].shape[-1])[128 * k0:128 * (k0 + kt)]
        n = len(cl)
        dst = w[at:at + 128 * kt * n].reshape(128, kt, n)
        real = [c for c in cl if c >= 0]
        if real == list(range(real[0], real[0] + len(real))):
            part = src[:, real[0]:real[0] + len(real)]
        else:
            part = src[:, real]
        dst[:, :, len(real):] = 0
        dst[:, :, :len(real)] = part.reshape(kt, 128, len(real)).transpose(1, 0, 2)
        at += 128 * kt * n
    lora = np.zeros((128, 3, 1024), np.float32)
    lora[0:64, 0] = inp["rwkv_w2_2"][0]
    lora[64:128, 0] = inp["rwkv_a2_2"][0]
    lora[:, 1] = inp["rwkv_g2_2"][0][0:128]
    lora[0:32, 2] = inp["rwkv_g2_2"][0][128:160]
    arrays = {
        "in_cst_dram": constants(inp),
        "in_x_dram": np.ascontiguousarray(inp["x"][0].T.reshape(16, 128, SEQ).transpose(1, 0, 2).reshape(128, -1)),
        "in_pos_dram": np.ascontiguousarray(np.broadcast_to(inp["positions_2"].reshape(1, SEQ), (128, SEQ))),
        "in_lora_dram": lora.reshape(128, 3072),
        "in_w_dram": w,
    }
    r = _run(nc, [arrays], core_ids=[0])
    o = r.results[0]["out_0_dram"].reshape(128, 16, SEQ)
    return np.ascontiguousarray(o.transpose(2, 1, 0).reshape(1, SEQ, DM))
```

```python
from contextlib import ExitStack

import numpy as np
import concourse.bass as bass
from concourse import mybir

F32 = mybir.dt.float32
I32 = mybir.dt.int32
ALU = mybir.AluOpType
ACT = mybir.ActivationFunctionType
AX = mybir.AxisListType
MUL, ADD, SUB, MAX = ALU.mult, ALU.add, ALU.subtract, ALU.max

SEQ = 256
DM = 2048
BLK = 1024
RING = 6
HIGH = 4
F32R = mybir.dt.float32r
SPLIT = {"w_in", "w_ffn_gate", "w_ffn_up", "w_ffn_down", "w_in_2", "ffn_w_gate_2", "ffn_w_up_2", "ffn_w_down_2"}
NEG = -1e30
EPS = 1e-6


class Queue:

    def __init__(self, sem, serial):
        self.sem, self.serial, self.n, self.ops, self.seen = sem, serial, 0, [], {}

    def wait(self, *toks):
        for t in toks:
            if t is None:
                continue
            if isinstance(t, list):
                self.wait(*t)
                continue
            sem, v = t
            if self.seen.get(id(sem), 0) < v:
                self.seen[id(sem)] = v
                self.ops.append(lambda e, sem=sem, v=v: e.wait_ge(sem, v))

    def do(self, fn, *toks):
        self.wait(*toks)
        if self.serial and self.n:
            self.wait((self.sem, self.n))
        self.n += 1
        sem = self.sem
        self.ops.append(lambda e: fn(e).then_inc(sem, 1))
        return (self.sem, self.n)

    def raw(self, fn):
        self.ops.append(fn)

    def last(self):
        return (self.sem, self.n) if self.n else None


class Bank:
    def __init__(self, ap):
        self.ap, self.free = ap, []


class Banks:
    def __init__(self, banks):
        self.b, self.i = banks, 0

    def take(self):
        self.i += 1
        return self.b[(self.i - 1) % len(self.b)]


class Arena:
    def __init__(self, ap, n):
        self.ap, self.n, self.at = ap, n, 0

    def take(self, *dims):
        size = 1
        for d in dims:
            size *= d
        a = self.ap[:, self.at:self.at + size]
        self.at += size
        assert self.at <= self.n, (self.at, self.n)
        return shaped(a, dims)


def shaped(a, dims):
    if len(dims) == 1:
        return a
    if len(dims) == 2:
        return a.rearrange("p (a b) -> p a b", a=dims[0])
    return a.rearrange("p (a b c) -> p a b c", a=dims[0], b=dims[1])


def over(ap, n):
    return ap.unsqueeze(2).to_broadcast([ap.shape[0], ap.shape[1], n])


def rep(ap, n):
    return ap.unsqueeze(1).to_broadcast([ap.shape[0], n, ap.shape[1]])


def layout():
    at, out = 0, {}
    for name, n in [
        ("ident", 128), ("ones", 128), ("bones", 128), ("utri", 128), ("M1", 128), ("MT", 7 * 128),
        ("zero", 128), ("causal", 128), ("causalT", 128), ("SU", 128),
        ("head", 2), ("R1", 128), ("R2", 128), ("cos1", 256), ("sin1", 256), ("inv2", 1), ("cmpmask", 32), ("anyv", 2),
        ("eps", 1), ("eps128", 1), ("eps64", 1), ("zc", 1), ("halfpi", 1),
        ("norm1", 16), ("norm2", 16), ("normf", 16), ("attn_g", 16), ("ffn_g", 16), ("final_g", 16),
        ("conv", 4 * 24), ("a_log", 8), ("dt_bias", 8), ("dn_norm", 1), ("pe_k", 32), ("pe_v", 32),
        ("w2k", 128), ("w2v", 128), ("mu", 27), ("w0", 8), ("a0", 8), ("k_k", 8), ("k_a", 8), ("r_k", 8),
        ("gn_w", 8), ("gn_b", 8), ("qn", 4), ("kvn", 4), ("conv2", 3 * 44), ("conv2b", 44),
    ]:
        out[name] = (at, n)
        at += n
    return out, at


def build(nc, known=None):
    cols, NC = layout()
    specs = []
    ctx = ExitStack()
    with ctx:
        base = (nc.sbuf_base + 63) // 64 * 64
        total = (nc.sbuf_bytes_remaining // 4 // 64) * 64 - 64
        ctx.enter_context(nc.sbuf_tensor("all", [128, total], F32))
        place = [0]

        def sb(name, n, dt=F32, at=None):
            if at is None:
                at = place[0]
                place[0] += (n + 15) // 16 * 16
                assert place[0] <= total
            return nc.alloc_sbuf_tensor_at(name, [128, n], dt, offset=base + 4 * at)

        def sem(name):
            return ctx.enter_context(nc.semaphore(name))

        cst = sb("cst", NC)
        xT_ = sb("xT", 16 * SEQ)
        yT_ = sb("yT", 16 * SEQ)
        h_at = place[0]
        hh_ = sb("hh", 16 * SEQ, F32R)
        hl_ = sb("hl", 16 * SEQ, F32R)
        hhF_ = sb("hhF", 16 * SEQ, F32, at=h_at)
        hlF_ = sb("hlF", 16 * SEQ, F32, at=h_at + 16 * SEQ)
        ring_at = place[0]
        ring = sb("ring", RING * BLK)
        ringl = sb("ringl", RING * BLK, F32R, at=ring_at)
        high = sb("high", HIGH * BLK, F32R)
        posi = sb("posi", SEQ, I32)
        u_at = place[0]
        NU = (total - u_at) // 64 * 64
        U_ = sb("U", NU)
        ah_ = sb("ah", 32 * SEQ, F32R, at=u_at + 256)
        al_ = sb("al", 32 * SEQ, F32R, at=u_at + 256 + 32 * SEQ)
        alF_ = sb("alF", 32 * SEQ, F32, at=u_at + 256 + 32 * SEQ)
        psum = [ctx.enter_context(nc.psum_tensor(f"ps{i}", [128, 512], F32)) for i in range(8)]
        banks = [Bank(p) for p in psum]

        PE = Queue(sem("s_pe"), False)
        DV = Queue(sem("s_dve"), True)
        AC = Queue(sem("s_act"), True)
        PO = Queue(sem("s_pool"), True)
        SP = Queue(sem("s_sp"), False)
        s_cst, s_x, s_pos, s_out, s_lora = sem("s_cst"), sem("s_x"), sem("s_pos"), sem("s_out"), sem("s_lora")
        s_ring = [sem(f"s_ring{i}") for i in range(RING)]

        d_cst = nc.dram_tensor("in_cst_dram", [128, NC], F32, kind="ExternalInput").ap()
        d_x = nc.dram_tensor("in_x_dram", [128, 16 * SEQ], F32, kind="ExternalInput").ap()
        d_pos = nc.dram_tensor("in_pos_dram", [128, SEQ], I32, kind="ExternalInput").ap()
        d_lora = nc.dram_tensor("in_lora_dram", [128, 3 * 1024], F32, kind="ExternalInput").ap()
        d_out = nc.dram_tensor("out_0_dram", [128, 16 * SEQ], F32, kind="ExternalOutput").ap()
        stream = {}

        xT = shaped(xT_[:, :], (16, SEQ))
        hh, hl, hhF, hlF = [shaped(a[:, :], (16, SEQ)) for a in (hh_, hl_, hhF_, hlF_)]
        ah, al, alF = [shaped(a[:, :], (32, SEQ)) for a in (ah_, al_, alF_)]
        yT = shaped(yT_[:, :], (16, SEQ))

        def C(name, a=0, b=None):
            at, n = cols[name]
            return cst[:, at + a:at + (n if b is None else b)]

        ident, ones, bones = C("ident"), C("ones"), C("bones")


        def load(m):
            slot = m % RING

            def fn(e):
                if m < len(specs):
                    off, n = stream["at"][m]
                    e.dma_start(ring[:, slot * BLK:slot * BLK + n],
                                stream["ap"][off:off + 128 * n].rearrange("(p n) -> p n", p=128))\
                        .then_inc(s_ring[slot], 16)
            return fn

        known_split = [k for k, sp in enumerate(known or []) if sp[0] in SPLIT]
        order = {m: k for k, m in enumerate(known_split)}
        split_tok, freed = {}, {}

        def arrived(m):
            return (s_ring[m % RING], 16 * (m // RING + 1))

        def split(m):
            k = order[m]
            prev = known_split[k - HIGH] if k >= HIGH else None
            if m >= RING and m - RING not in freed or prev is not None and prev not in freed:
                return False
            _, _, kt, cl = known[m]
            n = kt * len(cl)
            o, g = (m % RING) * BLK, (k % HIGH) * BLK
            half = n // 2
            toks = []
            for x, y in ((0, half), (half, n)):
                t = copy(high[:, g + x:g + y], ring[:, o + x:o + y], arrived(m), freed.get(prev))
                toks.append((x, y, t))
            for x, y, t in toks:
                t = tt(DV, ringl[:, o + x:o + y], ring[:, o + x:o + y], high[:, g + x:g + y], SUB, t)
            split_tok[m] = t
            return True

        def look_ahead(m):
            if known is None:
                return
            for j in range(m, min(m + HIGH, len(known))):
                if j in order and j not in split_tok and not split(j):
                    assert j > m
                    break

        class Block:
            def __init__(self, name, k0, kt, cl):
                self.m = m = len(specs)
                assert kt * len(cl) <= BLK
                assert m < RING or (m - RING) in freed
                specs.append((name, k0, kt, list(cl)))
                assert known is None or known[m] == specs[m]
                self.nc = len(cl)
                self.split = name in SPLIT
                look_ahead(m)
                self.base = (m % RING) * BLK
                self.tok = arrived(m)
                if self.split and known:
                    self.tok = split_tok[m]
                    self.hbase = (order[m] % HIGH) * BLK
                else:
                    self.hbase = 0

            def tile(self, k, a, b):
                at = self.base + k * self.nc
                if self.split:
                    g = self.hbase + k * self.nc
                    return high[:, g + a:g + b], ringl[:, at + a:at + b]
                return ring[:, at + a:at + b], None

            def release(self, tok):
                freed[self.m] = tok
                SP.wait(tok)
                SP.raw(load(self.m + RING))

        def product(out, w, x, start, stop, last, w_moves=False):
            if w[1] is None:
                terms = [(w[0], x[0])]
            else:
                terms = [(w[0], x[0]), (w[0], x[1]), (w[1], x[0])]
            for j, (p, q) in enumerate(terms):
                if w_moves:
                    p, q = q, p
                f = mml if last and j == len(terms) - 1 else mm
                tok = f(out, p, q, start and j == 0, stop and j == len(terms) - 1)
            return tok

        SP.raw(lambda e: e.dma_start(cst[:, :], d_cst).then_inc(s_cst, 16))
        SP.raw(lambda e: e.dma_start(xT_[:, :], d_x).then_inc(s_x, 16))
        for m in range(RING):
            SP.raw(load(m))
        SP.raw(lambda e: e.dma_start(posi[:, :], d_pos).then_inc(s_pos, 16))
        t_cst, t_x, t_pos, t_lora = (s_cst, 16), (s_x, 16), (s_pos, 16), (s_lora, 16)
        for q in (PE, DV, AC, PO):
            q.wait(t_cst)

        def mm(out, l, r, start, stop):
            PE.raw(lambda e: e.matmul(out, l, r, start=start, stop=stop))

        def mml(out, l, r, start, stop):
            return PE.do(lambda e: e.matmul(out, l, r, start=start, stop=stop))

        def trl(out, i):
            return PE.do(lambda e: e.transpose(out, i, ident))

        def act(out, i, f, *toks, scale=1.0, bias=None):
            if bias is None:
                return AC.do(lambda e: e.activation(out, i, f, scale=scale), *toks)
            return AC.do(lambda e: e.activation(out, i, f, scale=scale, bias=bias), *toks)

        def copy(out, i, *toks, scale=1.0):
            return act(out, i, ACT.Copy, *toks, scale=scale)

        def tt(q, out, a, b, op, *toks):
            return q.do(lambda e: e.tensor_tensor(out, a, b, op), *toks)

        def ts(q, out, a, s1, s2, op0, op1, *toks):
            return q.do(lambda e: e.tensor_scalar(out, a, s1, s2, op0, op1), *toks)

        def ts1(q, out, a, s1, op0, *toks):
            return q.do(lambda e: e.tensor_scalar(out, a, s1, None, op0), *toks)

        def stt(q, out, a, s, b, op0, op1, *toks):
            return q.do(lambda e: e.scalar_tensor_tensor(out=out, in0=a, scalar=s, in1=b, op0=op0, op1=op1), *toks)

        def recip(out, a, *toks):
            return DV.do(lambda e: e.reciprocal(out, a), *toks)

        def red(out, a, op, *toks):
            return DV.do(lambda e: e.tensor_reduce(out, a, AX.X, op), *toks)

        def until(key, table):
            while key not in table:
                yield

        gbanks = Banks(banks[0:2])
        done = {}

        def tgemm(name, tiles, kt, rhs, pre, evac, k0=0):
            tpb = max(1, 8 // kt)
            blk = None
            for g in range(0, len(tiles), 2):
                b = gbanks.take()
                out = shaped(b.ap[:, :], (2, SEQ))
                PE.wait(b.free, pre)
                two = tiles[g:g + 2]
                for u, cl in enumerate(two):
                    i = g + u
                    for ka in range(0, kt, 8):
                        kn = min(8, kt - ka)
                        if i % tpb == 0:
                            blk = Block(name, k0 + ka, kn, [c for t in tiles[i:i + tpb] for c in t])
                            PE.wait(blk.tok)
                        at = (i % tpb) * 128
                        for k in range(kn):
                            tok = product(out[:, u, :], blk.tile(k, at, at + 128), rhs(ka + k),
                                          ka + k == 0, ka + k == kt - 1, k == kn - 1)
                        if i % tpb == tpb - 1 or i == len(tiles) - 1:
                            blk.release(tok)
                            yield
                b.free = [None]
                r = evac(g // 2, out[:, 0:len(two), :], tok)
                if hasattr(r, "send"):
                    r = yield from r
                b.free = [r]
                yield

        def rowgemm(name, cl, kt, lhs, pre, evac):
            per = BLK // len(cl)
            b = [gbanks.take() for _ in range(2)]
            PE.wait(b[0].free, b[1].free, pre)
            toks = [None, None]
            for a in range(0, kt, per):
                n = min(per, kt - a)
                blk = Block(name, a, n, cl)
                PE.wait(blk.tok)
                for i in range(2):
                    for k in range(n):
                        toks[i] = product(b[i].ap[:, 0:len(cl)], blk.tile(k, 0, len(cl)), lhs(a + k, i),
                                          a + k == 0, a + k == kt - 1, k == n - 1, w_moves=True)
                blk.release(toks[1])
                if a + n < kt:
                    yield
            for i in range(2):
                b[i].free = [evac(i, b[i].ap[:, 0:len(cl)], toks[i])]
            yield

        def two_part(src, hi, lo, *toks):
            t = copy(hi, src, *toks)
            return tt(DV, lo, src, hi, SUB, t)

        def norm(src, gain, pre, dst=None):
            b = gbanks.take()
            n = 4
            sq = []
            for j in range(0, 16, n):
                o, i = hlF[:, j:j + n, :], src[:, j:j + n, :]
                if (j // n) % 2:
                    sq.append(tt(DV, o, i, i, MUL, pre))
                else:
                    sq.append(act(o, i, ACT.Square, pre))
            PE.wait(b.free)
            for k in range(16):
                PE.wait(sq[k // n])
                f = mml if k == 15 else mm
                tok = f(b.ap[:, 0:SEQ], ones, hlF[:, k, :], k == 0, k == 15)
            rt = rtmp[:, 0:SEQ]
            t = act(rt, b.ap[:, 0:SEQ], ACT.Sqrt, tok, DV.last(), scale=1.0 / DM, bias=C("eps"))
            b.free = [t]
            recip(rt, rt, t)
            toks = []
            for k in range(0, 16, 2):
                o = hlF if dst is None else dst
                for j in (k, k + 1):
                    t = stt(DV, o[:, j, :], src[:, j, :], C(gain, j, j + 1), rt, MUL, MUL, tok)
                if dst is None:
                    t = copy(hh[:, k:k + 2, :], o[:, k:k + 2, :], t)
                    if k:
                        d = slice(k - 2, k)
                        toks[-1] = toks[-2] = tt(DV, hl[:, d, :], hlF[:, d, :], hh[:, d, :], SUB, toks[-1])
                toks += [t, t]
            if dst is None:
                toks[-1] = toks[-2] = tt(DV, hl[:, 14:16, :], hlF[:, 14:16, :], hh[:, 14:16, :], SUB, toks[-1])
            return toks

        ar = Arena(U_[:, :], NU)
        rtmp = ar.take(SEQ)

        th = [None]

        def hk(k):
            PE.wait(th[0][k])
            return hh[:, k, :], hl[:, k, :]

        def hki(k, i):
            PE.wait(th[0][k])
            return hh[:, k, i * 128:(i + 1) * 128], hl[:, k, i * 128:(i + 1) * 128]

        def plain(a):
            return lambda k: (a[:, k, :], None)

        def C128(a):
            return list(range(a, a + 128))

        def tiles_of(a, n):
            return [C128(a + 128 * i) for i in range(n)]

        th[0] = norm(xT, "norm1", t_x)
        t_h = None

        Q0, KV0, NG0, DQ0, DZ0, DA0, DB0, MG0 = 0, 1024, 2560, 2584, 5656, 6680, 6688, 6696

        mark1 = ar.at
        qT = ar.take(8, SEQ)
        ksT, kwT = ar.take(2, SEQ), ar.take(2, SEQ)
        vs, vw = ar.take(2, 256), ar.take(2, 256)
        kc = ar.take(32)
        vc = ar.take(2, 128)
        kv_at = ar.at
        kcT_, vcT = ar.take(2, SEQ), ar.take(2, SEQ)
        rp1 = ar.take(2, SEQ)
        at0 = ar.at
        Bb = ar.take(32, 33)
        hid, hid2 = ar.take(33), ar.take(33)
        ar.at = at0
        Sb = [ar.take(1024), U_[:, kv_at:kv_at + 1024]]
        PT = [ar.take(4, 128) for _ in range(5)]
        assert ar.at >= at0 + 33 * 34
        mxb, smb = ar.take(4), ar.take(4)
        dn0 = ar.at
        gl = ar.take(2, 40)
        gate = ar.take(2, 24)
        beta = ar.take(2, 8)
        gdec = ar.take(2, 8)
        gct, ngc, kdf = ar.take(2, 8), ar.take(2, 8), ar.take(2, 8)
        ea, sp1, sp2 = ar.take(8), ar.take(2, 8), ar.take(2, 8)

        side = {}

        def rope(buf, cosn, sinn, R, t, key, rb, tmp, nt):
            b = rb.take()
            PE.wait(b.free, t)
            v = shaped(b.ap[:, 0:nt * SEQ], (nt, SEQ))
            t1 = mml(v, R, buf, True, True)
            t2 = tt(DV, tmp, v, rep(sinn, nt), MUL, t1)
            b.free = [t2]
            t2 = tt(DV, buf, buf, rep(cosn, nt), MUL, t1)
            t2 = tt(DV, buf, buf, tmp, ADD)
            done[key] = t2

        nb = Banks(banks[2:5])
        db = Banks(banks[5:8])
        t_raw = {}

        def keep(dst, key):
            def evac(g, ap, tok):
                t = copy(dst, ap, tok)
                t_raw[key] = t
                return t
            return evac

        def main1a():
            for g in range(4):
                yield from tgemm("w_in", tiles_of(Q0 + 256 * g, 2), 16, hk, t_h, keep(qT[:, 2 * g:2 * g + 2, :], ("q", g)))
            for key, j, dst in (("kc", 0, kcT_), ("vc", 1, vcT), ("ks", 2, ksT), ("kw", 4, kwT)):
                yield from tgemm("w_in", tiles_of(KV0 + 256 * j, 2), 16, hk, t_h, keep(dst, key))
            for key, j, dst in (("vs", 3, vs), ("vw", 5, vw)):
                def ev(i, ap, tok, dst=dst, key=key):
                    t = copy(dst[:, i, :], ap, tok)
                    t_raw[key] = t
                    return t
                yield from rowgemm("w_in", list(range(KV0 + 256 * j, KV0 + 256 * j + 256)), 16, hki, t_h, ev)

            def evg(i, ap, tok):
                t = copy(gl[:, i, :], ap, tok)
                t_raw["gl"] = t
                return t
            yield from rowgemm("w_in", list(range(NG0, NG0 + 24)) + list(range(DA0, DA0 + 16)), 16, hki, t_h, evg)

        def gates():
            yield from until("gl", t_raw)
            t = act(gate, gl[:, :, 0:24], ACT.Tanh, t_raw["gl"], scale=0.5)
            t = ts(DV, gate, gate, 0.5, 0.5, MUL, ADD, t)
            for i in range(2):
                g3 = gate[:, i, :].rearrange("p (h b) -> p h b", b=3)[:, :, 0]
                t = ts1(DV, g3, g3, C("anyv", i, i + 1), MUL)
            done["gate"] = t
            yield
            t = act(beta, gl[:, :, 32:40], ACT.Tanh, scale=0.5)
            t = ts(DV, beta, beta, 0.5, 0.5, MUL, ADD, t)
            t = tt(DV, sp1, gl[:, :, 24:32], rep(C("dt_bias"), 2), ADD)
            t = ts1(DV, sp2, sp1, -1.0, MUL)
            t = tt(DV, sp2, sp2, sp1, ALU.min)
            t = act(sp2, sp2, ACT.Exp, t)
            t = act(sp2, sp2, ACT.Ln, bias=C("ones", 0, 1))
            t1 = act(ea, C("a_log"), ACT.Exp)
            yield
            t = ts1(DV, sp1, sp1, 0.0, MAX)
            t = tt(DV, sp1, sp1, sp2, ADD, t1)
            t = stt(DV, gdec, sp1, -1.0, rep(ea, 2), MUL, MUL)
            b = db.take()
            PE.wait(b.free, t)
            g16 = gdec.rearrange("p a b -> p (a b)")
            mml(b.ap[:, 0:16], C("utri"), g16, True, True)
            t = mml(b.ap[:, 16:32], ones, g16, True, True)
            yield
            gc16 = gct.rearrange("p a b -> p (a b)")
            t = copy(gc16, b.ap[:, 0:16], t)
            t1 = copy(ngc.rearrange("p a b -> p (a b)"), b.ap[:, 0:16], scale=-1.0)
            t = tt(DV, kdf.rearrange("p a b -> p (a b)"), b.ap[:, 16:32], gc16, SUB, t1)
            b.free = [t]
            t = act(kdf, kdf, ACT.Exp, t)
            done["dn"] = t
            yield

        def compress(src, key, pe, w1, w2, is_k):
            yield from until(key, t_raw)
            t0 = t_raw[key]
            if is_k:
                yield from until("rope" + key, done)
                t0 = done["rope" + key]
            t = DV.do(lambda e: e.memset(Bb, 0.0), PE.last())
            for h in range(2):
                for half in range(2):
                    o = Bb[:, 16 * half:16 * half + 16, 16 * h:16 * h + 15]
                    i = src[:, h, 16 * half:16 * half + 240].rearrange("p (n j) -> p j n", j=16)
                    t = DV.do(lambda e, o=o, i=i: e.tensor_copy(o, i), t0)
            o = Bb[:, :, 32]
            t = DV.do(lambda e: e.tensor_copy(o, C(pe)))
            yield
            b = nb.take()
            PE.wait(b.free, t)
            for a in range(0, 32, 8):
                blk = Block(w1, a, 8, range(128))
                PE.wait(blk.tok)
                for j in range(8):
                    f = mml if j == 7 else mm
                    tok = f(b.ap[:, 0:33], blk.tile(j, 0, 128)[0], Bb[:, a + j, :], a + j == 0, a + j == 31)
                blk.release(tok)
                yield
            yield
            t = copy(hid, b.ap[:, 0:33], tok)
            b.free = [t]
            x = hid[:, 0:32]
            u = hid2[:, 0:32]
            t = ts1(DV, x, x, hid[:, 32:33], ADD, t)
            t = tt(DV, u, x, x, MUL)
            t = ts(DV, u, u, 0.044715, 1.0, MUL, ADD)
            t = tt(DV, u, u, x, MUL)
            yield
            t = act(u, u, ACT.Tanh, t, scale=0.7978845608028654)
            t = stt(DV, u, u, 1.0, x, ADD, MUL, t)
            b = nb.take()
            PE.wait(b.free, t)
            if is_k:
                t = mml(b.ap[:, 0:32], C(w2), u, True, True)
                yield
                t = copy(kc, b.ap[:, 0:32], t, scale=0.5)
                b.free = [t]
                done["kc"] = t
            else:
                for h in range(2):
                    t = mml(b.ap[0:16, 128 * h:128 * h + 128], hid2[:, 16 * h:16 * h + 16], C(w2), True, True)
                yield
                t = copy(vc[0:16, :, :], shaped(b.ap[0:16, 0:256], (2, 128)), t, scale=0.5)
                b.free = [t]
                done["vc"] = t
            yield

        def softmax4(S, nk, t, mult):
            t = red(mxb, S, MAX, t)
            t = tt(DV, S, S, over(mxb, nk), SUB)
            yield
            t = act(S, S, ACT.Exp, t)
            yield
            t = red(smb, S, ADD, t)
            t = recip(smb, smb)
            if mult is not None:
                t = tt(DV, smb, smb, mult, MUL)
            t = tt(DV, S, S, over(smb, nk), MUL)
            yield
            return t

        def score_banks(rb, i, pair, scale, S, war):
            nk = 128 * (i + 1)
            per = 512 // nk
            for a in range(0, 4, per):
                b = rb.take()
                PE.wait(b.free)
                v = shaped(b.ap[:, :], (per, nk))
                for h in range(a, a + per):
                    tok = pair(h, v[:, h - a, :], nk)
                yield
                m = C("causal") if i == 0 else cst[:, cols["zero"][0]:cols["zero"][0] + 256]
                t = stt(DV, S[:, a:a + per, :], v, scale, rep(m, per), MUL, ADD, tok, war)
                b.free = [t]
            yield
            return t

        def turn(rb, S, j, dst, t, war):
            b = rb.take()
            PE.wait(b.free, t)
            for h in range(4):
                tok = trl(b.ap[:, 128 * h:128 * h + 128], S[:, h, 128 * j:128 * j + 128])
            yield
            t = copy(dst, shaped(b.ap[:, :], (4, 128)), tok, war)
            b.free = [t]
            yield
            return t, tok

        def nsa():
            for g in range(4):
                yield from until(("q", g), t_raw)
                rope(qT[:, 2 * g:2 * g + 2, :], C("cos1"), C("sin1"), C("R1"), t_raw[("q", g)], ("rq", g), nb, rp1, 2)
                yield
            yield from until("kc", t_raw)
            rope(kcT_, C("cos1"), C("sin1"), C("R1"), t_raw["kc"], "ropekc", nb, rp1, 2)
            yield
            yield from compress(kcT_, "kc", "pe_k", "cmp_w1_k", "w2k", True)
            yield from compress(vcT, "vc", "pe_v", "cmp_w1_v", "w2v", False)
            yield from until("ks", t_raw)
            rope(ksT, C("cos1"), C("sin1"), C("R1"), t_raw["ks"], "ropeks", nb, rp1, 2)
            yield
            yield from until("kw", t_raw)
            rope(kwT, C("cos1"), C("sin1"), C("R1"), t_raw["kw"], "ropekw", nb, rp1, 2)
            yield from until("vw", t_raw)
            yield from until("gate", done)
            t_q = done[("rq", 3)]
            scale = 128 ** -0.5
            free_S = [done["kc"], done["vc"]]
            free_S2 = [[done["kc"], done["vc"]], [done["kc"], done["vc"]]]
            free_PT = [[done["kc"], done["vc"]] for _ in range(5)]
            turn_n = 0
            for kv in range(2):
                for i in range(2):
                    q = [qT[:, 4 * kv + h, 128 * i:128 * i + 128] for h in range(4)]
                    gt = gate[:, i, :].rearrange("p (h b) -> p h b", b=3)[:, 4 * kv:4 * kv + 4, :]
                    s = turn_n % 2
                    turn_n += 1
                    S = shaped(Sb[s][:, 0:64], (4, 16))
                    b = nb.take()
                    PE.wait(b.free, t_q, done["kc"])
                    for h in range(4):
                        tok = mml(b.ap[:, 16 * h:16 * h + 16], q[h], kc[:, 16 * kv:16 * kv + 16], True, True)
                    yield
                    t = stt(DV, S, shaped(b.ap[:, 0:64], (4, 16)), scale, rep(C("cmpmask", 16 * i, 16 * i + 16), 4),
                            MUL, ADD, tok, free_S2[s])
                    b.free = [t]
                    t = yield from softmax4(S, 16, t, gt[:, :, 0])
                    b = nb.take()
                    PE.wait(b.free, t)
                    for h in range(4):
                        tok = trl(b.ap[0:16, 128 * h:128 * h + 128], S[:, h, :])
                    yield
                    free_S2[s] = [tok]
                    t = copy(PT[0][0:16, :, :], shaped(b.ap[0:16, :], (4, 128)), tok, free_PT[0])
                    b.free = [t]
                    pt = [(PT[0][0:16, :, :], vc[0:16, kv, :], t, 0)]
                    n = 1
                    for br, kT, v, key in ((1, ksT, vs, "vs"), (2, kwT, vw, "vw")):
                        s = turn_n % 2
                        turn_n += 1
                        nk = 128 * (i + 1)
                        S = shaped(Sb[s][:, 0:4 * nk], (4, nk))

                        def pair(h, out, nk, kT=kT):
                            PE.wait(done["ropeks"], done["ropekw"])
                            return mml(out, q[h], kT[:, kv, 0:nk], True, True)
                        t = yield from score_banks(nb, i, pair, scale, S, free_S2[s])
                        t = yield from softmax4(S, nk, t, gt[:, :, br])
                        for j in range(i + 1):
                            t2, tok = yield from turn(nb, S, j, PT[n], t, free_PT[n])
                            pt.append((PT[n], v[:, j, 128 * kv:128 * kv + 128], [t2, t_raw[key]], n))
                            n += 1
                        free_S2[s] = [tok]
                    b = nb.take()
                    PE.wait(b.free)
                    for h in range(4):
                        for j, (P, v, t, _) in enumerate(pt):
                            PE.wait(t, done["vc"])
                            f = mml if j == len(pt) - 1 else mm
                            tok = f(b.ap[:, 128 * h:128 * h + 128], v, P[:, h, :], j == 0, j == len(pt) - 1)
                    for (_, _, _, n) in pt:
                        free_PT[n] = [tok]
                    yield
                    t = copy(yT[:, 4 * kv:4 * kv + 4, 128 * i:128 * i + 128], shaped(b.ap[:, :], (4, 128)), tok)
                    b.free = [t]
                    yield
            done["nsa"] = t

        def invert(rb, X, XT, LT, Y, CT, t_x, t_xt, t_lt, war):
            ty, tp = war, None
            tx, txt = t_x, t_xt
            for lev in range(1, 7):
                tc = tt(PO, CT, LT, rep(C("MT", 128 * lev, 128 * lev + 128), 4), MUL, t_lt, ty)
                b = rb.take()
                PE.wait(b.free, tc, tx)
                for m in range(4):
                    tok = mml(b.ap[:, 128 * m:128 * m + 128], CT[:, m, :], X[:, m, :], True, True)
                yield
                ty = tok
                te = copy(Y, shaped(b.ap[:, :], (4, 128)), tok, tp)
                b.free = [te]
                yield
                if lev < 6:
                    b = rb.take()
                    PE.wait(b.free, te, txt)
                    for m in range(4):
                        tok = mml(b.ap[:, 128 * m:128 * m + 128], XT[:, m, :], Y[:, m, :], True, True)
                b2 = rb.take()
                PE.wait(b2.free, te, txt)
                for m in range(4):
                    tok2 = mml(b2.ap[:, 128 * m:128 * m + 128], Y[:, m, :], XT[:, m, :], True, True)
                tp = tok2
                yield
                if lev < 6:
                    tx = tt(DV, X, X, shaped(b.ap[:, :], (4, 128)), SUB, tok)
                    b.free = [tx]
                txt = tt(DV, XT, XT, shaped(b2.ap[:, :], (4, 128)), SUB, tok2)
                b2.free = [txt]
                yield
            return txt

        raw = [ar.take(6, 259) for _ in range(2)]
        zr = [ar.take(2, SEQ) for _ in range(2)]
        cv = ar.take(6, SEQ)
        tm = ar.take(6, SEQ)
        EG, DT = ar.take(4, 128), ar.take(4, 128)
        UG, Dd, CTm = [shaped(tm[:, 2 * j:2 * j + 2, :].rearrange("p a b -> p (a b)"), (4, 128)) for j in range(3)]
        Kg, qd, Vr, Kd = ar.take(2, 128), ar.take(2, 128), ar.take(4, 128), ar.take(2, 128)
        Lm, LTm, At = [ar.take(4, 128) for _ in range(3)]
        Xm, XTm, Ym = EG, DT, Lm
        Rr, VN, Sd = ar.take(2, 128), ar.take(4, 128), ar.take(2, 128)
        free_raw = {}
        for r in raw:
            t_pad = PO.do(lambda e, r=r: e.memset(r[:, :, 0:3], 0.0))

        def main1b():
            for g in range(4):
                for n, base in enumerate((DQ0, DQ0 + 1024, DQ0 + 2048, DZ0)):
                    def evac(_, ap, tok, n=n, g=g):
                        if g >= 2:
                            yield from until(g - 2, free_raw)
                        w = free_raw[g - 2] if g >= 2 else None
                        dst = zr[g % 2] if n == 3 else raw[g % 2][:, 2 * n:2 * n + 2, 3:259]
                        t = copy(dst, ap, tok, w)
                        if n == 3:
                            t_raw[("dn", g)] = t
                        return t
                    yield from tgemm("w_in", tiles_of(base + 256 * g, 2), 16, hk, t_h, evac)

        def deltanet():
            yield from until("dn", done)
            for g in range(4):
                yield from until(("dn", g), t_raw)
                R = raw[g % 2]
                t_in = t_raw[("dn", g)]
                for s in range(3):
                    for h in range(2):
                        n = 2 * s + h
                        ct = 8 * s + 2 * g + h
                        w = [C("conv", 24 * j + ct, 24 * j + ct + 1) for j in range(4)]
                        t = ts1(DV, cv[:, n, :], R[:, n, 0:256], w[0], MUL, t_in, t_pad, PE.last())
                        for j in range(1, 4):
                            t = stt(DV, cv[:, n, :], R[:, n, j:j + 256], w[j], cv[:, n, :], MUL, ADD)
                    yield
                t = act(tm, cv, ACT.Tanh, t, PO.last(), scale=0.5)
                yield
                t = stt(DV, cv, tm, 1.0, cv, ADD, MUL, t)
                t = act(tm[:, 0:4, :], cv[:, 0:4, :], ACT.Square, t, scale=0.5)
                yield
                for s in range(2):
                    b = db.take()
                    PE.wait(b.free, t)
                    v = shaped(b.ap[:, :], (2, SEQ))
                    tok = mml(v, ones, tm[:, 2 * s:2 * s + 2, :], True, True)
                    t2 = act(tm[:, 2 * s:2 * s + 2, :], v, ACT.Sqrt, tok, scale=(128.0, 1.0)[s], bias=C(("eps128", "eps")[s]))
                    b.free = [t2]
                yield
                t = recip(tm[:, 0:4, :], tm[:, 0:4, :], t2)
                t = stt(DV, cv[:, 0:4, :], cv[:, 0:4, :], 0.5, tm[:, 0:4, :], MUL, MUL)
                t = ts1(DV, cv[:, 4:6, :], cv[:, 4:6, :], 0.5, MUL)
                t_cv = t
                yield

                def qT_(m):
                    return cv[:, m // 2, 128 * (m % 2):128 * (m % 2) + 128]

                def kT_(m):
                    return cv[:, 2 + m // 2, 128 * (m % 2):128 * (m % 2) + 128]

                def vT_(m):
                    return cv[:, 4 + m // 2, 128 * (m % 2):128 * (m % 2) + 128]

                def col(a, m):
                    hh = 2 * g + m // 2
                    return a[:, m % 2, hh:hh + 1]
                for m in range(4):
                    t = ts1(PO, UG[:, m, :], C("utri"), col(gdec, m), MUL, done["dn"], PE.last(), DV.last())
                b = db.take()
                PE.wait(b.free, t)
                GB = shaped(b.ap[:, :], (4, 128))
                t_gb = mml(GB, ones, UG, True, True)
                yield
                t_eg = act(EG, GB, ACT.Exp, t_gb, DV.last())
                t = tt(DV, DT, GB, rep(C("causalT"), 4), ADD, t_gb, t_eg)
                t1 = stt(DV, Dd, GB, -1.0, rep(C("causal"), 4), MUL, ADD)
                b.free = [t1, t_eg]
                for m in range(4):
                    act(DT[:, m, :], DT[:, m, :], ACT.Exp, t1, bias=col(ngc, m))
                    t_d = act(Dd[:, m, :], Dd[:, m, :], ACT.Exp, bias=col(gct, m))
                yield
                b = db.take()
                PE.wait(b.free, t_cv)
                for m in range(4):
                    tok = mml(b.ap[:, 128 * m:128 * m + 128], kT_(m), kT_(m), True, True)
                for m in range(4):
                    t = stt(DV, Lm[:, m, :], b.ap[:, 128 * m:128 * m + 128], col(beta, m), Dd[:, m, :],
                            MUL, MUL, tok, t_d)
                b.free = [t]
                t_l = t
                b = db.take()
                PE.wait(b.free)
                for m in range(4):
                    tok = mml(b.ap[:, 128 * m:128 * m + 128], kT_(m), qT_(m), True, True)
                t_at = tt(DV, At, shaped(b.ap[:, :], (4, 128)), DT, MUL, tok)
                b.free = [t_at]
                yield
                b = db.take()
                PE.wait(b.free, t_l)
                for m in range(4):
                    tok = trl(b.ap[:, 128 * m:128 * m + 128], Lm[:, m, :])
                yield
                t_lt = copy(LTm, shaped(b.ap[:, :], (4, 128)), tok, PO.last())
                b.free = [t_lt]
                for h in range(2):
                    t = tt(PO, Kg[:, h, :], kT_(2 * h + 1), EG[:, 2 * h + 1, :], MUL, t_eg, t_cv)
                    t_kg = tt(PO, qd[:, h, :], qT_(2 * h + 1), EG[:, 2 * h + 1, :], MUL)
                t = tt(PO, Xm, Lm, rep(C("M1"), 4), MUL, t_l, t_at)
                t = tt(PO, XTm, LTm, rep(C("MT", 0, 128), 4), MUL, t_lt)
                t_x1 = tt(DV, Xm, rep(ident, 4), Xm, SUB, t)
                t_xt1 = tt(DV, XTm, rep(ident, 4), XTm, SUB)
                yield
                b = db.take()
                PE.wait(b.free, t_cv)
                for m in range(4):
                    tok = trl(b.ap[:, 128 * m:128 * m + 128], vT_(m))
                t_v = copy(Vr, shaped(b.ap[:, :], (4, 128)), tok)
                b.free = [t_v]
                b = db.take()
                PE.wait(b.free)
                for h in range(2):
                    tok = trl(b.ap[:, 128 * h:128 * h + 128], kT_(2 * h))
                for h in range(2):
                    t = ts1(DV, Kd[:, h, :], b.ap[:, 128 * h:128 * h + 128], col(kdf, 2 * h), MUL, tok)
                b.free = [t]
                yield
                t_inv = yield from invert(db, Xm, XTm, LTm, Ym, CTm, t_x1, t_xt1, t_lt, None)
                for h in range(2):
                    t = ts1(DV, Rr[:, h, :], Vr[:, 2 * h, :], col(beta, 2 * h), MUL, t_v)
                b = db.take()
                PE.wait(b.free, t, t_inv)
                for h in range(2):
                    tok = mml(b.ap[:, 128 * h:128 * h + 128], XTm[:, 2 * h, :], Rr[:, h, :], True, True)
                t_r0 = tok
                yield
                vn = VN.rearrange("p (h c) n -> p h c n", c=2)
                t_vn = copy(vn[:, :, 0, :], shaped(b.ap[:, 0:256], (2, 128)), tok)
                b.free = [t_vn]
                yield
                b = db.take()
                PE.wait(b.free, t_vn)
                for h in range(2):
                    tok = mml(b.ap[:, 128 * h:128 * h + 128], Kd[:, h, :], VN[:, 2 * h, :], True, True)
                yield
                t_s = copy(Sd, shaped(b.ap[:, 0:256], (2, 128)), tok)
                b.free = [t_s]
                yield
                b = db.take()
                PE.wait(b.free, t_s, t_kg)
                for h in range(2):
                    tok = mml(b.ap[:, 128 * h:128 * h + 128], Kg[:, h, :], Sd[:, h, :], True, True)
                yield
                for h in range(2):
                    t = tt(DV, Rr[:, h, :], Vr[:, 2 * h + 1, :], b.ap[:, 128 * h:128 * h + 128], SUB, tok, t_r0)
                    b.free = [t]
                    t = ts1(DV, Rr[:, h, :], Rr[:, h, :], col(beta, 2 * h + 1), MUL)
                b = db.take()
                PE.wait(b.free, t)
                for h in range(2):
                    tok = mml(b.ap[:, 128 * h:128 * h + 128], XTm[:, 2 * h + 1, :], Rr[:, h, :], True, True)
                yield
                t_vn = copy(vn[:, :, 1, :], shaped(b.ap[:, 0:256], (2, 128)), tok)
                b.free = [t_vn]
                yield
                b = db.take()
                PE.wait(b.free, t_vn, t_at)
                for m in range(4):
                    o = b.ap[:, 128 * m:128 * m + 128]
                    if m % 2:
                        mm(o, Sd[:, m // 2, :], qd[:, m // 2, :], True, False)
                    tok = mml(o, VN[:, m, :], At[:, m, :], m % 2 == 0, True)
                yield
                oc = tm[:, 0:2, :]
                sq = tm[:, 2:4, :]
                zz = tm[:, 4:6, :]
                t_o = copy(oc, shaped(b.ap[:, :], (2, SEQ)), tok)
                b.free = [t_o]
                t = tt(PO, sq, oc, oc, MUL, t_o)
                b = db.take()
                PE.wait(b.free, t)
                tok = mml(b.ap[:, :], ones, sq.rearrange("p a b -> p (a b)"), True, True)
                t_z = act(zz, zr[g % 2], ACT.Tanh, scale=0.5)
                yield
                t = act(sq, shaped(b.ap[:, :], (2, SEQ)), ACT.Sqrt, tok, scale=1.0 / 128, bias=C("eps"))
                b.free = [t]
                t = recip(sq, sq, t)
                t = stt(DV, zz, zz, 1.0, zr[g % 2], ADD, MUL, t_z)
                free_raw[g] = t
                t = stt(DV, oc, oc, C("dn_norm"), sq, MUL, MUL)
                t = stt(DV, yT[:, 8 + 2 * g:10 + 2 * g, :], oc, 0.5, zz, MUL, MUL)
                yield
            done["deltanet"] = t

        mark2 = ar.at
        ar.at = mark1
        mixT = ar.take(16, SEQ)
        sg = [ar.take(2, SEQ) for _ in range(2)]
        assert ar.at <= dn0
        ar.at = mark2
        sgf = [[], []]

        def merge(part, w_up, key):
            yield from until("nsa", done)
            for g in range(8):
                s = g % 2

                def evm(_, ap, tok):
                    t = act(sg[s], ap, ACT.Tanh, tok, sgf[s], done["nsa"], PE_nsa[0], scale=0.5)
                    sgf[s] = [t]
                    return t
                yield from tgemm("w_in", tiles_of(MG0 + DM * part + 256 * g, 2), 16, hk, t_h, evm)
                if g == 0:
                    yield from until(key, done)

                def evu(_, ap, tok):
                    m = mixT[:, 2 * g:2 * g + 2, :]
                    if part == 0:
                        t = stt(DV, m, sg[s], 1.0, ap, ADD, MUL, tok, sgf[s])
                        sgf[s] = [t]
                        return t
                    t0 = stt(DV, sg[s], sg[s], 1.0, ap, ADD, MUL, tok, sgf[s])
                    t = tt(DV, m, m, sg[s], ADD)
                    sgf[s] = [t]
                    done[("mix", g)] = t
                    return t0
                yield from tgemm(w_up, tiles_of(256 * g, 2), 8, lambda k: (yT[:, 8 * part + k, :], None), done[key], evu)
        PE_nsa = [None]

        def wout(name, src, kt, k0, pre, scale=None):
            def ev(g, ap, tok):
                x = xT[:, 2 * g:2 * g + 2, :]
                if scale is None:
                    return tt(DV, x, x, ap, ADD, tok)
                return stt(DV, x, ap, scale, x, MUL, ADD, tok)
            yield from tgemm(name, tiles_of(0, 16), kt, src, pre, ev, k0=k0)

        def run(main, sides, ratio=1, sratio=1):
            alive = [s for s in sides]
            m_alive = True
            stuck = 0
            while m_alive or alive:
                before = (PE.n, DV.n, AC.n, PO.n, len(PE.ops), len(done), len(t_raw), len(free_raw))
                if m_alive:
                    for _ in range(ratio):
                        try:
                            next(main)
                        except StopIteration:
                            m_alive = False
                            break
                for s in list(alive):
                    for _ in range(sratio):
                        try:
                            next(s)
                        except StopIteration:
                            alive.remove(s)
                            break
                after = (PE.n, DV.n, AC.n, PO.n, len(PE.ops), len(done), len(t_raw), len(free_raw))
                stuck = stuck + 1 if after == before else 0
                assert stuck < 50, "no generator moves"

        def main1():
            yield from main1a()
            yield from main1b()
            yield from merge(0, "w_up_nsa", "nsa")
            yield from merge(1, "w_up_dn", "deltanet")
            yield from wout("w_o", plain(mixT), 16, 0, done[("mix", 7)], scale=0.5)

        run(main1(), [gates(), nsa(), deltanet()])

        def fence():
            toks = [q.last() for q in (PE, DV, AC, PO)]
            for q in (PE, DV, AC, PO):
                q.wait(toks)

        LOTS = [(0, 16), (16, 32), (32, 44)]

        def ffn(names, gain, gate_evac, temps):
            fence()
            th[0] = norm(xT, gain, None)
            act_tok = {}
            down_tok = [None, None, None]

            def lot(n):
                a, b = LOTS[n]
                for g in range(a // 2, b // 2):
                    at = 16 * (n % 2) + 2 * g - a
                    yield from tgemm(names[0], tiles_of(256 * g, 2), 16, hk, None, lambda _, ap, tok: gate_evac(g, ap, tok))

                    def evu(_, ap, tok):
                        v = alF[:, at:at + 2, :]
                        t0 = stt(DV, v, temps(g), 0.5, ap, MUL, MUL, tok, down_tok[n - 2] if n >= 2 else None)
                        t = two_part(v, ah[:, at:at + 2, :], al[:, at:at + 2, :], t0)
                        act_tok[2 * g] = act_tok[2 * g + 1] = t
                        return t0
                    yield from tgemm(names[1], tiles_of(256 * g, 2), 16, hk, None, evu)

            def down(n):
                a, b = LOTS[n]

                def rhs(k):
                    PE.wait(act_tok[a + k])
                    at = 16 * (n % 2) + k
                    return ah[:, at, :], al[:, at, :]
                yield from wout(names[2], rhs, b - a, a, None)
                down_tok[n] = PE.last()
            yield from lot(0)
            yield from lot(1)
            yield from down(0)
            yield from lot(2)
            yield from down(1)
            yield from down(2)

        ar.at = mark1 + 64 * SEQ
        tb1 = [ar.take(2, SEQ) for _ in range(2)]

        def gate1(g, ap, tok):
            t = act(tb1[g % 2], ap, ACT.Tanh, tok, DV.last(), scale=0.5)
            return stt(DV, tb1[g % 2], tb1[g % 2], 1.0, ap, ADD, MUL, t)
        run(ffn(("w_ffn_gate", "w_ffn_up", "w_ffn_down"), "norm2", gate1, lambda g: tb1[g % 2]), [])

        fence()
        norm(xT, "normf", None, dst=xT)
        t_x = DV.last()
        ar.at = mark1
        lw0 = ar.take(1, 1024)
        lw12 = yT_[:, 8 * SEQ:16 * SEQ]
        lw = [lw0[:, 0, :], lw12[:, 0:1024], lw12[:, 1024:2048]]
        SP.wait(DV.last(), PE.last(), AC.last())
        SP.raw(lambda e: e.dma_start(lw[0], d_lora[:, 0:1024]).then_inc(s_lora, 16))
        SP.raw(lambda e: e.dma_start(lw12, d_lora[:, 1024:3072]).then_inc(s_lora, 16))
        t_lora = (s_lora, 32)
        th[0] = norm(xT, "attn_g", t_x)

        cos2, sin2 = ar.take(SEQ), ar.take(SEQ)
        lh = ar.take(4, SEQ)
        cqT, ckvT, kpe = ar.take(4, SEQ), ar.take(4, SEQ), ar.take(2, SEQ)

        def trig():
            n, a = lh[:, 0, :], lh[:, 1, :]
            t = DV.do(lambda e: e.tensor_copy(a, posi[:, :]), t_pos)
            t = ts1(DV, a, a, C("inv2"), MUL)
            for dst, shift in ((sin2, 0.0), (cos2, float(np.float32(np.pi / 2)))):
                t = ts(DV, n, a, 1.0 / (2 * np.pi), shift / (2 * np.pi), MUL, ADD)
                t = ts1(DV, n, n, 12582912.0, ADD)
                t = ts1(DV, n, n, 12582912.0, SUB)
                t = stt(DV, dst, n, -6.28125, a, MUL, ADD)
                t = stt(DV, dst, n, -0.0019340515136718750, dst, MUL, ADD)
                t = stt(DV, dst, n, -float(2 * np.pi - 6.28125 - 0.0019340515136718750), dst, MUL, ADD)
                if shift:
                    t = ts1(DV, dst, dst, shift, ADD)
                t = ts(DV, dst, dst, 3.1415925, -3.1415925, ALU.min, MAX)
                t = act(dst, dst, ACT.Sin, t)
            done["trig"] = t
        trig()

        RK0 = 3072
        PO.wait(DV.last(), PE.last(), AC.last())

        NS = 2
        ws = []
        ws0 = ar.at
        for _ in range(NS):
            w = {}
            w["raw"] = ar.take(3, 257)
            a0 = ar.at
            w["r"], w["k"] = ar.take(SEQ), ar.take(SEQ)
            w["LD"], w["C"], w["E"], w["KK"], w["A"], w["F"] = [ar.take(SEQ) for _ in range(6)]
            end = ar.at
            ar.at = a0
            w["X"], w["XT"], w["CT"], w["Y"] = [ar.take(4, 128) for _ in range(4)]
            assert ar.at == end
            w["v"], w["g"], w["bon"] = [ar.take(SEQ) for _ in range(3)]
            w["AR"] = ar.take(2, 2, 128)
            w["B"], w["K"] = ar.take(2, SEQ), ar.take(2, SEQ)
            w["P1"], w["P2"] = ar.take(4, 256), ar.take(4, 256)
            w["Vp"] = ar.take(2, 2, 128)
            w["SAp"] = ar.take(2, 128)
            w["G"] = ar.take(128)
            w["Br"], w["Kr"] = ar.take(128), ar.take(128)
            w["S"] = ar.take(128)
            w["em"] = ar.take(4)
            ws.append(w)
            PO.do(lambda e, w=w: e.memset(w["raw"][:, :, 0:1], 0.0))
            PO.do(lambda e, w=w: e.memset(w["Vp"], 0.0))
            padz = PO.do(lambda e, w=w: e.memset(w["SAp"], 0.0))
        lraw = shaped(ws[1]["P2"].rearrange("p a b -> p (a b)")[:, 0:771], (3, 257))
        padz = PO.do(lambda e: e.memset(lraw[:, :, 0:1], 0.0))
        for q in (DV, AC, PE):
            q.wait(padz)
        free_rw, t_rw = {}, {}
        mla_at = ar.at

        def main2():
            lt = [C128(RK0), C128(RK0 + 128), list(range(RK0 + 256, RK0 + 288)) + [-1] * 96]

            def evl(g, ap, tok):
                t = copy(lraw[:, 2 * g:2 * g + ap.shape[1], 1:257], ap, tok)
                done[("lraw", g)] = t
                return t
            yield from tgemm("w_in_2", lt, 16, hk, t_h, evl)
            for p in range(8):
                w = ws[p % NS]
                for g in range(2):
                    def evr(_, ap, tok):
                        if p >= NS:
                            yield from until(p - NS, free_rw)
                        t = copy(w["raw"][:, 2 * g:2 * g + ap.shape[1], 1:257], ap, tok,
                                 free_rw[p - NS] if p >= NS else None)
                        if g:
                            t_rw[p] = t
                        return t
                    tl = [C128(128 * p), C128(1024 + 128 * p)] if g == 0 else [C128(2048 + 128 * p)]
                    yield from tgemm("w_in_2", tl, 16, hk, t_h, evr)
            CQ0 = 3360
            for g in range(4):
                dst = (cqT, ckvT)[g // 2][:, 2 * (g % 2):2 * (g % 2) + 2, :]
                yield from tgemm("w_in_2", tiles_of(CQ0 + 256 * g, 2), 16, hk, t_h, keep(dst, ("c", g)))
            pe_cols = list(range(CQ0 + 1024, CQ0 + 1088))
            yield from tgemm("w_in_2", [pe_cols + pe_cols], 16, hk, t_h, keep(kpe[:, 0:1, :], "kpe"))
            t_end = PE.last()
            qn = hlF[:, 0:8, :]
            qp = hlF[:, 8:12, :]
            done["qn"], done["qp"] = qn, qp
            for key, src, gain in (("cq", cqT, "qn"), ("ckv", ckvT, "kvn")):
                t = [t_raw[("c", g)] for g in range(4)]
                sq = hlF[:, 12:16, :]
                t = tt(DV, sq, src, src, MUL, t, t_end, PE.last())
                b = gbanks.take()
                PE.wait(b.free, t)
                for k in range(4):
                    tok = mml(b.ap[:, 0:SEQ], ones, sq[:, k, :], k == 0, k == 3)
                t = act(rtmp, b.ap[:, 0:SEQ], ACT.Sqrt, tok, DV.last(), scale=1.0 / 512, bias=C("eps"))
                b.free = [t]
                t = recip(rtmp, rtmp, t)
                for k in range(4):
                    t = stt(DV, src[:, k, :], src[:, k, :], C(gain, k, k + 1), rtmp, MUL, MUL)
                done["n" + key] = t
                yield

            def evq(g, ap, tok):
                t = copy(hlF[:, 2 * g:2 * g + 2, :], ap, tok)
                t_raw[("mq", g)] = t
                return t
            uq = [list(range(192 * h, 192 * h + 128)) for h in range(8)]
            uq += [[192 * h + 128 + j for h in (2 * a, 2 * a + 1) for j in range(64)] for a in range(4)]
            yield from tgemm("mla_w_uq_2", uq, 4, plain(cqT), done["ncq"], evq)
            done["mla_q"] = True
            kn = hhF[:, 0:8, :]
            vm = shaped(hhF_[:, 8 * SEQ:16 * SEQ], (2, 1024))
            done["kn"], done["vm"] = kn, vm
            wait0 = [t_end]

            def evk(g, ap, tok):
                t = copy(kn[:, 2 * g:2 * g + 2, :], ap, tok, wait0)
                t_raw[("mk", g)] = t
                return t
            yield from tgemm("mla_w_ukv_2", [list(range(256 * h, 256 * h + 128)) for h in range(8)], 4,
                             plain(ckvT), done["nckv"], evk)
            for a in range(4):
                def evv(i, ap, tok):
                    t = copy(vm[:, i, 256 * a:256 * a + 256], ap, tok, wait0)
                    t_raw[("mv", a)] = t
                    return t
                vcols = [256 * h + 128 + j for h in range(2 * a, 2 * a + 2) for j in range(128)]
                yield from rowgemm("mla_w_ukv_2", vcols, 4,
                                   lambda k, i: (ckvT[:, k, 128 * i:128 * i + 128], None), done["nckv"], evv)
            done["mla_kv"] = True
            yield from until("rwkv0", done)
            yield from until("rwkv1", done)
            yield from wout("w_out_2", plain(yT), 8, 0, [done["rwkv0"], done["rwkv1"]])
            yield from until("mla", done)
            yield from wout("w_out_2", lambda k: (yT[:, 8 + k, :], None), 8, 8, done["mla"])

        def lora():
            for g in range(2):
                yield from until(("lraw", g), done)
            for j in range(3):
                d = lh[:, j, :]
                t = tt(DV, d, lraw[:, j, 0:256], lraw[:, j, 1:257], SUB, done[("lraw", 0)], done[("lraw", 1)],
                       done["trig"])
                t = stt(DV, d, d, C("mu", 24 + j, 25 + j), lraw[:, j, 1:257], MUL, ADD)
                yield
            t1 = ts1(DV, lh[:, 3, :], lh[:, 0, :], C("head", 1, 2), MUL)
            act(lh[:, 0, :], lh[:, 0, :], ACT.Tanh, t1)
            t = act(lh[:, 1:3, :], lh[:, 1:3, :], ACT.Tanh, scale=0.5)
            t = ts(DV, lh[:, 1:3, :], lh[:, 1:3, :], 0.5, 0.5, MUL, ADD, t)
            t = ts1(DV, lh[:, 0, :], lh[:, 0, :], C("head", 0, 1), MUL)
            done["lora"] = t
            yield

        def rwkv(s, rb):
            w = ws[s]
            v, G_, bon, AR, Bt, Kt = w["v"], w["g"], w["bon"], w["AR"], w["B"], w["K"]
            P1, P2, Vp, SAp, G, Br, Kr, S = [w[n] for n in ("P1", "P2", "Vp", "SAp", "G", "Br", "Kr", "S")]
            yield from until("lora", done)
            t_y = None
            for p in range(s, 8, NS):
                yield from until(p, t_rw)
                raw, r, k, LD, Cc, E, KK, A, F = [w[n] for n in ("raw", "r", "k", "LD", "C", "E", "KK", "A", "F")]
                pc = slice(128 * p, 128 * p + 128)
                c1 = slice(p, p + 1)

                def V1(name):
                    return C(name, p, p + 1)
                for j, d in enumerate((r, k, v)):
                    t = tt(DV, d, raw[:, j, 0:256], raw[:, j, 1:257], SUB, t_rw[p], PE.last())
                    t = stt(DV, d, d, C("mu", 8 * j + p, 8 * j + p + 1), raw[:, j, 1:257], MUL, ADD)
                free_rw[p] = t
                t_h3 = t
                b = rb.take()
                PE.wait(b.free, done["lora"], t_lora)
                mml(b.ap[:, 0:256], lw[0][:, pc], lh[:, 0, :], True, True)
                tok = mml(b.ap[:, 256:512], lw[0][:, pc], lh[:, 3, :], True, True)
                b2 = rb.take()
                PE.wait(b2.free)
                mml(b2.ap[:, 0:256], lw[1][:, pc], lh[:, 1, :], True, False)
                tok2 = mml(b2.ap[:, 0:256], lw[2][:, pc], lh[:, 2, :], False, True)
                yield
                t = ts(DV, LD, b.ap[:, 0:256], V1("w0"), 0.5, ADD, MUL, tok)
                t = ts(DV, A, b.ap[:, 256:512], V1("a0"), 0.5, ADD, MUL)
                b.free = [t]
                act(LD, LD, ACT.Tanh, t)
                act(A, A, ACT.Tanh)
                t = copy(G_, b2.ap[:, 0:256], tok2)
                b2.free = [t]
                yield
                ec = 0.5 * float(np.exp(-0.5))
                t = ts(DV, LD, LD, -ec, -ec, MUL, ADD, t)
                t = ts(DV, A, A, 0.5, 0.5, MUL, ADD)
                t = ts1(DV, KK, k, V1("k_k"), MUL)
                t_kk = act(E, KK, ACT.Square, t)
                for c in range(2):
                    cs = slice(128 * c, 128 * c + 128)
                    t_c = DV.do(lambda e, cs=cs: e.tensor_tensor_scan(Cc[:, cs], ones, LD[:, cs], 0.0, MUL, ADD))
                b = rb.take()
                PE.wait(b.free, t_kk)
                tok = mml(b.ap[:, 0:256], bones, E, True, True)
                yield
                t = ts1(DV, E, b.ap[:, 0:256], 1e-24, MAX, tok)
                b.free = [t]
                t = act(E, E, ACT.Sqrt, t)
                t1 = stt(DV, F, A, -1.0, k, ADD, MUL)
                t1 = stt(DV, k, F, V1("k_a"), k, MUL, ADD)
                yield
                t = recip(E, E, t)
                t = tt(DV, KK, KK, E, MUL)
                t = tt(DV, A, A, KK, MUL)
                t = tt(DV, E, r, k, MUL)
                t = ts1(DV, E, E, V1("r_k"), MUL)
                b = rb.take()
                PE.wait(b.free, t)
                tok = mml(b.ap[:, 0:256], bones, E, True, True)
                yield
                t = tt(DV, bon, b.ap[:, 0:256], v, MUL, tok)
                b.free = [t]
                for c in range(2):
                    cs = slice(128 * c, 128 * c + 128)
                    t = ts1(DV, w["em"][:, c:c + 1], Cc[:, 128 * c + 127:128 * c + 128], 0.5, MUL)
                    t = ts1(DV, E[:, cs], Cc[:, cs], w["em"][:, c:c + 1], SUB)
                t = tt(DV, LD, E, LD, SUB)
                t = tt(DV, w["em"][:, 2:3], w["em"][:, 0:1], w["em"][:, 1:2], ADD)
                yield
                t1 = act(F, LD, ACT.Exp, t)
                t2 = act(Cc, E, ACT.Exp)
                t3 = act(LD, E, ACT.Exp, scale=-1.0)
                t4 = act(w["em"][:, 3:4], w["em"][:, 2:3], ACT.Exp)
                yield
                t = tt(DV, AR[:, :, 0, :], shaped(KK, (2, 128)), shaped(F, (2, 128)), MUL, t1)
                t = tt(DV, AR[:, :, 1, :], shaped(r, (2, 128)), shaped(Cc, (2, 128)), MUL, t2)
                for h in range(2):
                    t = stt(DV, Bt[:, h, :], A, C("head", h, h + 1), LD, MUL, MUL, t3)
                    t_ab = stt(DV, Kt[:, h, :], k, C("head", h, h + 1), LD, MUL, MUL)
                yield
                b = rb.take()
                PE.wait(b.free, t_ab, t_h3)
                tok = trl(b.ap[:, 0:128], v[:, 0:128])
                tok = trl(b.ap[:, 128:256], v[:, 128:256])
                for h in range(2):
                    mml(b.ap[:, 256:384], Bt[:, h, 0:128], ident, h == 0, h == 1)
                for h in range(2):
                    tok = mml(b.ap[:, 384:512], Kt[:, h, 0:128], ident, h == 0, h == 1)
                yield
                for h in range(2):
                    t = copy(Vp[:, :, h, 64 * h:64 * h + 64], shaped(b.ap[:, 0:256], (2, 128))[:, :, 64 * h:64 * h + 64], tok, t_y)
                copy(Br, b.ap[:, 256:384])
                t_rows = copy(Kr, b.ap[:, 384:512])
                b.free = [t_rows]
                SUm = C("SU")
                for h in range(2):
                    for P, src in ((P1, Bt), (P2, Kt)):
                        b = rb.take()
                        PE.wait(b.free)
                        for c in range(2):
                            tok = mml(b.ap[:, 256 * c:256 * c + 256], src[:, h, 128 * c:128 * c + 128],
                                      AR[:, c, :, :].rearrange("p a b -> p (a b)"), True, True)
                        yield
                        bv = b.ap[:, :].rearrange("p (c a n) -> p c a n", c=2, a=2)
                        Pv = P.rearrange("p m (a n) -> p m a n", a=2)[:, 2 * h:2 * h + 2, :, :]
                        t = tt(DV, Pv[:, :, 0, :], bv[:, :, 0, :], rep(SUm, 2), MUL, tok)
                        t = tt(DV, Pv[:, :, 1, :], bv[:, :, 1, :], rep(C("utri"), 2), MUL)
                        b.free = [t]
                t_p = t
                X, XT, CT, Y = w["X"], w["XT"], w["CT"], w["Y"]
                b = rb.take()
                PE.wait(b.free)
                for h in range(2):
                    for c in range(2):
                        m = 2 * h + c
                        tok = mml(b.ap[:, 128 * m:128 * m + 128], AR[:, c, 0, :], Bt[:, h, 128 * c:128 * c + 128],
                                  True, True)
                yield
                LT = P1[:, :, 0:128]
                t = tt(DV, X, shaped(b.ap[:, :], (4, 128)), rep(C("M1"), 4), MUL, tok, AC.last())
                b.free = [t]
                t_x1 = tt(DV, X, rep(ident, 4), X, SUB)
                t = tt(PO, XT, LT, rep(C("MT", 0, 128), 4), MUL, t_p)
                t_xt1 = tt(PO, XT, rep(ident, 4), XT, SUB)
                yield
                t_inv = yield from invert(rb, X, XT, LT, Y, CT, t_x1, t_xt1, t_p, None)
                for c in range(2):
                    b = rb.take()
                    PE.wait(b.free, t_rows, t_inv)
                    if c == 1:
                        PE.wait(t_s)
                        mm(b.ap[:, 0:128], AR[:, 1, 0, :], S, True, False)
                    for h in range(2):
                        hc = slice(64 * h, 64 * h + 64)
                        tok = mml(b.ap[:, hc], P2[:, 2 * h + c, 0:128], Vp[:, c, h, hc], c == 0, c == 0 or h == 1)
                    yield
                    t = copy(G, b.ap[:, 0:128], tok)
                    b.free = [t]
                    yield
                    b = rb.take()
                    PE.wait(b.free, t)
                    for h in range(2):
                        hc = slice(64 * h, 64 * h + 64)
                        tok = mml(b.ap[:, hc], XT[:, 2 * h + c, :], G[:, hc], True, True)
                    yield
                    for h in range(2):
                        hc = slice(64 * h, 64 * h + 64)
                        t_sa = copy(SAp[:, h, hc], b.ap[:, hc], tok, PE.last(), scale=-1.0)
                    b.free = [t_sa]
                    yield
                    b = rb.take()
                    PE.wait(b.free, t_sa)
                    o = b.ap[:, 0:128]
                    if c == 1:
                        mm(o, S, AR[:, 1, 1, :], True, False)
                    for h in range(2):
                        mm(o, SAp[:, h, :], P1[:, 2 * h + c, 128:256], c == 0 and h == 0, False)
                        tok = mml(o, Vp[:, c, h, :], P2[:, 2 * h + c, 128:256], False, h == 1)
                    if c == 0:
                        b2 = rb.take()
                        PE.wait(b2.free)
                        n = 0
                        for rows, src in ((Br, SAp), (Kr, Vp[:, 0, :, :])):
                            for h in range(2):
                                tok2 = mml(b2.ap[:, 0:128], rows, src[:, h, :], n == 0, n == 3)
                                n += 1
                    yield
                    yc = w["X"].rearrange("p a b -> p (a b)")[:, 0:256]
                    t_yc = copy(yc[:, 128 * c:128 * c + 128], o, tok)
                    b.free = [t_yc]
                    if c == 0:
                        t_s = stt(DV, S, b2.ap[:, 0:128], w["em"][:, 3:4], bones, MUL, MUL, tok2)
                        b2.free = [t_s]
                    yield
                t_y = tok
                sq = w["X"].rearrange("p a b -> p (a b)")[:, 256:512]
                rs = w["CT"].rearrange("p a b -> p (a b)")[:, 0:256]
                b = rb.take()
                PE.wait(b.free, t_yc)
                tok = mml(b.ap[:, 0:256], bones, yc, True, True)
                yield
                t = stt(DV, yc, b.ap[:, 0:256], -1.0 / 64, yc, MUL, ADD, tok)
                b.free = [t]
                t = act(sq, yc, ACT.Square, t)
                b = rb.take()
                PE.wait(b.free, t)
                tok = mml(b.ap[:, 0:256], bones, sq, True, True)
                yield
                t = act(rs, b.ap[:, 0:256], ACT.Sqrt, tok, PE.last(), scale=1.0 / 64, bias=C("eps64"))
                b.free = [t]
                yield
                t = recip(rs, rs, t)
                t = tt(DV, yc, yc, rs, MUL)
                t = ts(DV, yc, yc, V1("gn_w"), V1("gn_b"), MUL, ADD)
                t = tt(DV, yc, yc, bon, ADD)
                t = tt(DV, yT[:, p, :], yc, G_, MUL)
                yield
            done[f"rwkv{s}"] = t

        rb0, rb1 = Banks(banks[2:5]), Banks(banks[5:8])
        ws_at = [0, 0]
        ws_at[0] = ws0
        assert ws_at[0] + NS * ((mla_at - ws_at[0]) // NS) == mla_at
        mxb2 = ar.take(4)
        smb2 = ar.take(4)

        def mla():
            rb = Banks(banks[2:5])
            yield from until("kpe", t_raw)
            rpt = rtmp
            yield from until("mla_q", done)
            yield from until("rwkv0", done)
            yield from until("rwkv1", done)
            yield from until("mla_kv", done)
            qn, qp, kn, vm = done["qn"], done["qp"], done["kn"], done["vm"]
            wa = Arena(U_[:, :], NU)
            wa.at = ws_at[0]
            tmp = wa.take(2, SEQ)
            Sm = [wa.take(1024), wa.take(1024)]
            PTm = [wa.take(4, 128) for _ in range(4)]
            assert wa.at <= mla_at
            DV.wait(done["rwkv0"], done["rwkv1"], done["trig"], PE.last(), AC.last())
            AC.wait(PE.last(), DV.last())
            for a in range(2):
                rope(qp[:, 2 * a:2 * a + 2, :], cos2, sin2, C("R2"), [t_raw[("mq", 4 + a)]], ("rqp", a), rb, tmp, 2)
                yield
            rope(kpe[:, 0:1, :], cos2, sin2, C("R2"), t_raw["kpe"], "rkpe", rb, tmp[:, 0:1, :], 1)
            ts1(DV, kpe[:, 1, :], kpe[:, 0, :], C("head", 1, 2), MUL)
            done["rkpe"] = ts1(DV, kpe[:, 0, :], kpe[:, 0, :], C("head", 0, 1), MUL)
            yield
            scale = 192 ** -0.5
            free_S = [[], []]
            free_P = [[], [], [], []]
            u = 0
            for a in range(2):
                for i in range(2):
                    nk = 128 * (i + 1)
                    S = shaped(Sm[u % 2][:, 0:4 * nk], (4, nk))

                    def pair(h, out, nk):
                        hh = 4 * a + h
                        PE.wait(t_raw[("mk", 3)], done["rkpe"], done[("rqp", 1)])
                        mm(out, qn[:, hh, 128 * i:128 * i + 128], kn[:, hh, 0:nk], True, False)
                        return mml(out, qp[:, hh // 2, 128 * i:128 * i + 128], kpe[:, hh % 2, 0:nk], False, True)
                    t = yield from score_banks(rb, i, pair, scale, S, free_S[u % 2])
                    t = yield from softmax4b(S, nk, t)
                    pt = []
                    for j in range(i + 1):
                        n = 2 * (u % 2) + j
                        t2, tok = yield from turn(rb, S, j, PTm[n], t, free_P[n])
                        pt.append((PTm[n], j, t2, n))
                    free_S[u % 2] = [tok]
                    b = rb.take()
                    PE.wait(b.free, t_raw[("mv", 3)])
                    for h in range(4):
                        hh = 4 * a + h
                        for x, (P, j, t2, n) in enumerate(pt):
                            PE.wait(t2)
                            tok = mml(b.ap[:, 128 * h:128 * h + 128], vm[:, j, 128 * hh:128 * hh + 128], P[:, h, :],
                                      x == 0, x == len(pt) - 1)
                    for (_, _, _, n) in pt:
                        free_P[n] = [tok]
                    yield
                    t = copy(yT[:, 8 + 4 * a:12 + 4 * a, 128 * i:128 * i + 128], shaped(b.ap[:, :], (4, 128)), tok)
                    b.free = [t]
                    u += 1
                    yield
            done["mla"] = t

        def softmax4b(S, nk, t):
            mx, sm = mxb2, smb2
            t = red(mx, S, MAX, t)
            t = tt(DV, S, S, over(mx, nk), SUB)
            yield
            t = act(S, S, ACT.Exp, t)
            yield
            t = red(sm, S, ADD, t)
            t = recip(sm, sm)
            t = tt(DV, S, S, over(sm, nk), MUL)
            yield
            return t

        t_raw.clear()
        for key in ("kc", "vc"):
            done.pop(key, None)
        run(main2(), [lora(), rwkv(0, rb0), rwkv(1, rb1), mla()])

        ar.at = mark1 + 64 * SEQ
        gp = [ar.take(2, 258) for _ in range(2)]
        cb = [ar.take(2, SEQ) for _ in range(2)]
        tb2 = [ar.take(2, SEQ) for _ in range(2)]
        fence()
        for x in gp:
            tz = PO.do(lambda e, x=x: e.memset(x[:, :, 0:2], 0.0))

        def gate2(g, ap, tok):
            s = g % 2
            t0 = copy(gp[s][:, :, 2:258], ap, tok, DV.last())
            for u in range(2):
                ct = 2 * g + u
                w = [C("conv2", 44 * j + ct, 44 * j + ct + 1) for j in range(3)]
                o = cb[s][:, u, :]
                ts(DV, o, gp[s][:, u, 0:256], w[0], C("conv2b", ct, ct + 1), MUL, ADD, t0, tz)
                stt(DV, o, gp[s][:, u, 1:257], w[1], o, MUL, ADD)
                t = stt(DV, o, gp[s][:, u, 2:258], w[2], o, MUL, ADD)
            t = act(tb2[s], cb[s], ACT.Tanh, t, scale=0.5)
            stt(DV, tb2[s], tb2[s], 1.0, cb[s], ADD, MUL, t)
            return t0
        run(ffn(("ffn_w_gate_2", "ffn_w_up_2", "ffn_w_down_2"), "ffn_g", gate2, lambda g: tb2[g % 2]), [])
        fence()
        t_n = norm(xT, "final_g", None, dst=hhF)
        hflat = hhF_[:, :]
        for j in range(4):
            SP.wait(t_n[4 * j + 3])
            SP.raw(lambda e, j=j: e.dma_start(d_out[:, 1024 * j:1024 * j + 1024], hflat[:, 1024 * j:1024 * j + 1024])
                   .then_inc(s_out, 16))
        SP.wait((s_out, 64))

        at, off = [], 0
        for (_, _, kt, cl) in specs:
            at.append((off, kt * len(cl)))
            off += 128 * kt * len(cl)
        stream["at"] = at
        stream["ap"] = nc.dram_tensor("in_w_dram", [off], F32, kind="ExternalInput").ap()

        block = ctx.enter_context(nc.Block())

        @block.sync
        def _(e):
            for f in SP.ops:
                f(e)

        @block.gpsimd
        def _(e):
            for f in PO.ops:
                f(e)

        @block.scalar
        def _(e):
            for f in AC.ops:
                f(e)

        @block.vector
        def _(e):
            for f in DV.ops:
                f(e)

        @block.tensor
        def _(e):
            for f in PE.ops:
                f(e)
    return specs, off


def constants(inp):
    cols, n = layout()
    out = np.zeros((128, n), np.float32)

    def put(name, a):
        at, w = cols[name]
        assert a.shape == (128, w), (name, a.shape)
        out[:, at:at + w] = a

    def chan(v):
        return np.asarray(v).reshape(-1, 128).T

    i = np.arange(128)
    I, J = i[:, None], i[None, :]
    put("ident", np.eye(128, dtype=np.float32))
    put("ones", np.ones((128, 128), np.float32))
    put("bones", (I // 64 == J // 64).astype(np.float32))
    put("utri", (I <= J).astype(np.float32))
    put("SU", (I < J).astype(np.float32))
    put("head", np.stack([i < 64, i >= 64], 1).astype(np.float32))

    def M(s):
        return ((I // s) % 2 == 1) & (J // s == I // s - 1)
    put("M1", M(1).astype(np.float32))
    put("MT", np.concatenate([M(2 ** l).T for l in range(7)], 1).astype(np.float32))
    put("causal", np.where(J <= I, 0, NEG).astype(np.float32))
    put("causalT", np.where(J >= I, 0, NEG).astype(np.float32))
    R1 = np.zeros((128, 128), np.float32)
    R1[i[:64] + 64, i[:64]] = -1
    R1[i[:64], i[:64] + 64] = 1
    put("R1", R1)
    R2 = np.zeros((128, 128), np.float32)
    for b in (0, 64):
        for j in range(32):
            R2[b + j + 32, b + j] = -1
            R2[b + j, b + j + 32] = 1
    put("R2", R2)
    inv1 = (1.0 / (10000.0 ** (np.arange(0, 128, 2) / 128))).astype(np.float32)
    ang = np.arange(SEQ, dtype=np.float32)[None, :] * inv1[i % 64][:, None]
    put("cos1", np.cos(ang))
    put("sin1", np.sin(ang))
    put("inv2", (10000.0 ** (-(i % 32) / 32)).astype(np.float32)[:, None])
    c = np.arange(16)
    cm = [np.where((c[None, :] * 16 + 31 <= (128 * t + i)[:, None]) & (c[None, :] < 15), 0, NEG) for t in range(2)]
    put("cmpmask", np.concatenate(cm, 1).astype(np.float32))
    put("anyv", np.stack([i >= 31, i >= 0], 1).astype(np.float32))
    put("eps", np.full((128, 1), EPS, np.float32))
    put("eps128", np.full((128, 1), 128 * EPS, np.float32))
    put("eps64", np.full((128, 1), 64e-5, np.float32))
    for name, key in (("norm1", "norm1_w"), ("norm2", "norm2_w"), ("normf", "norm_f_w"), ("attn_g", "attn_norm_g_2"),
                      ("ffn_g", "ffn_norm_g_2"), ("final_g", "final_norm_g_2"), ("w0", "rwkv_w0_2"),
                      ("a0", "rwkv_a0_2"), ("k_k", "rwkv_k_k_2"), ("k_a", "rwkv_k_a_2"), ("r_k", "rwkv_r_k_2"),
                      ("gn_w", "rwkv_gn_w_2"), ("gn_b", "rwkv_gn_b_2"), ("qn", "mla_q_norm_g_2"),
                      ("kvn", "mla_kv_norm_g_2"), ("conv2b", "ffn_conv_b_2"), ("dn_norm", "dn_norm_w"),
                      ("conv", "conv_w"), ("conv2", "ffn_conv_w_2")):
        put(name, chan(inp[key]))
    put("a_log", np.broadcast_to(inp["a_log"].reshape(1, 8), (128, 8)))
    put("dt_bias", np.broadcast_to(inp["dt_bias"].reshape(1, 8), (128, 8)))
    put("pe_k", inp["cmp_pe_k"][0].T)
    put("pe_v", inp["cmp_pe_v"][0].T)
    put("w2k", inp["cmp_w2_k"][0])
    put("w2v", inp["cmp_w2_v"][0])
    mu = np.zeros(27 * 128, np.float32)
    mu[:3360] = inp["rwkv_mu_2"].reshape(-1)
    put("mu", chan(mu))
    return out


def kernel(**inputs):
    import concourse.bacc as _bacc
    from concourse.bass_utils import run_bass_kernel_spmd as _run

    inp = {k: np.asarray(v) for k, v in inputs.items()}
    nc = _bacc.Bacc("TRN2", target_bir_lowering=False, num_devices=1)
    specs, _ = build(_bacc.Bacc("TRN2", target_bir_lowering=False, num_devices=1))
    _, total = build(nc, specs)
    w = np.empty(total, np.float32)
    at = 0
    for name, k0, kt, cl in specs:
        src = inp[name].reshape(-1, inp[name].shape[-1])[128 * k0:128 * (k0 + kt)]
        n = len(cl)
        dst = w[at:at + 128 * kt * n].reshape(128, kt, n)
        real = [c for c in cl if c >= 0]
        if real == list(range(real[0], real[0] + len(real))):
            part = src[:, real[0]:real[0] + len(real)]
        else:
            part = src[:, real]
        dst[:, :, len(real):] = 0
        dst[:, :, :len(real)] = part.reshape(kt, 128, len(real)).transpose(1, 0, 2)
        at += 128 * kt * n
    lora = np.zeros((128, 3, 1024), np.float32)
    lora[0:64, 0] = inp["rwkv_w2_2"][0]
    lora[64:128, 0] = inp["rwkv_a2_2"][0]
    lora[:, 1] = inp["rwkv_g2_2"][0][0:128]
    lora[0:32, 2] = inp["rwkv_g2_2"][0][128:160]
    arrays = {
        "in_cst_dram": constants(inp),
        "in_x_dram": np.ascontiguousarray(inp["x"][0].T.reshape(16, 128, SEQ).transpose(1, 0, 2).reshape(128, -1)),
        "in_pos_dram": np.ascontiguousarray(np.broadcast_to(inp["positions_2"].reshape(1, SEQ), (128, SEQ))),
        "in_lora_dram": lora.reshape(128, 3072),
        "in_w_dram": w,
    }
    r = _run(nc, [arrays], core_ids=[0])
    o = r.results[0]["out_0_dram"].reshape(128, 16, SEQ)
    return np.ascontiguousarray(o.transpose(2, 1, 0).reshape(1, SEQ, DM))
```

```python
from contextlib import ExitStack

import numpy as np
import concourse.bass as bass
from concourse import mybir

F32 = mybir.dt.float32
I32 = mybir.dt.int32
ALU = mybir.AluOpType
ACT = mybir.ActivationFunctionType
AX = mybir.AxisListType
MUL, ADD, SUB, MAX = ALU.mult, ALU.add, ALU.subtract, ALU.max

SEQ = 256
DM = 2048
BLK = 1024
SLACK = 0.0
TO_PE, FROM_PE, SELF = 210.0, 90.0, 130.0
STEP = 1
RING = 6
HIGH = 4
F32R = mybir.dt.float32r
SPLIT = {"w_in", "w_ffn_gate", "w_ffn_up", "w_ffn_down", "w_in_2", "ffn_w_gate_2", "ffn_w_up_2", "ffn_w_down_2",
         "w_up_nsa", "w_up_dn", "w_o", "w_out_2"}
NEG = -1e30
EPS = 1e-6


class Queue:

    ends = {}
    newest = 0.0
    pe_sem = None

    def __init__(self, sem, serial):
        self.sem, self.serial, self.n, self.ops, self.seen = sem, serial, 0, [], {}
        self.at, self.ready = 0.0, 0.0

    def lag(self, sem):
        if sem is self.sem:
            return SELF
        if not self.serial:
            return TO_PE
        return FROM_PE if sem is Queue.pe_sem else 135.0

    def wait(self, *toks):
        for t in toks:
            if t is None:
                continue
            if isinstance(t, list):
                self.wait(*t)
                continue
            sem, v = t
            self.ready = max(self.ready, Queue.ends.get((id(sem), v), 0.0) + self.lag(sem))
            if self.seen.get(id(sem), 0) < v:
                self.seen[id(sem)] = v
                self.ops.append(lambda e, sem=sem, v=v: e.wait_ge(sem, v))

    def take(self, cost):
        self.at = max(self.at, self.ready) + cost
        Queue.newest = max(Queue.newest, self.at)

    def do(self, fn, *toks, cost=0.0, alone=False):
        self.wait(*toks)
        if self.serial and self.n and not alone:
            self.wait((self.sem, self.n))
        self.n += 1
        sem = self.sem
        self.take(cost)
        Queue.ends[(id(sem), self.n)] = self.at
        self.ops.append(lambda e: fn(e).then_inc(sem, 1))
        return (self.sem, self.n)

    def raw(self, fn, cost=0.0):
        self.take(cost)
        self.ops.append(fn)

    def last(self):
        return (self.sem, self.n) if self.n else None


def width(ap):
    n = 1
    for d in ap.shape[1:]:
        n *= d
    return n


class Bank:
    def __init__(self, ap):
        self.ap, self.free = ap, []


class Banks:
    def __init__(self, banks):
        self.b, self.i = banks, 0

    def take(self):
        self.i += 1
        return self.b[(self.i - 1) % len(self.b)]


class Arena:
    def __init__(self, ap, n):
        self.ap, self.n, self.at = ap, n, 0

    def take(self, *dims):
        size = 1
        for d in dims:
            size *= d
        a = self.ap[:, self.at:self.at + size]
        self.at += size
        assert self.at <= self.n, (self.at, self.n)
        return shaped(a, dims)


def shaped(a, dims):
    if len(dims) == 1:
        return a
    if len(dims) == 2:
        return a.rearrange("p (a b) -> p a b", a=dims[0])
    return a.rearrange("p (a b c) -> p a b c", a=dims[0], b=dims[1])


def over(ap, n):
    return ap.unsqueeze(2).to_broadcast([ap.shape[0], ap.shape[1], n])


def rep(ap, n):
    return ap.unsqueeze(1).to_broadcast([ap.shape[0], n, ap.shape[1]])


def layout():
    at, out = 0, {}
    for name, n in [
        ("ones", 128), ("norm1", 16), ("eps", 1), ("ident", 128), ("bones", 128), ("utri", 128), ("SL", 128), ("MC", 7 * 128),
        ("zero", 128), ("causal", 128), ("causalT", 128), ("SU", 128),
        ("head", 2), ("R1", 128), ("R2", 128), ("cos1", 256), ("sin1", 256), ("inv2", 1), ("cmpmask", 32), ("anyv", 2),
        ("eps128", 1), ("eps64", 1), ("zc", 1), ("halfpi", 1),
        ("norm2", 16), ("normf", 16), ("attn_g", 16), ("ffn_g", 16), ("final_g", 16),
        ("conv", 4 * 24), ("a_log", 8), ("dt_bias", 8), ("dn_norm", 1), ("pe_k", 32), ("pe_v", 32),
        ("w2k", 128), ("w2v", 128), ("mu", 27), ("w0", 8), ("a0", 8), ("k_k", 8), ("k_a", 8), ("r_k", 8),
        ("gn_w", 8), ("gn_b", 8), ("qn", 4), ("kvn", 4), ("conv2", 3 * 44), ("conv2b", 44),
    ]:
        out[name] = (at, n)
        at += n
    return out, at


def build(nc, known=None):
    cols, NC = layout()
    specs = []
    Queue.ends.clear()
    ctx = ExitStack()
    with ctx:
        base = (nc.sbuf_base + 63) // 64 * 64
        total = (nc.sbuf_bytes_remaining // 4 // 64) * 64 - 64
        ctx.enter_context(nc.sbuf_tensor("all", [128, total], F32))
        place = [0]

        def sb(name, n, dt=F32, at=None):
            if at is None:
                at = place[0]
                place[0] += (n + 15) // 16 * 16
                assert place[0] <= total
            return nc.alloc_sbuf_tensor_at(name, [128, n], dt, offset=base + 4 * at)

        def sem(name):
            return ctx.enter_context(nc.semaphore(name))

        cst = sb("cst", NC)
        xT_ = sb("xT", 16 * SEQ)
        y_at = place[0]
        yT_ = sb("yT", 16 * SEQ)
        h_at = place[0]
        hh_ = sb("hh", 16 * SEQ, F32R)
        hl_ = sb("hl", 16 * SEQ, F32R)
        hhF_ = sb("hhF", 16 * SEQ, F32, at=h_at)
        hlF_ = sb("hlF", 16 * SEQ, F32, at=h_at + 16 * SEQ)
        ring_at = place[0]
        ring = sb("ring", RING * BLK)
        ringl = sb("ringl", RING * BLK, F32R, at=ring_at)
        high = sb("high", HIGH * BLK, F32R)
        posi = sb("posi", SEQ, I32)
        u_at = place[0]
        NU = (total - u_at) // 64 * 64
        U_ = sb("U", NU)
        ah_ = sb("ah", 32 * SEQ, F32R, at=u_at + 256)
        al_ = sb("al", 32 * SEQ, F32R, at=u_at + 256 + 32 * SEQ)
        alF_ = sb("alF", 32 * SEQ, F32, at=u_at + 256 + 32 * SEQ)
        psum = [ctx.enter_context(nc.psum_tensor(f"ps{i}", [128, 512], F32)) for i in range(8)]
        banks = [Bank(p) for p in psum]

        PE = Queue(sem("s_pe"), False)
        Queue.pe_sem = PE.sem
        DV = Queue(sem("s_dve"), True)
        AC = Queue(sem("s_act"), True)
        PO = Queue(sem("s_pool"), True)
        SP = Queue(sem("s_sp"), False)
        s_cst, s_c0, s_pos, s_out, s_lora = sem("s_cst"), sem("s_c0"), sem("s_pos"), sem("s_out"), sem("s_lora")
        s_x = [sem(f"s_x{i}") for i in range(4)]
        s_ring = [sem(f"s_ring{i}") for i in range(RING)]

        d_cst = nc.dram_tensor("in_cst_dram", [128, NC], F32, kind="ExternalInput").ap()
        d_x = nc.dram_tensor("in_x_dram", [128, 16 * SEQ], F32, kind="ExternalInput").ap()
        d_pos = nc.dram_tensor("in_pos_dram", [128, SEQ], I32, kind="ExternalInput").ap()
        d_lora = nc.dram_tensor("in_lora_dram", [128, 3 * 1024], F32, kind="ExternalInput").ap()
        d_out = nc.dram_tensor("out_0_dram", [128, 16 * SEQ], F32, kind="ExternalOutput").ap()
        stream = {}

        xT = shaped(xT_[:, :], (16, SEQ))
        hh, hl, hhF, hlF = [shaped(a[:, :], (16, SEQ)) for a in (hh_, hl_, hhF_, hlF_)]
        ah, al, alF = [shaped(a[:, :], (32, SEQ)) for a in (ah_, al_, alF_)]
        yT = shaped(yT_[:, :], (16, SEQ))

        def C(name, a=0, b=None):
            at, n = cols[name]
            return cst[:, at + a:at + (n if b is None else b)]

        ident, ones, bones = C("ident"), C("ones"), C("bones")


        def load(m):
            slot = m % RING

            def fn(e):
                if m < len(specs):
                    off, n = stream["at"][m]
                    e.dma_start(ring[:, slot * BLK:slot * BLK + n],
                                stream["ap"][off:off + 128 * n].rearrange("(p n) -> p n", p=128))\
                        .then_inc(s_ring[slot], 16)
            return fn

        known_split = [k for k, sp in enumerate(known or []) if sp[0] in SPLIT]
        order = {m: k for k, m in enumerate(known_split)}
        split_tok, freed = {}, {}

        def arrived(m):
            return (s_ring[m % RING], 16 * (m // RING + 1))

        def split(m):
            k = order[m]
            prev = known_split[k - HIGH] if k >= HIGH else None
            if m >= RING and m - RING not in freed or prev is not None and prev not in freed:
                return False
            _, _, kt, cl = known[m]
            n = kt * len(cl)
            o, g = (m % RING) * BLK, (k % HIGH) * BLK
            half = n // 2
            toks = []
            for x, y in ((0, half), (half, n)):
                hi, w = high[:, g + x:g + y], ring[:, o + x:o + y]
                t = AC.do(lambda e, hi=hi, w=w: e.activation(hi, w, ACT.Copy, scale=1.0), arrived(m), freed.get(prev),
                          cost=cost(AC, hi), alone=True)
                toks.append((x, y, t))
            out = []
            for q, (x, y, t) in zip((PO, DV), toks):
                lo, w, hi = ringl[:, o + x:o + y], ring[:, o + x:o + y], high[:, g + x:g + y]
                out.append(q.do(lambda e, lo=lo, w=w, hi=hi: e.tensor_tensor(lo, w, hi, SUB), t, cost=cost(q, lo),
                                alone=True))
            split_tok[m] = out
            return True

        def look_ahead(m):
            if known is None:
                return
            for j in range(m, min(m + HIGH, len(known))):
                if j in order and j not in split_tok and not split(j):
                    assert j > m
                    break

        class Block:
            def __init__(self, name, k0, kt, cl):
                self.m = m = len(specs)
                assert kt * len(cl) <= BLK
                assert m < RING or (m - RING) in freed
                specs.append((name, k0, kt, list(cl)))
                assert known is None or known[m] == specs[m]
                self.nc = len(cl)
                self.split = name in SPLIT
                look_ahead(m)
                self.base = (m % RING) * BLK
                self.tok = arrived(m)
                if self.split and known:
                    self.tok = split_tok[m]
                    self.hbase = (order[m] % HIGH) * BLK
                else:
                    self.hbase = 0

            def tile(self, k, a, b):
                at = self.base + k * self.nc
                if self.split:
                    g = self.hbase + k * self.nc
                    return high[:, g + a:g + b], ringl[:, at + a:at + b]
                return ring[:, at + a:at + b], None

            def release(self, tok):
                freed[self.m] = tok
                SP.wait(tok)
                SP.raw(load(self.m + RING))

        def product(out, w, x, start, stop, last, w_moves=False):
            if w[1] is None:
                terms = [(w[0], x[0])]
            else:
                terms = [(w[0], x[0]), (w[0], x[1]), (w[1], x[0])]
            for j, (p, q) in enumerate(terms):
                if w_moves:
                    p, q = q, p
                f = mml if last and j == len(terms) - 1 else mm
                tok = f(out, p, q, start and j == 0, stop and j == len(terms) - 1)
            return tok

        NC0 = 128 + 16 + 1
        SP.raw(lambda e: e.dma_start(cst[:, 0:NC0], d_cst[:, 0:NC0]).then_inc(s_c0, 16))
        for i in range(4):
            c = slice(4 * SEQ * i, 4 * SEQ * (i + 1))
            SP.raw(lambda e, i=i, c=c: e.dma_start(xT_[:, c], d_x[:, c]).then_inc(s_x[i], 16))
        for m in range(2):
            SP.raw(load(m))
        SP.raw(lambda e: e.dma_start(cst[:, NC0:NC], d_cst[:, NC0:NC]).then_inc(s_cst, 16))
        SP.raw(lambda e: e.dma_start(posi[:, :], d_pos).then_inc(s_pos, 16))
        for m in range(2, RING):
            SP.raw(load(m))
        t_cst, t_c0, t_x, t_pos, t_lora = (s_cst, 16), (s_c0, 16), [(x, 16) for x in s_x], (s_pos, 16), (s_lora, 16)
        for q in (PE, DV, AC, PO):
            q.wait(t_c0)

        table = [None]

        def mm_cost(r):
            return max(64, width(r)) * (1 if r.dtype == F32R else 4) / 2.37

        def cost(q, out):
            n = width(out)
            return {id(DV): 68 + 1.04 * n, id(AC): 90 + 0.83 * n, id(PO): 150 + 2.1 * n}[id(q)]

        def mm(out, l, r, start, stop):
            PE.raw(lambda e: e.matmul(out, l, r, start=start, stop=stop), cost=mm_cost(r))

        def mml(out, l, r, start, stop):
            return PE.do(lambda e: e.matmul(out, l, r, start=start, stop=stop), cost=mm_cost(r))

        def trl(out, i):
            return PE.do(lambda e: e.transpose(out, i, ident), cost=215)

        def act(out, i, f, *toks, scale=1.0, bias=None, alone=False):
            c = cost(AC, out)
            kind = f if f in (ACT.Sqrt, ACT.Sin, ACT.Ln) else None if f in (ACT.Exp, ACT.Tanh) else table[0]
            if kind != table[0]:
                table[0] = kind
                c += 1283
            if bias is None:
                return AC.do(lambda e: e.activation(out, i, f, scale=scale), *toks, cost=c, alone=alone)
            return AC.do(lambda e: e.activation(out, i, f, scale=scale, bias=bias), *toks, cost=c + 90, alone=alone)

        def copy(out, i, *toks, scale=1.0):
            return act(out, i, ACT.Copy, *toks, scale=scale, alone=True)

        def tt(q, out, a, b, op, *toks, alone=False):
            return q.do(lambda e: e.tensor_tensor(out, a, b, op), *toks, cost=cost(q, out), alone=alone)

        def ts(q, out, a, s1, s2, op0, op1, *toks):
            return q.do(lambda e: e.tensor_scalar(out, a, s1, s2, op0, op1), *toks, cost=cost(q, out))

        def ts1(q, out, a, s1, op0, *toks, alone=False):
            return q.do(lambda e: e.tensor_scalar(out, a, s1, None, op0), *toks, cost=cost(q, out), alone=alone)

        def stt(q, out, a, s, b, op0, op1, *toks, alone=False):
            return q.do(lambda e: e.scalar_tensor_tensor(out=out, in0=a, scalar=s, in1=b, op0=op0, op1=op1), *toks,
                        cost=cost(q, out), alone=alone)

        def recip(out, a, *toks):
            return DV.do(lambda e: e.reciprocal(out, a), *toks, cost=60 + 6.3 * width(out))

        def red(out, a, op, *toks):
            return DV.do(lambda e: e.tensor_reduce(out, a, AX.X, op), *toks, cost=cost(DV, a))

        def until(key, table):
            while key not in table:
                yield "blocked"

        gbanks = Banks(banks[0:2])
        done = {}

        def tgemm(name, tiles, kt, rhs, pre, evac, k0=0):
            tpb = max(1, 8 // kt)
            blk = None
            for g in range(0, len(tiles), 2):
                b = gbanks.take()
                out = shaped(b.ap[:, :], (2, SEQ))
                PE.wait(b.free, pre)
                two = tiles[g:g + 2]
                for u, cl in enumerate(two):
                    i = g + u
                    for ka in range(0, kt, 8):
                        kn = min(8, kt - ka)
                        if i % tpb == 0:
                            blk = Block(name, k0 + ka, kn, [c for t in tiles[i:i + tpb] for c in t])
                            PE.wait(blk.tok)
                        at = (i % tpb) * 128
                        for k in range(kn):
                            tok = product(out[:, u, :], blk.tile(k, at, at + 128), rhs(ka + k),
                                          ka + k == 0, ka + k == kt - 1, k == kn - 1)
                            if k % STEP == STEP - 1 and k < kn - 1:
                                yield
                        if i % tpb == tpb - 1 or i == len(tiles) - 1:
                            blk.release(tok)
                            yield
                b.free = [None]
                r = evac(g // 2, out[:, 0:len(two), :], tok)
                if hasattr(r, "send"):
                    r = yield from r
                b.free = [r]
                yield

        def rowgemm(name, cl, kt, lhs, pre, evac):
            per = BLK // len(cl)
            b = [gbanks.take() for _ in range(2)]
            PE.wait(b[0].free, b[1].free, pre)
            toks = [None, None]
            for a in range(0, kt, per):
                n = min(per, kt - a)
                blk = Block(name, a, n, cl)
                PE.wait(blk.tok)
                for i in range(2):
                    for k in range(n):
                        toks[i] = product(b[i].ap[:, 0:len(cl)], blk.tile(k, 0, len(cl)), lhs(a + k, i),
                                          a + k == 0, a + k == kt - 1, k == n - 1, w_moves=True)
                blk.release(toks[1])
                if a + n < kt:
                    yield
            for i in range(2):
                b[i].free = [evac(i, b[i].ap[:, 0:len(cl)], toks[i])]
            yield

        def two_part(src, hi, lo, *toks):
            t = copy(hi, src, *toks)
            return tt(DV, lo, src, hi, SUB, t, *toks, alone=True)

        class Sums:

            def start(self):
                self.war = PE.last()
                self.pending, self.n = [], 0

            def add(self, k, *toks):
                t = act(hlF[:, k:k + 2, :], xT[:, k:k + 2, :], ACT.Square, self.war, *toks, alone=True)
                self.pending.append((k, t))

            def flush(self):
                if self.n == 0:
                    PE.wait(self.bank.free)
                for k, t in self.pending:
                    PE.wait(t)
                    for j in (k, k + 1):
                        self.tok = mml(self.bank.ap[:, 0:SEQ], ones, hlF[:, j, :], self.n == 0, self.n == 15)
                        self.n += 1
                self.pending = []

        sums = Sums()
        sums.bank = banks[7]

        def norm(gain, dst=None, following=False):
            look_ahead(len(specs))
            sums.flush()
            rt = rtmp[:, 0:SEQ]
            tok = sums.tok
            t = act(rt, sums.bank.ap[:, 0:SEQ], ACT.Sqrt, tok, DV.last(), scale=1.0 / DM, bias=C("eps"))
            sums.bank.free = [t]
            t_r = recip(rt, rt, t)
            if following:
                sums.start()
            toks = []
            for k in range(0, 16, 2):
                o = hlF if dst is None else dst
                for j in (k, k + 1):
                    t = stt(DV, o[:, j, :], xT[:, j, :], C(gain, j, j + 1), rt, MUL, MUL, tok, alone=(k, j) != (0, 0))
                if following:
                    sums.flush()
                    sums.add(k, t)
                if dst is None:
                    t = copy(hh[:, k:k + 2, :], o[:, k:k + 2, :], t)
                    if k % 4:
                        t = tt(PO, hl[:, k:k + 2, :], hlF[:, k:k + 2, :], hh[:, k:k + 2, :], SUB, t, alone=True)
                toks += [t, t]
                if dst is None and k % 4:
                    d = slice(k - 2, k)
                    toks[k - 2] = toks[k - 1] = tt(DV, hl[:, d, :], hlF[:, d, :], hh[:, d, :], SUB, toks[k - 2], alone=True)
            return toks

        ar = Arena(U_[:, :], NU)
        rtmp = ar.take(SEQ)

        th = [None]

        def hk(k):
            PE.wait(th[0][k])
            return hh[:, k, :], hl[:, k, :]

        def hki(k, i):
            PE.wait(th[0][k])
            return hh[:, k, i * 128:(i + 1) * 128], hl[:, k, i * 128:(i + 1) * 128]

        def plain(a):
            return lambda k: (a[:, k, :], None)

        def C128(a):
            return list(range(a, a + 128))

        def tiles_of(a, n):
            return [C128(a + 128 * i) for i in range(n)]

        sums.start()
        for k in range(0, 16, 2):
            sums.add(k, t_x[k // 4])
        DV.wait(t_x)
        th[0] = norm("norm1")
        for q in (PE, DV, AC, PO):
            q.wait(t_cst)
        t_h = None

        Q0, KV0, NG0, DQ0, DZ0, DA0, DB0, MG0 = 0, 1024, 2560, 2584, 5656, 6680, 6688, 6696

        mark1 = ar.at
        qT = ar.take(8, SEQ)
        ksT, kwT = ar.take(2, SEQ), ar.take(2, SEQ)
        vs, vw = ar.take(2, 256), ar.take(2, 256)
        kc = ar.take(32)
        vc = ar.take(2, 128)
        kv_at = ar.at
        kcT_, vcT = ar.take(2, SEQ), ar.take(2, SEQ)
        rp1 = ar.take(2, SEQ)
        at0 = ar.at
        Bb = ar.take(32, 33)
        hid, hid2 = ar.take(33), ar.take(33)
        ar.at = at0
        Sb = [ar.take(1024), U_[:, kv_at:kv_at + 1024]]
        PT = [ar.take(4, 128) for _ in range(5)]
        assert ar.at >= at0 + 33 * 34
        mxb, smb = ar.take(4), ar.take(4)
        dn0 = ar.at
        gl = ar.take(2, 40)
        gate = ar.take(2, 24)
        beta = ar.take(2, 8)
        gdec = ar.take(2, 8)
        gct, ngc, kdf = ar.take(2, 8), ar.take(2, 8), ar.take(2, 8)
        ea, sp1, sp2 = ar.take(8), ar.take(2, 8), ar.take(2, 8)

        side = {}

        def rope(buf, cosn, sinn, R, t, key, rb, tmp, nt):
            b = rb.take()
            PE.wait(b.free, t)
            v = shaped(b.ap[:, 0:nt * SEQ], (nt, SEQ))
            t1 = mml(v, R, buf, True, True)
            t2 = tt(DV, tmp, v, rep(sinn, nt), MUL, t1)
            b.free = [t2]
            t2 = tt(DV, buf, buf, rep(cosn, nt), MUL, t1)
            t2 = tt(DV, buf, buf, tmp, ADD)
            done[key] = t2

        nb = Banks(banks[2:5])
        db = Banks(banks[5:8])
        t_raw = {}

        def keep(dst, key):
            def evac(g, ap, tok):
                t = copy(dst, ap, tok)
                t_raw[key] = t
                return t
            return evac

        def main_gates():
            raw = qT[:, 7, :]
            tl = list(range(NG0, NG0 + 24)) + list(range(DA0, DA0 + 16)) + [-1] * 88

            def evg(_, ap, tok):
                t = done["rawg"] = copy(raw, ap[:, 0, :], tok)
                return t
            yield from tgemm("w_in", [tl], 16, hk, t_h, evg)
            yield
            b = gbanks.take()
            PE.wait(b.free, done["rawg"])
            for i in range(2):
                tok = trl(b.ap[:, 128 * i:128 * i + 128], raw[:, 128 * i:128 * i + 128])
            t = copy(gl, shaped(b.ap[:, 0:256], (2, 128))[:, :, 0:40], tok)
            b.free = [t]
            t_raw["gl"] = t
            yield

        def main_t(key, j, dst):
            yield from tgemm("w_in", tiles_of(KV0 + 256 * j, 2), 16, hk, t_h, keep(dst, key))

        def main_rows(key, j, dst):
            def ev(i, ap, tok):
                t = copy(dst[:, i, :], ap, tok)
                t_raw[key] = t
                return t
            yield from rowgemm("w_in", list(range(KV0 + 256 * j, KV0 + 256 * j + 256)), 16, hki, t_h, ev)

        def gates():
            yield from until("gl", t_raw)
            t = act(gate, gl[:, :, 0:24], ACT.Tanh, t_raw["gl"], scale=0.5)
            t = ts(DV, gate, gate, 0.5, 0.5, MUL, ADD, t)
            for i in range(2):
                g3 = gate[:, i, :].rearrange("p (h b) -> p h b", b=3)[:, :, 0]
                t = ts1(DV, g3, g3, C("anyv", i, i + 1), MUL)
            done["gate"] = t
            yield
            t = act(beta, gl[:, :, 32:40], ACT.Tanh, scale=0.5)
            t = ts(DV, beta, beta, 0.5, 0.5, MUL, ADD, t)
            t = tt(DV, sp1, gl[:, :, 24:32], rep(C("dt_bias"), 2), ADD)
            t = ts1(DV, sp2, sp1, -1.0, MUL)
            t = tt(DV, sp2, sp2, sp1, ALU.min)
            t = act(sp2, sp2, ACT.Exp, t)
            t = act(sp2, sp2, ACT.Ln, bias=C("ones", 0, 1))
            t1 = act(ea, C("a_log"), ACT.Exp)
            yield
            t = ts1(DV, sp1, sp1, 0.0, MAX)
            t = tt(DV, sp1, sp1, sp2, ADD, t1)
            t = stt(DV, gdec, sp1, -1.0, rep(ea, 2), MUL, MUL)
            yield
            b = db.take()
            PE.wait(b.free, t)
            g16 = gdec.rearrange("p a b -> p (a b)")
            mml(b.ap[:, 0:16], C("utri"), g16, True, True)
            t = mml(b.ap[:, 16:32], ones, g16, True, True)
            yield
            gc16 = gct.rearrange("p a b -> p (a b)")
            t = copy(gc16, b.ap[:, 0:16], t)
            t1 = copy(ngc.rearrange("p a b -> p (a b)"), b.ap[:, 0:16], scale=-1.0)
            t = tt(DV, kdf.rearrange("p a b -> p (a b)"), b.ap[:, 16:32], gc16, SUB, t1)
            b.free = [t]
            t = act(kdf, kdf, ACT.Exp, t)
            done["dn"] = t
            yield

        def cmp_hidden(key, w1):
            yield from until("B" + key, done)
            b = gbanks.take()
            PE.wait(b.free, done["B" + key])
            for a in range(0, 32, 8):
                blk = Block(w1, a, 8, range(128))
                PE.wait(blk.tok)
                for j in range(8):
                    f = mml if j == 7 else mm
                    tok = f(b.ap[:, 0:33], blk.tile(j, 0, 128)[0], Bb[:, a + j, :], a + j == 0, a + j == 31)
                blk.release(tok)
                yield
            b.free = [copy(hid, b.ap[:, 0:33], tok)]
            done["hid" + key] = b.free[0]
            yield

        def compress(src, key, pe, w2, is_k):
            yield from until(key, t_raw)
            t0 = t_raw[key]
            if is_k:
                t0 = done["rope" + key]
            t = DV.do(lambda e: e.memset(Bb, 0.0), done.get("hidkc"), cost=1100)
            for h in range(2):
                for half in range(2):
                    o = Bb[:, 16 * half:16 * half + 16, 16 * h:16 * h + 15]
                    i = src[:, h, 16 * half:16 * half + 240].rearrange("p (n j) -> p j n", j=16)
                    t = DV.do(lambda e, o=o, i=i: e.tensor_copy(o, i), t0, cost=200)
            o = Bb[:, :, 32]
            t = DV.do(lambda e: e.tensor_copy(o, C(pe)), cost=100)
            done["B" + key] = t
            yield from until("hid" + key, done)
            t = done["hid" + key]
            x = hid[:, 0:32]
            u = hid2[:, 0:32]
            t = ts1(DV, x, x, hid[:, 32:33], ADD, t)
            t = tt(DV, u, x, x, MUL)
            t = ts(DV, u, u, 0.044715, 1.0, MUL, ADD)
            t = tt(DV, u, u, x, MUL)
            yield
            t = act(u, u, ACT.Tanh, t, scale=0.7978845608028654)
            t = stt(DV, u, u, 1.0, x, ADD, MUL, t)
            yield
            b = nb.take()
            PE.wait(b.free, t)
            if is_k:
                t = mml(b.ap[:, 0:32], C(w2), u, True, True)
                yield
                t = copy(kc, b.ap[:, 0:32], t, scale=0.5)
                b.free = [t]
                done["kc"] = t
            else:
                for h in range(2):
                    t = mml(b.ap[0:16, 128 * h:128 * h + 128], hid2[:, 16 * h:16 * h + 16], C(w2), True, True)
                yield
                t = copy(vc[0:16, :, :], shaped(b.ap[0:16, 0:256], (2, 128)), t, scale=0.5)
                b.free = [t]
                done["vc"] = t_raw["kvc"] = t
            yield

        def softmax4(S, nk, t, mult):
            t = red(mxb, S, MAX, t)
            t = tt(DV, S, S, over(mxb, nk), SUB)
            yield
            t = act(S, S, ACT.Exp, t)
            yield
            t = red(smb, S, ADD, t)
            t = recip(smb, smb)
            if mult is not None:
                t = tt(DV, smb, smb, mult, MUL)
            t = tt(DV, S, S, over(smb, nk), MUL)
            yield
            return t

        def score_banks(rb, i, pair, scale, S, war):
            nk = 128 * (i + 1)
            per = 512 // nk
            for a in range(0, 4, per):
                yield
                b = rb.take()
                PE.wait(b.free)
                v = shaped(b.ap[:, :], (per, nk))
                for h in range(a, a + per):
                    tok = pair(h, v[:, h - a, :], nk)
                yield
                m = C("causal") if i == 0 else cst[:, cols["zero"][0]:cols["zero"][0] + 256]
                t = stt(DV, S[:, a:a + per, :], v, scale, rep(m, per), MUL, ADD, tok, war, alone=True)
                b.free = [t]
            yield
            return t

        def turn(rb, S, j, dst, t, war):
            yield
            b = rb.take()
            PE.wait(b.free, t)
            for h in range(4):
                tok = trl(b.ap[:, 128 * h:128 * h + 128], S[:, h, 128 * j:128 * j + 128])
            yield
            t = copy(dst, shaped(b.ap[:, :], (4, 128)), tok, war)
            b.free = [t]
            yield
            return t, tok

        def nsa():
            for g in range(4):
                yield from until(("q", g), t_raw)
                rope(qT[:, 2 * g:2 * g + 2, :], C("cos1"), C("sin1"), C("R1"), t_raw[("q", g)], ("rq", g), nb, rp1, 2)
                yield
            yield from until("kc", t_raw)
            rope(kcT_, C("cos1"), C("sin1"), C("R1"), t_raw["kc"], "ropekc", nb, rp1, 2)
            yield
            yield from compress(kcT_, "kc", "pe_k", "w2k", True)
            yield from compress(vcT, "vc", "pe_v", "w2v", False)
            yield from until("ks", t_raw)
            rope(ksT, C("cos1"), C("sin1"), C("R1"), t_raw["ks"], "ropeks", nb, rp1, 2)
            yield
            yield from until("kw", t_raw)
            rope(kwT, C("cos1"), C("sin1"), C("R1"), t_raw["kw"], "ropekw", nb, rp1, 2)
            yield from until("gate", done)
            t_q = done[("rq", 3)]
            scale = 128 ** -0.5
            free_S = [done["kc"], done["vc"]]
            free_S2 = [[done["kc"], done["vc"]], [done["kc"], done["vc"]]]
            free_PT = [[done["kc"], done["vc"]] for _ in range(5)]
            turn_n = 0
            for kv in range(2):
                for i in range(2):
                    q = [qT[:, 4 * kv + h, 128 * i:128 * i + 128] for h in range(4)]
                    gt = gate[:, i, :].rearrange("p (h b) -> p h b", b=3)[:, 4 * kv:4 * kv + 4, :]
                    s = turn_n % 2
                    turn_n += 1
                    S = shaped(Sb[s][:, 0:64], (4, 16))
                    yield
                    b = nb.take()
                    PE.wait(b.free, t_q, done["kc"])
                    for h in range(4):
                        tok = mml(b.ap[:, 16 * h:16 * h + 16], q[h], kc[:, 16 * kv:16 * kv + 16], True, True)
                    yield
                    t = stt(DV, S, shaped(b.ap[:, 0:64], (4, 16)), scale, rep(C("cmpmask", 16 * i, 16 * i + 16), 4),
                            MUL, ADD, tok, free_S2[s])
                    b.free = [t]
                    t = yield from softmax4(S, 16, t, gt[:, :, 0])
                    yield
                    b = nb.take()
                    PE.wait(b.free, t)
                    for h in range(4):
                        tok = trl(b.ap[0:16, 128 * h:128 * h + 128], S[:, h, :])
                    yield
                    free_S2[s] = [tok]
                    t = copy(PT[0][0:16, :, :], shaped(b.ap[0:16, :], (4, 128)), tok, free_PT[0])
                    b.free = [t]
                    pt = [(PT[0][0:16, :, :], vc[0:16, kv, :], (t, "kvc"), 0)]
                    n = 1
                    for br, kT, v, key in ((1, ksT, vs, "vs"), (2, kwT, vw, "vw")):
                        s = turn_n % 2
                        turn_n += 1
                        nk = 128 * (i + 1)
                        S = shaped(Sb[s][:, 0:4 * nk], (4, nk))

                        def pair(h, out, nk, kT=kT):
                            PE.wait(done["ropeks"], done["ropekw"])
                            return mml(out, q[h], kT[:, kv, 0:nk], True, True)
                        t = yield from score_banks(nb, i, pair, scale, S, free_S2[s])
                        t = yield from softmax4(S, nk, t, gt[:, :, br])
                        for j in range(i + 1):
                            t2, tok = yield from turn(nb, S, j, PT[n], t, free_PT[n])
                            pt.append((PT[n], v[:, j, 128 * kv:128 * kv + 128], (t2, key), n))
                            n += 1
                        free_S2[s] = [tok]
                    yield from until("vw", t_raw)
                    yield
                    b = nb.take()
                    PE.wait(b.free)
                    for h in range(4):
                        for j, (P, v, t, _) in enumerate(pt):
                            PE.wait(t[0], t_raw[t[1]])
                            f = mml if j == len(pt) - 1 else mm
                            tok = f(b.ap[:, 128 * h:128 * h + 128], v, P[:, h, :], j == 0, j == len(pt) - 1)
                    for (_, _, _, n) in pt:
                        free_PT[n] = [tok]
                    yield
                    t = copy(yT[:, 4 * kv:4 * kv + 4, 128 * i:128 * i + 128], shaped(b.ap[:, :], (4, 128)), tok)
                    b.free = [t]
                    yield
            done["nsa"] = t

        def invert(rb, X, XT, L, LT, Y, t_l, t_lt, t_free):
            def cols(M, s, t):
                return M.rearrange("p m (b t s) -> p m t b s", t=2, s=s)[:, :, t, :, :]

            def icols(t):
                v = ident.rearrange("p (b t s) -> p t b s", t=2, s=1)[:, t, :, :]
                return v.unsqueeze(1).to_broadcast([128, 4, 64, 1])

            def half(ap, s, t, m=None):
                v = ap.rearrange("p m (t b s) -> p m t b s", t=2, s=s)[:, :, t, :, :]
                return v if m is None else v[:, m, :, :]

            def mask(lev, t):
                return rep(C("MC", 128 * lev + 64 * t, 128 * lev + 64 * t + 64), 4)
            Yt = Y.rearrange("p m (t n) -> p m t n", t=2)
            tt(PO, Yt[:, :, 1, :], cols(LT, 1, 1).rearrange("p m b s -> p m (b s)"), mask(0, 1), MUL, t_lt, t_free)
            for M, t in ((X, 1), (XT, 0)):
                PO.do(lambda e, M=M, t=t: e.tensor_copy(out=cols(M, 1, t), in_=icols(t)), cost=700)
            txt = tt(PO, cols(XT, 1, 1), icols(1), half(Y, 1, 1), SUB)
            tt(DV, Yt[:, :, 0, :], cols(L, 1, 0).rearrange("p m b s -> p m (b s)"), mask(0, 0), MUL, t_l, t_free)
            tx = tt(DV, cols(X, 1, 0), icols(0), half(Y, 1, 0), SUB)
            yield
            for lev in range(1, 7):
                s = 2 ** lev
                t0 = 0 if lev < 6 else 1
                b = rb.take()
                PE.wait(b.free, t_l, t_lt, tx, txt)
                B = shaped(b.ap[:, :], (4, 128))
                for t, lhs, M in ((0, LT, X), (1, L, XT))[t0:]:
                    for m in range(4):
                        tok = mml(half(B, s, t, m), lhs[:, m, :], cols(M, s, t)[:, m, :, :], True, True)
                yield
                Bt = B.rearrange("p m (t n) -> p m t n", t=2)
                if t0:
                    te = tt(DV, Yt[:, :, 1, :], Bt[:, :, 1, :], mask(lev, 1), MUL, tok, alone=True)
                else:
                    te = tt(DV, Y, B, rep(C("MC", 128 * lev, 128 * lev + 128), 4), MUL, tok, alone=True)
                b.free = [te]
                yield
                b = rb.take()
                PE.wait(b.free, te)
                B = shaped(b.ap[:, :], (4, 128))
                for t, lhs in ((0, XT), (1, X))[t0:]:
                    for m in range(4):
                        tok = mml(B[:, m, 64 * t:64 * t + 64], lhs[:, m, :], Y[:, m, 64 * t:64 * t + 64], True, True)
                yield
                if not t0:
                    tx = tt(DV, cols(X, s, 0), cols(X, s, 0), half(B, s, 0), SUB, tok, alone=True)
                txt = tt(DV, cols(XT, s, 1), cols(XT, s, 1), half(B, s, 1), SUB, tok, alone=True)
                b.free = [txt]
                yield
            return txt

        raw = [ar.take(6, 259) for _ in range(2)]
        zr = [ar.take(2, SEQ) for _ in range(2)]
        cv = ar.take(6, SEQ)
        tm = ar.take(6, SEQ)
        EG, DT = ar.take(4, 128), ar.take(4, 128)
        UG, Dd, Ym = [shaped(tm[:, 2 * j:2 * j + 2, :].rearrange("p a b -> p (a b)"), (4, 128)) for j in range(3)]
        Kg, qd, Vr, Kd = ar.take(2, 128), ar.take(2, 128), ar.take(4, 128), ar.take(2, 128)
        Lm, LTm, At = [ar.take(4, 128) for _ in range(3)]
        Xm, XTm = EG, DT
        Rr, VN, Sd = ar.take(2, 128), ar.take(4, 128), ar.take(2, 128)
        free_raw, free_z = {}, {}
        for r in raw:
            t_pad = PO.do(lambda e, r=r: e.memset(r[:, :, 0:3], 0.0))

        def main_dn(g):
            for n, base in enumerate((DQ0, DQ0 + 1024, DQ0 + 2048, DZ0)):
                def evac(_, ap, tok, n=n, g=g):
                    table, w = (free_z, None) if n == 3 else (free_raw, None)
                    if g >= 2:
                        yield from until(g - 2, table)
                        w = table[g - 2]
                    dst = zr[g % 2] if n == 3 else raw[g % 2][:, 2 * n:2 * n + 2, 3:259]
                    t = copy(dst, ap, tok, w)
                    if n == 2:
                        t_raw[("dn", g)] = t
                    if n == 3:
                        t_raw[("z", g)] = t
                    return t
                yield from tgemm("w_in", tiles_of(base + 256 * g, 2), 16, hk, t_h, evac)

        def deltanet():
            yield from until("dn", done)
            t_pe = PE.last()
            for g in range(4):
                yield from until(("dn", g), t_raw)
                R = raw[g % 2]
                t_in = t_raw[("dn", g)]
                for s in range(3):
                    for h in range(2):
                        n = 2 * s + h
                        ct = 8 * s + 2 * g + h
                        w = [C("conv", 24 * j + ct, 24 * j + ct + 1) for j in range(4)]
                        t = ts1(DV, cv[:, n, :], R[:, n, 0:256], w[0], MUL, t_in, t_pad, t_pe)
                        for j in range(1, 4):
                            t = stt(DV, cv[:, n, :], R[:, n, j:j + 256], w[j], cv[:, n, :], MUL, ADD)
                    yield
                free_raw[g] = t
                t = act(tm, cv, ACT.Tanh, t, t_pe, scale=0.5)
                yield
                t = stt(DV, cv, tm, 1.0, cv, ADD, MUL, t)
                t = act(tm[:, 0:4, :], cv[:, 0:4, :], ACT.Square, t, scale=0.5)
                yield
                for s in range(2):
                    yield
                    b = db.take()
                    PE.wait(b.free, t)
                    v = shaped(b.ap[:, :], (2, SEQ))
                    tok = mml(v, ones, tm[:, 2 * s:2 * s + 2, :], True, True)
                    t2 = act(tm[:, 2 * s:2 * s + 2, :], v, ACT.Sqrt, tok, scale=(128.0, 1.0)[s], bias=C(("eps128", "eps")[s]))
                    b.free = [t2]
                yield
                t = recip(tm[:, 0:4, :], tm[:, 0:4, :], t2)
                t = stt(DV, cv[:, 0:4, :], cv[:, 0:4, :], 0.5, tm[:, 0:4, :], MUL, MUL)
                t = ts1(DV, cv[:, 4:6, :], cv[:, 4:6, :], 0.5, MUL)
                t_cv = t
                yield

                def qT_(m):
                    return cv[:, m // 2, 128 * (m % 2):128 * (m % 2) + 128]

                def kT_(m):
                    return cv[:, 2 + m // 2, 128 * (m % 2):128 * (m % 2) + 128]

                def vT_(m):
                    return cv[:, 4 + m // 2, 128 * (m % 2):128 * (m % 2) + 128]

                def col(a, m):
                    hh = 2 * g + m // 2
                    return a[:, m % 2, hh:hh + 1]
                for m in range(4):
                    t = ts1(DV, UG[:, m, :], C("utri"), col(gdec, m), MUL, done["dn"], alone=m > 0)
                yield
                b = db.take()
                PE.wait(b.free, t)
                GB = shaped(b.ap[:, :], (4, 128))
                t_gb = mml(GB, ones, UG, True, True)
                yield
                t_eg = act(EG, GB, ACT.Exp, t_gb)
                t = tt(DV, DT, GB, rep(C("causalT"), 4), ADD, t_gb, t_eg)
                t1 = stt(DV, Dd, GB, -1.0, rep(C("causal"), 4), MUL, ADD)
                b.free = [t1, t_eg]
                for m in range(4):
                    act(DT[:, m, :], DT[:, m, :], ACT.Exp, t1, bias=col(ngc, m), alone=True)
                    t_d = act(Dd[:, m, :], Dd[:, m, :], ACT.Exp, bias=col(gct, m), alone=True)
                yield
                b = db.take()
                PE.wait(b.free, t_cv)
                for m in range(4):
                    tok = mml(b.ap[:, 128 * m:128 * m + 128], kT_(m), kT_(m), True, True)
                for m in range(4):
                    t = stt(DV, Lm[:, m, :], b.ap[:, 128 * m:128 * m + 128], col(beta, m), Dd[:, m, :],
                            MUL, MUL, tok, t_d, alone=m > 0)
                b.free = [t]
                t_l = t
                yield
                b = db.take()
                PE.wait(b.free)
                for m in range(4):
                    tok = mml(b.ap[:, 128 * m:128 * m + 128], kT_(m), qT_(m), True, True)
                t_at = tt(DV, At, shaped(b.ap[:, :], (4, 128)), DT, MUL, tok)
                b.free = [t_at]
                yield
                b = db.take()
                PE.wait(b.free, t_l)
                for m in range(4):
                    tok = trl(b.ap[:, 128 * m:128 * m + 128], Lm[:, m, :])
                yield
                t_lt = copy(LTm, shaped(b.ap[:, :], (4, 128)), tok)
                b.free = [t_lt]
                for h in range(2):
                    t = tt(PO, Kg[:, h, :], kT_(2 * h + 1), EG[:, 2 * h + 1, :], MUL, t_eg, t_cv, alone=True)
                    t_kg = tt(PO, qd[:, h, :], qT_(2 * h + 1), EG[:, 2 * h + 1, :], MUL, alone=True)
                yield
                yield
                b = db.take()
                PE.wait(b.free, t_cv)
                for m in range(4):
                    tok = trl(b.ap[:, 128 * m:128 * m + 128], vT_(m))
                t_v = copy(Vr, shaped(b.ap[:, :], (4, 128)), tok)
                b.free = [t_v]
                yield
                b = db.take()
                PE.wait(b.free)
                for h in range(2):
                    tok = trl(b.ap[:, 128 * h:128 * h + 128], kT_(2 * h))
                for h in range(2):
                    t = ts1(DV, Kd[:, h, :], b.ap[:, 128 * h:128 * h + 128], col(kdf, 2 * h), MUL, tok, alone=True)
                b.free = [t]
                yield
                t_inv = yield from invert(db, Xm, XTm, Lm, LTm, Ym, t_l, t_lt, [t_at, t_kg])
                for h in range(2):
                    t = ts1(DV, Rr[:, h, :], Vr[:, 2 * h, :], col(beta, 2 * h), MUL, t_v)
                yield
                b = db.take()
                PE.wait(b.free, t, t_inv)
                for h in range(2):
                    tok = mml(b.ap[:, 128 * h:128 * h + 128], XTm[:, 2 * h, :], Rr[:, h, :], True, True)
                t_r0 = tok
                yield
                vn = VN.rearrange("p (h c) n -> p h c n", c=2)
                t_vn = copy(vn[:, :, 0, :], shaped(b.ap[:, 0:256], (2, 128)), tok)
                b.free = [t_vn]
                yield
                b = db.take()
                PE.wait(b.free, t_vn)
                for h in range(2):
                    tok = mml(b.ap[:, 128 * h:128 * h + 128], Kd[:, h, :], VN[:, 2 * h, :], True, True)
                yield
                t_s = copy(Sd, shaped(b.ap[:, 0:256], (2, 128)), tok)
                b.free = [t_s]
                yield
                b = db.take()
                PE.wait(b.free, t_s, t_kg)
                for h in range(2):
                    tok = mml(b.ap[:, 128 * h:128 * h + 128], Kg[:, h, :], Sd[:, h, :], True, True)
                yield
                for h in range(2):
                    t = tt(DV, Rr[:, h, :], Vr[:, 2 * h + 1, :], b.ap[:, 128 * h:128 * h + 128], SUB, tok, t_r0, alone=True)
                    b.free = [t]
                    t = ts1(DV, Rr[:, h, :], Rr[:, h, :], col(beta, 2 * h + 1), MUL)
                yield
                b = db.take()
                PE.wait(b.free, t)
                for h in range(2):
                    tok = mml(b.ap[:, 128 * h:128 * h + 128], XTm[:, 2 * h + 1, :], Rr[:, h, :], True, True)
                yield
                t_vn = copy(vn[:, :, 1, :], shaped(b.ap[:, 0:256], (2, 128)), tok)
                b.free = [t_vn]
                yield
                b = db.take()
                PE.wait(b.free, t_vn, t_at)
                for m in range(4):
                    o = b.ap[:, 128 * m:128 * m + 128]
                    if m % 2:
                        mm(o, Sd[:, m // 2, :], qd[:, m // 2, :], True, False)
                    tok = mml(o, VN[:, m, :], At[:, m, :], m % 2 == 0, True)
                yield
                oc = tm[:, 0:2, :]
                sq = tm[:, 2:4, :]
                zz = tm[:, 4:6, :]
                t_o = copy(oc, shaped(b.ap[:, :], (2, SEQ)), tok)
                b.free = [t_o]
                t = tt(PO, sq, oc, oc, MUL, t_o)
                yield
                b = db.take()
                PE.wait(b.free, t)
                tok = t_pe = mml(b.ap[:, :], ones, sq.rearrange("p a b -> p (a b)"), True, True)
                yield from until(("z", g), t_raw)
                t_z = act(zz, zr[g % 2], ACT.Tanh, t_raw[("z", g)], scale=0.5)
                yield
                t = act(sq, shaped(b.ap[:, :], (2, SEQ)), ACT.Sqrt, tok, scale=1.0 / 128, bias=C("eps"))
                b.free = [t]
                t = recip(sq, sq, t)
                t = stt(DV, zz, zz, 1.0, zr[g % 2], ADD, MUL, t_z)
                free_z[g] = t
                t = stt(DV, oc, oc, C("dn_norm"), sq, MUL, MUL)
                t = stt(DV, yT[:, 8 + 2 * g:10 + 2 * g, :], oc, 0.5, zz, MUL, MUL)
                yield
            done["deltanet"] = t

        mark2 = ar.at
        ar.at = mark1
        mixT = ar.take(16, SEQ)
        mixh_at = u_at + ar.at
        ar.take(16 * SEQ)
        sg = [ar.take(2, SEQ) for _ in range(2)]
        assert ar.at <= dn0
        ar.at = mark2
        mixl = shaped(sb("mixl", 16 * SEQ, F32R, at=u_at + mark1)[:, :], (16, SEQ))
        mixh = shaped(sb("mixh", 16 * SEQ, F32R, at=mixh_at)[:, :], (16, SEQ))
        yl = shaped(sb("yl", 16 * SEQ, F32R, at=y_at)[:, :], (16, SEQ))
        yh = [shaped(sb(f"yh{i}", 8 * SEQ, F32R, at=a)[:, :], (8, SEQ)) for i, a in enumerate((mixh_at, u_at + dn0))]
        sgf = [[], []]

        def parts_of_y(i, h, t):
            toks = []
            for k in range(0, 8, 2):
                a = slice(8 * i + k, 8 * i + k + 2)
                toks += [two_part(yT[:, a, :], h[:, k:k + 2, :], yl[:, a, :], t)] * 2

            def rhs(k):
                PE.wait(toks[k])
                return h[:, k, :], yl[:, 8 * i + k, :]
            return rhs

        def merge(part, w_up, key):
            rhs = None
            for g in range(8):
                s = g % 2

                def evm(_, ap, tok):
                    t = act(sg[s], ap, ACT.Tanh, tok, sgf[s], scale=0.5)
                    sgf[s] = [t]
                    return t
                if part == 0 and g == 0:
                    yield from until("nsa", done)
                    sgf[0], sgf[1] = [done["nsa"]], [done["nsa"]]
                yield from tgemm("w_in", tiles_of(MG0 + DM * part + 256 * g, 2), 16, hk, t_h, evm)
                if g == 0:
                    yield from until(key, done)
                    rhs = parts_of_y(part, yh[part], done[key])

                def evu(_, ap, tok):
                    m = mixT[:, 2 * g:2 * g + 2, :]
                    if part == 0:
                        t = stt(DV, m, sg[s], 1.0, ap, ADD, MUL, tok, sgf[s])
                        sgf[s] = [t]
                        done["up0"] = tok
                        return t
                    t0 = stt(DV, sg[s], sg[s], 1.0, ap, ADD, MUL, tok, sgf[s])
                    t = tt(DV, m, m, sg[s], ADD)
                    sgf[s] = [t]
                    done[("mix", g)] = two_part(m, mixh[:, 2 * g:2 * g + 2, :], mixl[:, 2 * g:2 * g + 2, :], t, done["up0"])
                    return t0
                yield from tgemm(w_up, tiles_of(256 * g, 2), 8, rhs, None, evu)

        def mixed(k):
            PE.wait(done[("mix", k // 2)])
            return mixh[:, k, :], mixl[:, k, :]

        def wout(name, src, kt, k0, pre, scale=None, sums=None):
            def ev(g, ap, tok):
                x = xT[:, 2 * g:2 * g + 2, :]
                if scale is None:
                    t = tt(DV, x, x, ap, ADD, tok, alone=True)
                else:
                    t = stt(DV, x, ap, scale, x, MUL, ADD, tok, alone=True)
                if sums:
                    sums.flush()
                    sums.add(2 * g, t)
                return t
            if sums:
                sums.start()
            yield from tgemm(name, tiles_of(0, 16), kt, src, pre, ev, k0=k0)

        def run(main, sides):
            gens = [main] + list(sides)
            ready = {id(g): 0.0 for g in gens}
            idle = set()
            while gens:
                awake = [g for g in gens if id(g) not in idle]
                assert awake, "no stream moves"
                others = sorted((g for g in awake if g is not main), key=lambda g: ready[id(g)])
                if others and (main not in awake or ready[id(others[0])] <= PE.at + SLACK):
                    g = others[0]
                else:
                    g = main
                Queue.newest = 0.0
                before = sum(len(q.ops) for q in (PE, DV, AC, PO)) + len(done)
                try:
                    blocked = next(g) == "blocked"
                except StopIteration:
                    gens.remove(g)
                    idle.clear()
                    continue
                if blocked:
                    if before != sum(len(q.ops) for q in (PE, DV, AC, PO)) + len(done):
                        idle.clear()
                    idle.add(id(g))
                else:
                    idle.clear()
                    ready[id(g)] = max(ready[id(g)], Queue.newest)

        def main1():
            yield from main_gates()
            yield from main_dn(0)
            for g in range(4):
                yield from tgemm("w_in", tiles_of(Q0 + 256 * g, 2), 16, hk, t_h, keep(qT[:, 2 * g:2 * g + 2, :], ("q", g)))
            yield from main_t("kc", 0, kcT_)
            yield from cmp_hidden("kc", "cmp_w1_k")
            yield from main_t("vc", 1, vcT)
            yield from main_t("ks", 2, ksT)
            yield from main_t("kw", 4, kwT)
            yield from cmp_hidden("vc", "cmp_w1_v")
            yield from main_dn(1)
            yield from main_rows("vs", 3, vs)
            yield from main_rows("vw", 5, vw)
            yield from main_dn(2)
            yield from main_dn(3)
            yield from merge(0, "w_up_nsa", "nsa")
            yield from merge(1, "w_up_dn", "deltanet")
            yield from wout("w_o", mixed, 16, 0, None, scale=0.5, sums=sums)

        run(main1(), [deltanet(), gates(), nsa()])

        def fence():
            toks = [q.last() for q in (PE, DV, AC, PO)]
            for q in (PE, DV, AC, PO):
                q.wait(toks)

        LOTS = [(0, 16), (16, 32), (32, 44)]

        def ffn(names, gain, gate_evac, temps):
            th[0] = norm(gain)
            act_tok = {}
            down_tok = [None, None, None]

            def lot(n):
                a, b = LOTS[n]
                for g in range(a // 2, b // 2):
                    at = 16 * (n % 2) + 2 * g - a
                    yield from tgemm(names[0], tiles_of(256 * g, 2), 16, hk, None, lambda _, ap, tok: gate_evac(g, ap, tok))

                    def evu(_, ap, tok):
                        v = alF[:, at:at + 2, :]
                        t0 = stt(DV, v, temps(g), 0.5, ap, MUL, MUL, tok, down_tok[n - 2] if n >= 2 else None)
                        t = two_part(v, ah[:, at:at + 2, :], al[:, at:at + 2, :], t0)
                        act_tok[2 * g] = act_tok[2 * g + 1] = t
                        return t0
                    yield from tgemm(names[1], tiles_of(256 * g, 2), 16, hk, None, evu)

            def down(n):
                a, b = LOTS[n]

                def rhs(k):
                    PE.wait(act_tok[a + k])
                    at = 16 * (n % 2) + k
                    return ah[:, at, :], al[:, at, :]
                yield from wout(names[2], rhs, b - a, a, None, sums=sums if n == 2 else None)
                down_tok[n] = PE.last()
            yield from lot(0)
            yield from lot(1)
            yield from down(0)
            yield from lot(2)
            yield from down(1)
            yield from down(2)

        ar.at = mark1 + 64 * SEQ
        tb1 = [ar.take(2, SEQ) for _ in range(2)]

        def gate1(g, ap, tok):
            t = act(tb1[g % 2], ap, ACT.Tanh, tok, DV.last(), scale=0.5)
            return stt(DV, tb1[g % 2], tb1[g % 2], 1.0, ap, ADD, MUL, t)
        run(ffn(("w_ffn_gate", "w_ffn_up", "w_ffn_down"), "norm2", gate1, lambda g: tb1[g % 2]), [])

        old = [q.last() for q in (PE, DV, AC, PO)]
        for q in (DV, AC, PO):
            q.wait(old)
        norm("normf", dst=xT, following=True)
        ar.at = mark1
        lw0 = ar.take(1, 1024)
        lw12 = yT_[:, 8 * SEQ:16 * SEQ]
        lw = [lw0[:, 0, :], lw12[:, 0:1024], lw12[:, 1024:2048]]
        SP.wait(old)
        SP.raw(lambda e: e.dma_start(lw[0], d_lora[:, 0:1024]).then_inc(s_lora, 16))
        SP.raw(lambda e: e.dma_start(lw12, d_lora[:, 1024:3072]).then_inc(s_lora, 16))
        t_lora = (s_lora, 32)

        cos2, sin2 = ar.take(SEQ), ar.take(SEQ)
        lh = ar.take(4, SEQ)
        cqT, ckvT, kpe = ar.take(4, SEQ), ar.take(4, SEQ), ar.take(2, SEQ)

        def trig():
            n, a = lh[:, 0, :], lh[:, 1, :]
            t = DV.do(lambda e: e.tensor_copy(a, posi[:, :]), t_pos)
            t = ts1(DV, a, a, C("inv2"), MUL)
            for dst, shift in ((sin2, 0.0), (cos2, float(np.float32(np.pi / 2)))):
                t = ts(DV, n, a, 1.0 / (2 * np.pi), shift / (2 * np.pi), MUL, ADD)
                t = ts1(DV, n, n, 12582912.0, ADD)
                t = ts1(DV, n, n, 12582912.0, SUB)
                t = stt(DV, dst, n, -6.28125, a, MUL, ADD)
                t = stt(DV, dst, n, -0.0019340515136718750, dst, MUL, ADD)
                t = stt(DV, dst, n, -float(2 * np.pi - 6.28125 - 0.0019340515136718750), dst, MUL, ADD)
                if shift:
                    t = ts1(DV, dst, dst, shift, ADD)
                t = ts(DV, dst, dst, 3.1415925, -3.1415925, ALU.min, MAX)
                t = act(dst, dst, ACT.Sin, t)
            done["trig"] = t
        RK0 = 3072
        NS = 2
        ws = []
        ws0 = ar.at
        for _ in range(NS):
            w = {}
            w["raw"] = ar.take(3, 257)
            a0 = ar.at
            w["r"], w["k"] = ar.take(SEQ), ar.take(SEQ)
            w["LD"], w["C"], w["E"], w["KK"], w["A"], w["F"] = [ar.take(SEQ) for _ in range(6)]
            end = ar.at
            ar.at = a0
            w["X"], w["XT"], w["L"], w["Y"] = [ar.take(4, 128) for _ in range(4)]
            assert ar.at == end
            w["v"], w["g"], w["bon"] = [ar.take(SEQ) for _ in range(3)]
            w["AR"] = ar.take(2, 2, 128)
            w["B"], w["K"] = ar.take(2, SEQ), ar.take(2, SEQ)
            w["P1"], w["P2"] = ar.take(4, 256), ar.take(4, 256)
            w["Vp"] = ar.take(2, 2, 128)
            w["SAp"] = ar.take(2, 128)
            w["G"] = ar.take(128)
            w["Br"], w["Kr"] = ar.take(128), ar.take(128)
            w["S"] = ar.take(128)
            w["em"] = ar.take(4)
            ws.append(w)
            PO.do(lambda e, w=w: e.memset(w["raw"][:, :, 0:1], 0.0))
            PO.do(lambda e, w=w: e.memset(w["Vp"], 0.0))
            padz = PO.do(lambda e, w=w: e.memset(w["SAp"], 0.0))
        lraw = shaped(ws[1]["P2"].rearrange("p a b -> p (a b)")[:, 0:771], (3, 257))
        padz = PO.do(lambda e: e.memset(lraw[:, :, 0:1], 0.0))
        th[0] = norm("attn_g")
        trig()
        for q in (DV, AC):
            q.wait(padz)
        free_rw, t_rw, t_lw = {}, {}, {}
        mla_at = ar.at
        y2_at = (ws0 + (ar.at - ws0) // NS + 15) // 16 * 16
        y2h = shaped(sb("y2h", 8 * SEQ, F32R, at=u_at + y2_at)[:, :], (8, SEQ))
        assert y2_at + 8 * SEQ <= mla_at

        def main2():
            lt = [C128(RK0), C128(RK0 + 128), list(range(RK0 + 256, RK0 + 288)) + [-1] * 96]

            def evl(g, ap, tok):
                t = copy(lraw[:, 2 * g:2 * g + ap.shape[1], 1:257], ap, tok)
                done[("lraw", g)] = t
                return t
            yield from tgemm("w_in_2", lt, 16, hk, t_h, evl)
            CQ0 = 3360

            def latent(g):
                dst = (cqT, ckvT)[g // 2][:, 2 * (g % 2):2 * (g % 2) + 2, :]
                yield from tgemm("w_in_2", tiles_of(CQ0 + 256 * g, 2), 16, hk, t_h, keep(dst, ("c", g)))
            for p in range(8):
                w = ws[p % NS]
                for g in range(2):
                    def evr(_, ap, tok):
                        if p >= NS:
                            yield from until(p - NS, free_rw)
                        t = copy(w["raw"][:, 2 * g:2 * g + ap.shape[1], 1:257], ap, tok,
                                 free_rw[p - NS] if p >= NS else None)
                        if g:
                            t_rw[p] = t
                        return t
                    tl = [C128(128 * p), C128(1024 + 128 * p)] if g == 0 else [C128(2048 + 128 * p)]
                    yield from tgemm("w_in_2", tl, 16, hk, t_h, evr)
                if 2 <= p < 6:
                    yield from latent(p - 2)
            pe_cols = list(range(CQ0 + 1024, CQ0 + 1088))
            yield from tgemm("w_in_2", [pe_cols + pe_cols], 16, hk, t_h, keep(kpe[:, 0:1, :], "kpe"))
            t_end = PE.last()
            qn = hlF[:, 0:8, :]
            qp = hlF[:, 8:12, :]
            done["qn"], done["qp"] = qn, qp
            for key, src, gain in (("cq", cqT, "qn"), ("ckv", ckvT, "kvn")):
                t = [t_raw[("c", g)] for g in range(4)]
                sq = hlF[:, 12:16, :]
                t = tt(DV, sq, src, src, MUL, t, t_end, PE.last())
                b = gbanks.take()
                PE.wait(b.free, t)
                for k in range(4):
                    tok = mml(b.ap[:, 0:SEQ], ones, sq[:, k, :], k == 0, k == 3)
                t = act(rtmp, b.ap[:, 0:SEQ], ACT.Sqrt, tok, DV.last(), scale=1.0 / 512, bias=C("eps"))
                b.free = [t]
                t = recip(rtmp, rtmp, t)
                for k in range(4):
                    t = stt(DV, src[:, k, :], src[:, k, :], C(gain, k, k + 1), rtmp, MUL, MUL)
                done["n" + key] = t
                yield

            def evq(g, ap, tok):
                t = copy(hlF[:, 2 * g:2 * g + 2, :], ap, tok)
                t_raw[("mq", g)] = t
                return t
            uq = [list(range(192 * h, 192 * h + 128)) for h in range(8)]
            uq += [[192 * h + 128 + j for h in (2 * a, 2 * a + 1) for j in range(64)] for a in range(4)]
            yield from tgemm("mla_w_uq_2", uq, 4, plain(cqT), done["ncq"], evq)
            done["mla_q"] = True
            kn = hhF[:, 0:8, :]
            vm = shaped(hhF_[:, 8 * SEQ:16 * SEQ], (2, 1024))
            done["kn"], done["vm"] = kn, vm
            wait0 = [t_end]

            def evk(g, ap, tok):
                t = copy(kn[:, 2 * g:2 * g + 2, :], ap, tok, wait0)
                t_raw[("mk", g)] = t
                return t
            yield from tgemm("mla_w_ukv_2", [list(range(256 * h, 256 * h + 128)) for h in range(8)], 4,
                             plain(ckvT), done["nckv"], evk)
            for a in range(4):
                def evv(i, ap, tok):
                    t = copy(vm[:, i, 256 * a:256 * a + 256], ap, tok, wait0)
                    t_raw[("mv", a)] = t
                    return t
                vcols = [256 * h + 128 + j for h in range(2 * a, 2 * a + 2) for j in range(128)]
                yield from rowgemm("mla_w_ukv_2", vcols, 4,
                                   lambda k, i: (ckvT[:, k, 128 * i:128 * i + 128], None), done["nckv"], evv)
            done["mla_kv"] = t_raw[("mv", 3)]
            yield from until("mla", done)
            rhs = parts_of_y(1, hl[:, 0:8, :], done["mla"])
            yield from wout("w_out_2", rhs, 8, 8, None)
            yield from until("rwkv0", done)
            yield from until("rwkv1", done)
            rhs = parts_of_y(0, y2h, [done["rwkv0"], done["rwkv1"]])
            yield from wout("w_out_2", rhs, 8, 0, None, sums=sums)

        def lora():
            for g in range(2):
                yield from until(("lraw", g), done)
            for j in range(3):
                d = lh[:, j, :]
                t = tt(DV, d, lraw[:, j, 0:256], lraw[:, j, 1:257], SUB, done[("lraw", 0)], done[("lraw", 1)],
                       done["trig"])
                t = stt(DV, d, d, C("mu", 24 + j, 25 + j), lraw[:, j, 1:257], MUL, ADD)
                yield
            t1 = ts1(DV, lh[:, 3, :], lh[:, 0, :], C("head", 1, 2), MUL)
            act(lh[:, 0, :], lh[:, 0, :], ACT.Tanh, t1)
            t = act(lh[:, 1:3, :], lh[:, 1:3, :], ACT.Tanh, scale=0.5)
            t = ts(DV, lh[:, 1:3, :], lh[:, 1:3, :], 0.5, 0.5, MUL, ADD, t)
            t = ts1(DV, lh[:, 0, :], lh[:, 0, :], C("head", 0, 1), MUL)
            done["lora"] = t
            yield

        def rwkv(s, rb):
            w = ws[s]
            v, G_, bon, AR, Bt, Kt = w["v"], w["g"], w["bon"], w["AR"], w["B"], w["K"]
            P1, P2, Vp, SAp, G, Br, Kr, S = [w[n] for n in ("P1", "P2", "Vp", "SAp", "G", "Br", "Kr", "S")]
            yield from until("lora", done)
            t_y = None
            t_pe, t_sap = PE.last(), None
            for p in range(s, 8, NS):
                yield from until(p, t_rw)
                raw, r, k, LD, Cc, E, KK, A, F = [w[n] for n in ("raw", "r", "k", "LD", "C", "E", "KK", "A", "F")]
                pc = slice(128 * p, 128 * p + 128)
                c1 = slice(p, p + 1)

                def V1(name):
                    return C(name, p, p + 1)
                t_d = [tt(DV, d, raw[:, j, 0:256], raw[:, j, 1:257], SUB, t_rw[p], t_pe, alone=j > 0)
                       for j, d in enumerate((r, k, v))]
                for j, d in enumerate((r, k, v)):
                    t = stt(DV, d, d, C("mu", 8 * j + p, 8 * j + p + 1), raw[:, j, 1:257], MUL, ADD, t_d[j],
                            alone=True)
                free_rw[p] = t
                t_h3 = t
                yield
                b = rb.take()
                PE.wait(b.free, done["lora"], t_lora)
                mml(b.ap[:, 0:256], lw[0][:, pc], lh[:, 0, :], True, True)
                tok = mml(b.ap[:, 256:512], lw[0][:, pc], lh[:, 3, :], True, True)
                yield
                b2 = rb.take()
                PE.wait(b2.free)
                mml(b2.ap[:, 0:256], lw[1][:, pc], lh[:, 1, :], True, False)
                tok2 = mml(b2.ap[:, 0:256], lw[2][:, pc], lh[:, 2, :], False, True)
                t_lw[p] = tok2
                yield
                t = ts(DV, LD, b.ap[:, 0:256], V1("w0"), 0.5, ADD, MUL, tok)
                t = ts(DV, A, b.ap[:, 256:512], V1("a0"), 0.5, ADD, MUL)
                b.free = [t]
                act(LD, LD, ACT.Tanh, t)
                act(A, A, ACT.Tanh, alone=True)
                t = copy(G_, b2.ap[:, 0:256], tok2)
                b2.free = [t]
                yield
                ec = 0.5 * float(np.exp(-0.5))
                t = ts(DV, LD, LD, -ec, -ec, MUL, ADD, t)
                t = ts(DV, A, A, 0.5, 0.5, MUL, ADD)
                t = ts1(DV, KK, k, V1("k_k"), MUL)
                t_kk = act(E, KK, ACT.Square, t)
                for c in range(2):
                    cs = slice(128 * c, 128 * c + 128)
                    t_c = DV.do(lambda e, cs=cs: e.tensor_tensor_scan(Cc[:, cs], ones, LD[:, cs], 0.0, MUL, ADD))
                yield
                b = rb.take()
                PE.wait(b.free, t_kk)
                tok = mml(b.ap[:, 0:256], bones, E, True, True)
                yield
                t = ts1(DV, E, b.ap[:, 0:256], 1e-24, MAX, tok)
                b.free = [t]
                t = act(E, E, ACT.Sqrt, t)
                t1 = stt(DV, F, A, -1.0, k, ADD, MUL)
                t1 = stt(DV, k, F, V1("k_a"), k, MUL, ADD)
                yield
                t = recip(E, E, t)
                t = tt(DV, KK, KK, E, MUL)
                t = tt(DV, A, A, KK, MUL)
                t = tt(DV, E, r, k, MUL)
                t = ts1(DV, E, E, V1("r_k"), MUL)
                yield
                b = rb.take()
                PE.wait(b.free, t)
                tok = mml(b.ap[:, 0:256], bones, E, True, True)
                yield
                t = tt(DV, bon, b.ap[:, 0:256], v, MUL, tok)
                b.free = [t]
                for c in range(2):
                    cs = slice(128 * c, 128 * c + 128)
                    t = ts1(DV, w["em"][:, c:c + 1], Cc[:, 128 * c + 127:128 * c + 128], 0.5, MUL)
                    t = ts1(DV, E[:, cs], Cc[:, cs], w["em"][:, c:c + 1], SUB)
                t = tt(DV, LD, E, LD, SUB)
                t = tt(DV, w["em"][:, 2:3], w["em"][:, 0:1], w["em"][:, 1:2], ADD)
                yield
                t1 = act(F, LD, ACT.Exp, t)
                t2 = act(Cc, E, ACT.Exp, alone=True)
                t3 = act(LD, E, ACT.Exp, t1, scale=-1.0, alone=True)
                t4 = act(w["em"][:, 3:4], w["em"][:, 2:3], ACT.Exp, alone=True)
                yield
                t = tt(DV, AR[:, :, 0, :], shaped(KK, (2, 128)), shaped(F, (2, 128)), MUL, t1)
                t = tt(DV, AR[:, :, 1, :], shaped(r, (2, 128)), shaped(Cc, (2, 128)), MUL, t2, alone=True)
                for h in range(2):
                    t = stt(DV, Bt[:, h, :], A, C("head", h, h + 1), LD, MUL, MUL, t3, alone=True)
                    t_ab = stt(DV, Kt[:, h, :], k, C("head", h, h + 1), LD, MUL, MUL, alone=True)
                yield
                yield
                b = rb.take()
                PE.wait(b.free, t_ab, t_h3)
                tok = trl(b.ap[:, 0:128], v[:, 0:128])
                tok = trl(b.ap[:, 128:256], v[:, 128:256])
                for h in range(2):
                    mml(b.ap[:, 256:384], Bt[:, h, 0:128], ident, h == 0, h == 1)
                for h in range(2):
                    tok = mml(b.ap[:, 384:512], Kt[:, h, 0:128], ident, h == 0, h == 1)
                yield
                for h in range(2):
                    t = copy(Vp[:, :, h, 64 * h:64 * h + 64], shaped(b.ap[:, 0:256], (2, 128))[:, :, 64 * h:64 * h + 64], tok, t_y)
                copy(Br, b.ap[:, 256:384])
                t_rows = copy(Kr, b.ap[:, 384:512])
                b.free = [t_rows]
                SUm = C("SU")
                for h in range(2):
                    for P, src in ((P1, Bt), (P2, Kt)):
                        yield
                        b = rb.take()
                        PE.wait(b.free)
                        for c in range(2):
                            tok = mml(b.ap[:, 256 * c:256 * c + 256], src[:, h, 128 * c:128 * c + 128],
                                      AR[:, c, :, :].rearrange("p a b -> p (a b)"), True, True)
                        yield
                        bv = b.ap[:, :].rearrange("p (c a n) -> p c a n", c=2, a=2)
                        Pv = P.rearrange("p m (a n) -> p m a n", a=2)[:, 2 * h:2 * h + 2, :, :]
                        t = tt(DV, Pv[:, :, 0, :], bv[:, :, 0, :], rep(SUm, 2), MUL, tok, alone=True)
                        t = tt(DV, Pv[:, :, 1, :], bv[:, :, 1, :], rep(C("utri"), 2), MUL, alone=True)
                        b.free = [t]
                t_p = t
                X, XT, L, Y = w["X"], w["XT"], w["L"], w["Y"]
                yield
                b = rb.take()
                PE.wait(b.free)
                for h in range(2):
                    for c in range(2):
                        m = 2 * h + c
                        tok = mml(b.ap[:, 128 * m:128 * m + 128], AR[:, c, 0, :], Bt[:, h, 128 * c:128 * c + 128],
                                  True, True)
                yield
                LT = P1[:, :, 0:128]
                t_l = tt(DV, L, shaped(b.ap[:, :], (4, 128)), rep(C("SL"), 4), MUL, tok, alone=True)
                b.free = [t_l]
                yield
                t_inv = yield from invert(rb, X, XT, L, LT, Y, t_l, t_p, [t_ab])
                for c in range(2):
                    yield
                    b = rb.take()
                    PE.wait(b.free, t_rows, t_inv)
                    if c == 1:
                        PE.wait(t_s)
                        mm(b.ap[:, 0:128], AR[:, 1, 0, :], S, True, False)
                    for h in range(2):
                        hc = slice(64 * h, 64 * h + 64)
                        tok = mml(b.ap[:, hc], P2[:, 2 * h + c, 0:128], Vp[:, c, h, hc], c == 0, c == 0 or h == 1)
                    yield
                    t = copy(G, b.ap[:, 0:128], tok)
                    b.free = [t]
                    yield
                    b = rb.take()
                    PE.wait(b.free, t)
                    for h in range(2):
                        hc = slice(64 * h, 64 * h + 64)
                        tok = mml(b.ap[:, hc], XT[:, 2 * h + c, :], G[:, hc], True, True)
                    yield
                    for h in range(2):
                        hc = slice(64 * h, 64 * h + 64)
                        t_sa = copy(SAp[:, h, hc], b.ap[:, hc], tok, t_sap, scale=-1.0)
                    b.free = [t_sa]
                    yield
                    yield
                    b = rb.take()
                    PE.wait(b.free, t_sa)
                    o = b.ap[:, 0:128]
                    if c == 1:
                        mm(o, S, AR[:, 1, 1, :], True, False)
                    for h in range(2):
                        mm(o, SAp[:, h, :], P1[:, 2 * h + c, 128:256], c == 0 and h == 0, False)
                        tok = mml(o, Vp[:, c, h, :], P2[:, 2 * h + c, 128:256], False, h == 1)
                    if c == 0:
                        yield
                        b2 = rb.take()
                        PE.wait(b2.free)
                        n = 0
                        for rows, src in ((Br, SAp), (Kr, Vp[:, 0, :, :])):
                            for h in range(2):
                                tok2 = mml(b2.ap[:, 0:128], rows, src[:, h, :], n == 0, n == 3)
                                n += 1
                        t_sap = tok2
                    else:
                        t_sap = tok
                    yield
                    yc = w["X"].rearrange("p a b -> p (a b)")[:, 0:256]
                    t_yc = copy(yc[:, 128 * c:128 * c + 128], o, tok)
                    b.free = [t_yc]
                    if c == 0:
                        t_s = stt(DV, S, b2.ap[:, 0:128], w["em"][:, 3:4], bones, MUL, MUL, tok2)
                        b2.free = [t_s]
                    yield
                t_y = tok
                sq = w["X"].rearrange("p a b -> p (a b)")[:, 256:512]
                rs = w["L"].rearrange("p a b -> p (a b)")[:, 0:256]
                yield
                b = rb.take()
                PE.wait(b.free, t_yc)
                tok = mml(b.ap[:, 0:256], bones, yc, True, True)
                yield
                t = stt(DV, yc, b.ap[:, 0:256], -1.0 / 64, yc, MUL, ADD, tok)
                b.free = [t]
                t = act(sq, yc, ACT.Square, t)
                yield
                b = rb.take()
                PE.wait(b.free, t)
                tok = t_pe = mml(b.ap[:, 0:256], bones, sq, True, True)
                yield
                t = act(rs, b.ap[:, 0:256], ACT.Sqrt, tok, scale=1.0 / 64, bias=C("eps64"))
                b.free = [t]
                yield
                t = recip(rs, rs, t)
                t = tt(DV, yc, yc, rs, MUL)
                t = ts(DV, yc, yc, V1("gn_w"), V1("gn_b"), MUL, ADD)
                t = tt(DV, yc, yc, bon, ADD)
                t = tt(DV, yT[:, p, :], yc, G_, MUL)
                yield
            done[f"rwkv{s}"] = t

        rb0, rb1 = Banks(banks[2:4]), Banks(banks[4:6])
        mxb2 = ar.take(4)
        smb2 = ar.take(4)

        def mla():
            rb = Banks(banks[6:8])
            yield from until("kpe", t_raw)
            yield from until("mla_q", done)
            yield from until("mla_kv", done)
            qn, qp, kn, vm = done["qn"], done["qp"], done["kn"], done["vm"]
            tmp = hlF[:, 12:14, :]
            Sm = [hlF_[:, 12 * SEQ:16 * SEQ], ckvT.rearrange("p a b -> p (a b)")]
            PTm = [shaped(cqT[:, 2 * j:2 * j + 2, :].rearrange("p a b -> p (a b)"), (4, 128)) for j in range(2)]
            DV.wait(done["mla_kv"], done["trig"])
            AC.wait(done["mla_kv"])
            for a in range(2):
                rope(qp[:, 2 * a:2 * a + 2, :], cos2, sin2, C("R2"), [t_raw[("mq", 4 + a)]], ("rqp", a), rb, tmp, 2)
                yield
            rope(kpe[:, 0:1, :], cos2, sin2, C("R2"), t_raw["kpe"], "rkpe", rb, tmp[:, 0:1, :], 1)
            ts1(DV, kpe[:, 1, :], kpe[:, 0, :], C("head", 1, 2), MUL)
            done["rkpe"] = ts1(DV, kpe[:, 0, :], kpe[:, 0, :], C("head", 0, 1), MUL)
            yield
            scale = 192 ** -0.5
            free_S = [[], []]
            free_P = [[], []]
            u = 0
            for a in range(2):
                for i in range(2):
                    nk = 128 * (i + 1)
                    S = shaped(Sm[u % 2][:, 0:4 * nk], (4, nk))

                    def pair(h, out, nk):
                        hh = 4 * a + h
                        PE.wait(t_raw[("mk", 3)], done["rkpe"], done[("rqp", 1)])
                        mm(out, qn[:, hh, 128 * i:128 * i + 128], kn[:, hh, 0:nk], True, False)
                        return mml(out, qp[:, hh // 2, 128 * i:128 * i + 128], kpe[:, hh % 2, 0:nk], False, True)
                    t = yield from score_banks(rb, i, pair, scale, S, free_S[u % 2])
                    t = yield from softmax4b(S, nk, t)
                    pt = []
                    for j in range(i + 1):
                        t2, tok = yield from turn(rb, S, j, PTm[j], t, free_P[j])
                        pt.append((PTm[j], j, t2, j))
                    free_S[u % 2] = [tok]
                    yield
                    b = rb.take()
                    PE.wait(b.free, t_raw[("mv", 3)])
                    for h in range(4):
                        hh = 4 * a + h
                        for x, (P, j, t2, n) in enumerate(pt):
                            PE.wait(t2)
                            tok = mml(b.ap[:, 128 * h:128 * h + 128], vm[:, j, 128 * hh:128 * hh + 128], P[:, h, :],
                                      x == 0, x == len(pt) - 1)
                    for (_, _, _, n) in pt:
                        free_P[n] = [tok]
                    yield
                    for p in range(8 - NS, 8):
                        yield from until(p, t_lw)
                    AC.wait([t_lw[p] for p in range(8 - NS, 8)])
                    t = copy(yT[:, 8 + 4 * a:12 + 4 * a, 128 * i:128 * i + 128], shaped(b.ap[:, :], (4, 128)), tok)
                    b.free = [t]
                    u += 1
                    yield
            done["mla"] = t

        def softmax4b(S, nk, t):
            mx, sm = mxb2, smb2
            t = red(mx, S, MAX, t)
            t = tt(DV, S, S, over(mx, nk), SUB)
            yield
            t = act(S, S, ACT.Exp, t)
            yield
            t = red(sm, S, ADD, t)
            t = recip(sm, sm)
            t = tt(DV, S, S, over(sm, nk), MUL)
            yield
            return t

        t_raw.clear()
        for key in ("kc", "vc"):
            done.pop(key, None)
        run(main2(), [lora(), rwkv(0, rb0), rwkv(1, rb1), mla()])

        ar.at = mark1 + 64 * SEQ
        gp = [ar.take(2, 258) for _ in range(2)]
        cb = [ar.take(2, SEQ) for _ in range(2)]
        tb2 = [ar.take(2, SEQ) for _ in range(2)]
        for x in gp:
            tz = PO.do(lambda e, x=x: e.memset(x[:, :, 0:2], 0.0), PE.last(), DV.last(), AC.last())

        def gate2(g, ap, tok):
            s = g % 2
            t0 = copy(gp[s][:, :, 2:258], ap, tok, DV.last())
            for u in range(2):
                ct = 2 * g + u
                w = [C("conv2", 44 * j + ct, 44 * j + ct + 1) for j in range(3)]
                o = cb[s][:, u, :]
                ts(DV, o, gp[s][:, u, 0:256], w[0], C("conv2b", ct, ct + 1), MUL, ADD, t0, tz)
                stt(DV, o, gp[s][:, u, 1:257], w[1], o, MUL, ADD)
                t = stt(DV, o, gp[s][:, u, 2:258], w[2], o, MUL, ADD)
            t = act(tb2[s], cb[s], ACT.Tanh, t, scale=0.5)
            stt(DV, tb2[s], tb2[s], 1.0, cb[s], ADD, MUL, t)
            return t0
        run(ffn(("ffn_w_gate_2", "ffn_w_up_2", "ffn_w_down_2"), "ffn_g", gate2, lambda g: tb2[g % 2]), [])
        t_n = norm("final_g", dst=hhF)
        hflat = hhF_[:, :]
        for j in range(4):
            SP.wait(t_n[4 * j + 3])
            SP.raw(lambda e, j=j: e.dma_start(d_out[:, 1024 * j:1024 * j + 1024], hflat[:, 1024 * j:1024 * j + 1024])
                   .then_inc(s_out, 16))
        SP.wait((s_out, 64))

        at, off = [], 0
        for (_, _, kt, cl) in specs:
            at.append((off, kt * len(cl)))
            off += 128 * kt * len(cl)
        stream["at"] = at
        stream["ap"] = nc.dram_tensor("in_w_dram", [off], F32, kind="ExternalInput").ap()

        block = ctx.enter_context(nc.Block())

        @block.sync
        def _(e):
            for f in SP.ops:
                f(e)

        @block.gpsimd
        def _(e):
            for f in PO.ops:
                f(e)

        @block.scalar
        def _(e):
            for f in AC.ops:
                f(e)

        @block.vector
        def _(e):
            for f in DV.ops:
                f(e)

        @block.tensor
        def _(e):
            for f in PE.ops:
                f(e)
    return specs, off


def constants(inp):
    cols, n = layout()
    out = np.zeros((128, n), np.float32)

    def put(name, a):
        at, w = cols[name]
        assert a.shape == (128, w), (name, a.shape)
        out[:, at:at + w] = a

    def chan(v):
        return np.asarray(v).reshape(-1, 128).T

    i = np.arange(128)
    I, J = i[:, None], i[None, :]
    put("ident", np.eye(128, dtype=np.float32))
    put("ones", np.ones((128, 128), np.float32))
    put("bones", (I // 64 == J // 64).astype(np.float32))
    put("utri", (I <= J).astype(np.float32))
    put("SU", (I < J).astype(np.float32))
    put("head", np.stack([i < 64, i >= 64], 1).astype(np.float32))

    K = np.arange(64)[None, :]
    put("SL", (I > J).astype(np.float32))
    put("MC", np.concatenate([I // 2 ** l == 2 * (K // 2 ** l) + 1 - t for l in range(7) for t in range(2)], 1).astype(np.float32))
    put("causal", np.where(J <= I, 0, NEG).astype(np.float32))
    put("causalT", np.where(J >= I, 0, NEG).astype(np.float32))
    R1 = np.zeros((128, 128), np.float32)
    R1[i[:64] + 64, i[:64]] = -1
    R1[i[:64], i[:64] + 64] = 1
    put("R1", R1)
    R2 = np.zeros((128, 128), np.float32)
    for b in (0, 64):
        for j in range(32):
            R2[b + j + 32, b + j] = -1
            R2[b + j, b + j + 32] = 1
    put("R2", R2)
    inv1 = (1.0 / (10000.0 ** (np.arange(0, 128, 2) / 128))).astype(np.float32)
    ang = np.arange(SEQ, dtype=np.float32)[None, :] * inv1[i % 64][:, None]
    put("cos1", np.cos(ang))
    put("sin1", np.sin(ang))
    put("inv2", (10000.0 ** (-(i % 32) / 32)).astype(np.float32)[:, None])
    c = np.arange(16)
    cm = [np.where((c[None, :] * 16 + 31 <= (128 * t + i)[:, None]) & (c[None, :] < 15), 0, NEG) for t in range(2)]
    put("cmpmask", np.concatenate(cm, 1).astype(np.float32))
    put("anyv", np.stack([i >= 31, i >= 0], 1).astype(np.float32))
    put("eps", np.full((128, 1), EPS, np.float32))
    put("eps128", np.full((128, 1), 128 * EPS, np.float32))
    put("eps64", np.full((128, 1), 64e-5, np.float32))
    for name, key in (("norm1", "norm1_w"), ("norm2", "norm2_w"), ("normf", "norm_f_w"), ("attn_g", "attn_norm_g_2"),
                      ("ffn_g", "ffn_norm_g_2"), ("final_g", "final_norm_g_2"), ("w0", "rwkv_w0_2"),
                      ("a0", "rwkv_a0_2"), ("k_k", "rwkv_k_k_2"), ("k_a", "rwkv_k_a_2"), ("r_k", "rwkv_r_k_2"),
                      ("gn_w", "rwkv_gn_w_2"), ("gn_b", "rwkv_gn_b_2"), ("qn", "mla_q_norm_g_2"),
                      ("kvn", "mla_kv_norm_g_2"), ("conv2b", "ffn_conv_b_2"), ("dn_norm", "dn_norm_w"),
                      ("conv", "conv_w"), ("conv2", "ffn_conv_w_2")):
        put(name, chan(inp[key]))
    put("a_log", np.broadcast_to(inp["a_log"].reshape(1, 8), (128, 8)))
    put("dt_bias", np.broadcast_to(inp["dt_bias"].reshape(1, 8), (128, 8)))
    put("pe_k", inp["cmp_pe_k"][0].T)
    put("pe_v", inp["cmp_pe_v"][0].T)
    put("w2k", inp["cmp_w2_k"][0])
    put("w2v", inp["cmp_w2_v"][0])
    mu = np.zeros(27 * 128, np.float32)
    mu[:3360] = inp["rwkv_mu_2"].reshape(-1)
    put("mu", chan(mu))
    return out


def kernel(**inputs):
    import concourse.bacc as _bacc
    from concourse.bass_utils import run_bass_kernel_spmd as _run

    inp = {k: np.asarray(v) for k, v in inputs.items()}
    nc = _bacc.Bacc("TRN2", target_bir_lowering=False, num_devices=1)
    specs, _ = build(_bacc.Bacc("TRN2", target_bir_lowering=False, num_devices=1))
    _, total = build(nc, specs)
    w = np.empty(total, np.float32)
    at = 0
    for name, k0, kt, cl in specs:
        src = inp[name].reshape(-1, inp[name].shape[-1])[128 * k0:128 * (k0 + kt)]
        n = len(cl)
        dst = w[at:at + 128 * kt * n].reshape(128, kt, n)
        real = [c for c in cl if c >= 0]
        if real == list(range(real[0], real[0] + len(real))):
            part = src[:, real[0]:real[0] + len(real)]
        else:
            part = src[:, real]
        dst[:, :, len(real):] = 0
        dst[:, :, :len(real)] = part.reshape(kt, 128, len(real)).transpose(1, 0, 2)
        at += 128 * kt * n
    lora = np.zeros((128, 3, 1024), np.float32)
    lora[0:64, 0] = inp["rwkv_w2_2"][0]
    lora[64:128, 0] = inp["rwkv_a2_2"][0]
    lora[:, 1] = inp["rwkv_g2_2"][0][0:128]
    lora[0:32, 2] = inp["rwkv_g2_2"][0][128:160]
    arrays = {
        "in_cst_dram": constants(inp),
        "in_x_dram": np.ascontiguousarray(inp["x"][0].T.reshape(16, 128, SEQ).transpose(1, 0, 2).reshape(128, -1)),
        "in_pos_dram": np.ascontiguousarray(np.broadcast_to(inp["positions_2"].reshape(1, SEQ), (128, SEQ))),
        "in_lora_dram": lora.reshape(128, 3072),
        "in_w_dram": w,
    }
    r = _run(nc, [arrays], core_ids=[0])
    o = r.results[0]["out_0_dram"].reshape(128, 16, SEQ)
    return np.ascontiguousarray(o.transpose(2, 1, 0).reshape(1, SEQ, DM))
```
